# Optimizing a Trainium2 kernel written in Bass

```python
import math
import jax, jax.numpy as jnp
from jax import lax
import numpy as np

D_MODEL = 1024
BATCH = 1
SEQ = 512
DEPTH = 2

N_A_LAYERS = DEPTH // 2
N_B_LAYERS = DEPTH - N_A_LAYERS
SSM_GROUP = 16
SSM_GROUPS = D_MODEL // SSM_GROUP
SSM_STATE = 64
SSM_CHUNK = 128
DT_MIN = 1e-3
DT_MAX = 1e-1
HEAD_DIM = 64
N_HEADS = D_MODEL // HEAD_DIM
N_KV_HEADS = N_HEADS // 4
GQA_GROUP = N_HEADS // N_KV_HEADS
WINDOW = 128
ATTN_BLOCK = 128
ROPE_THETA = 500000.0
ROT_DIM = HEAD_DIM // 4
D_FF = 4 * D_MODEL
PLE_DIM = 256
RMS_EPS = 1e-6
NEG_INF = -1e30


def rmsnorm(x, g):
    xf = x.astype(jnp.float32)
    y = xf * lax.rsqrt(jnp.mean(xf * xf, axis=-1, keepdims=True) + RMS_EPS)
    return (y * g.astype(jnp.float32)).astype(x.dtype)

def partial_rope(x, pos):
    inv = ROPE_THETA ** (-jnp.arange(0, ROT_DIM, 2, dtype=jnp.float32) / ROT_DIM)
    ang = pos.astype(jnp.float32)[:, None] * inv[None, :]
    cos = jnp.cos(ang)[None, :, None, :]
    sin = jnp.sin(ang)[None, :, None, :]
    xr = x[..., :ROT_DIM].astype(jnp.float32)
    x1, x2 = xr[..., :ROT_DIM // 2], xr[..., ROT_DIM // 2:]
    rot = jnp.concatenate([x1 * cos - x2 * sin, x2 * cos + x1 * sin], axis=-1).astype(x.dtype)
    return jnp.concatenate([rot, x[..., ROT_DIM:]], axis=-1)

def s5_mixer(u, lam_re, lam_im, log_dt, b_re, b_im, c_re, c_im, d, w_glu):
    bsz, seqlen, dm = u.shape
    f32 = jnp.float32
    lam_re = lam_re.astype(f32); lam_im = lam_im.astype(f32)
    b_re = b_re.astype(f32); b_im = b_im.astype(f32)
    c_re = c_re.astype(f32); c_im = c_im.astype(f32)
    dt = jnp.exp(log_dt.astype(f32))[:, None]
    mag = jnp.exp(lam_re * dt)
    a_r = mag * jnp.cos(lam_im * dt)
    a_i = mag * jnp.sin(lam_im * dt)
    den = lam_re * lam_re + lam_im * lam_im
    nr = a_r - 1.0
    coef_r = (nr * lam_re + a_i * lam_im) / den
    coef_i = (a_i * lam_re - nr * lam_im) / den
    bb_r = coef_r[..., None] * b_re - coef_i[..., None] * b_im
    bb_i = coef_r[..., None] * b_im + coef_i[..., None] * b_re

    n_chunks = seqlen // SSM_CHUNK
    ug = u.astype(f32).reshape(bsz, n_chunks, SSM_CHUNK, SSM_GROUPS, SSM_GROUP)
    ug = jnp.transpose(ug, (1, 0, 2, 3, 4))

    def combine(e1, e2):
        a1r, a1i, s1r, s1i = e1
        a2r, a2i, s2r, s2i = e2
        return (a2r * a1r - a2i * a1i,
                a2r * a1i + a2i * a1r,
                a2r * s1r - a2i * s1i + s2r,
                a2r * s1i + a2i * s1r + s2i)

    def chunk_step(carry, uc):
        cr, ci = carry
        bur = jnp.einsum('gnh,btgh->btgn', bb_r, uc)
        bui = jnp.einsum('gnh,btgh->btgn', bb_i, uc)
        ar = jnp.broadcast_to(a_r, bur.shape)
        ai = jnp.broadcast_to(a_i, bui.shape)
        pr, pi, sr, si = lax.associative_scan(combine, (ar, ai, bur, bui), axis=1)
        xr = sr + pr * cr[:, None] - pi * ci[:, None]
        xi = si + pr * ci[:, None] + pi * cr[:, None]
        y = jnp.einsum('ghn,btgn->btgh', c_re, xr) - jnp.einsum('ghn,btgn->btgh', c_im, xi)
        return (xr[:, -1], xi[:, -1]), y

    init = (jnp.zeros((bsz, SSM_GROUPS, SSM_STATE), f32), jnp.zeros((bsz, SSM_GROUPS, SSM_STATE), f32))
    _, ys = lax.scan(chunk_step, init, ug)
    y = jnp.transpose(ys, (1, 0, 2, 3, 4)).reshape(bsz, seqlen, dm)
    y = y + d.astype(f32) * u.astype(f32)
    y = jax.nn.gelu(y).astype(u.dtype)
    ab = y @ w_glu
    a, b = ab[..., :dm], ab[..., dm:]
    return a * jax.nn.sigmoid(b)

def swa_sink_attention(q, k, v, sinks):
    bsz, seqlen = q.shape[0], q.shape[1]
    nb = seqlen // ATTN_BLOCK
    f32 = jnp.float32
    qb = q.astype(f32).reshape(bsz, nb, ATTN_BLOCK, N_KV_HEADS, GQA_GROUP, HEAD_DIM)
    kb = k.astype(f32).reshape(bsz, nb, ATTN_BLOCK, N_KV_HEADS, HEAD_DIM)
    vb = v.astype(f32).reshape(bsz, nb, ATTN_BLOCK, N_KV_HEADS, HEAD_DIM)
    k_prev = jnp.concatenate([jnp.zeros_like(kb[:, :1]), kb[:, :-1]], axis=1)
    v_prev = jnp.concatenate([jnp.zeros_like(vb[:, :1]), vb[:, :-1]], axis=1)
    kk = jnp.concatenate([k_prev, kb], axis=2)
    vv = jnp.concatenate([v_prev, vb], axis=2)
    s = jnp.einsum('bnqkgd,bnjkd->bnkgqj', qb, kk) * (HEAD_DIM ** -0.5)
    qi = jnp.arange(ATTN_BLOCK)[:, None] + ATTN_BLOCK
    kj = jnp.arange(2 * ATTN_BLOCK)[None, :]
    band = (kj <= qi) & (qi - kj < WINDOW)
    has_prev = jnp.arange(nb) > 0
    mask = band[None] & ((kj >= ATTN_BLOCK)[None] | has_prev[:, None, None])
    s = jnp.where(mask[None, :, None, None], s, NEG_INF)
    sink = sinks.astype(f32).reshape(1, 1, N_KV_HEADS, GQA_GROUP, 1, 1)
    m = jnp.maximum(jnp.max(s, axis=-1, keepdims=True), sink)
    pr = jnp.exp(s - m)
    w = pr / (jnp.sum(pr, axis=-1, keepdims=True) + jnp.exp(sink - m))
    o = jnp.einsum('bnkgqj,bnjkd->bnqkgd', w, vv)
    return o.reshape(bsz, seqlen, N_HEADS * HEAD_DIM).astype(q.dtype)

def first_inputs(seed: int = 0) -> dict:
    key = jax.random.key(seed)
    ks = jax.random.split(key, 32)
    f32 = jnp.float32
    nrm = lambda k, shape, scale: jax.random.normal(k, shape, f32) * scale
    x = nrm(ks[0], (BATCH, SEQ, D_MODEL), 1.0)
    p = nrm(ks[1], (DEPTH, BATCH, SEQ, PLE_DIM), 1.0)
    norm_mix = 1.0 + nrm(ks[2], (DEPTH, D_MODEL), 0.02)
    ssm_lambda_re = -0.5 + nrm(ks[3], (N_A_LAYERS, SSM_GROUPS, SSM_STATE), 0.01)
    ssm_lambda_im = (jnp.pi * jnp.arange(SSM_STATE, dtype=f32))[None, None, :] + nrm(ks[4], (N_A_LAYERS, SSM_GROUPS, SSM_STATE), 0.01)
    ssm_log_dt = math.log(DT_MIN) + jax.random.uniform(ks[5], (N_A_LAYERS, SSM_GROUPS), f32) * (math.log(DT_MAX) - math.log(DT_MIN))
    ssm_b_re = nrm(ks[6], (N_A_LAYERS, SSM_GROUPS, SSM_STATE, SSM_GROUP), (2 * SSM_GROUP) ** -0.5)
    ssm_b_im = nrm(ks[7], (N_A_LAYERS, SSM_GROUPS, SSM_STATE, SSM_GROUP), (2 * SSM_GROUP) ** -0.5)
    ssm_c_re = nrm(ks[8], (N_A_LAYERS, SSM_GROUPS, SSM_GROUP, SSM_STATE), (2 * SSM_STATE) ** -0.5)
    ssm_c_im = nrm(ks[9], (N_A_LAYERS, SSM_GROUPS, SSM_GROUP, SSM_STATE), (2 * SSM_STATE) ** -0.5)
    ssm_d = nrm(ks[10], (N_A_LAYERS, D_MODEL), 1.0)
    ssm_w_glu = nrm(ks[11], (N_A_LAYERS, D_MODEL, 2 * D_MODEL), D_MODEL ** -0.5)
    kv_norm = 1.0 + nrm(ks[12], (D_MODEL,), 0.02)
    w_k = nrm(ks[13], (D_MODEL, N_KV_HEADS * HEAD_DIM), D_MODEL ** -0.5)
    w_v = nrm(ks[14], (D_MODEL, N_KV_HEADS * HEAD_DIM), D_MODEL ** -0.5)
    w_q = nrm(ks[15], (N_B_LAYERS, D_MODEL, N_HEADS * HEAD_DIM), D_MODEL ** -0.5)
    attn_sinks = nrm(ks[16], (N_B_LAYERS, N_HEADS), 0.5)
    w_o = nrm(ks[17], (N_B_LAYERS, N_HEADS * HEAD_DIM, D_MODEL), (N_HEADS * HEAD_DIM) ** -0.5)
    norm_mlp = 1.0 + nrm(ks[18], (DEPTH, D_MODEL), 0.02)
    w_up = nrm(ks[19], (DEPTH, D_MODEL, D_FF), D_MODEL ** -0.5)
    w_down = nrm(ks[20], (DEPTH, D_FF, D_MODEL), D_FF ** -0.5)
    norm_ple = 1.0 + nrm(ks[21], (DEPTH, D_MODEL), 0.02)
    w_ple_gate = nrm(ks[22], (DEPTH, D_MODEL, D_MODEL), D_MODEL ** -0.5)
    w_ple_proj = nrm(ks[23], (DEPTH, PLE_DIM, D_MODEL), PLE_DIM ** -0.5)
    norm_final = 1.0 + nrm(ks[24], (D_MODEL,), 0.02)
    return {'x': x, 'p': p, 'norm_mix': norm_mix,
            'ssm_lambda_re': ssm_lambda_re, 'ssm_lambda_im': ssm_lambda_im, 'ssm_log_dt': ssm_log_dt,
            'ssm_b_re': ssm_b_re, 'ssm_b_im': ssm_b_im, 'ssm_c_re': ssm_c_re, 'ssm_c_im': ssm_c_im,
            'ssm_d': ssm_d, 'ssm_w_glu': ssm_w_glu,
            'kv_norm': kv_norm, 'w_k': w_k, 'w_v': w_v, 'w_q': w_q, 'attn_sinks': attn_sinks, 'w_o': w_o,
            'norm_mlp': norm_mlp, 'w_up': w_up, 'w_down': w_down,
            'norm_ple': norm_ple, 'w_ple_gate': w_ple_gate, 'w_ple_proj': w_ple_proj,
            'norm_final': norm_final}

def first_block(x, p, norm_mix, ssm_lambda_re, ssm_lambda_im, ssm_log_dt, ssm_b_re, ssm_b_im,
              ssm_c_re, ssm_c_im, ssm_d, ssm_w_glu, kv_norm, w_k, w_v, w_q, attn_sinks, w_o,
              norm_mlp, w_up, w_down, norm_ple, w_ple_gate, w_ple_proj, norm_final):
    bsz, seqlen, _ = x.shape
    pos = jnp.arange(seqlen, dtype=jnp.int32)
    h = x
    k_shared = None
    v_shared = None
    for i in range(DEPTH):
        hn = rmsnorm(h, norm_mix[i])
        if i < N_A_LAYERS:
            mix = s5_mixer(hn, ssm_lambda_re[i], ssm_lambda_im[i], ssm_log_dt[i], ssm_b_re[i], ssm_b_im[i],
                           ssm_c_re[i], ssm_c_im[i], ssm_d[i], ssm_w_glu[i])
        else:
            j = i - N_A_LAYERS
            q = (hn @ w_q[j]).reshape(bsz, seqlen, N_HEADS, HEAD_DIM)
            q = partial_rope(q, pos)
            mix = swa_sink_attention(q, k_shared, v_shared, attn_sinks[j]) @ w_o[j]
        h = h + mix
        hm = rmsnorm(h, norm_mlp[i])
        h = h + jnp.square(jax.nn.relu(hm @ w_up[i])) @ w_down[i]
        gate = jax.nn.sigmoid(rmsnorm(h, norm_ple[i]) @ w_ple_gate[i])
        h = h + gate * (p[i] @ w_ple_proj[i])
        if i == N_A_LAYERS - 1:
            hk = rmsnorm(h, kv_norm)
            k_shared = partial_rope((hk @ w_k).reshape(bsz, seqlen, N_KV_HEADS, HEAD_DIM), pos)
            v_shared = (hk @ w_v).reshape(bsz, seqlen, N_KV_HEADS, HEAD_DIM)
    return rmsnorm(h, norm_final)


CHUNK = 64

N_B_LAYERS_2 = DEPTH // 2
N_A_LAYERS_2 = DEPTH - N_B_LAYERS_2

SSM_EXPAND = 2
SSM_D_INNER = SSM_EXPAND * D_MODEL
SSM_HEAD_DIM = 64
SSM_HEADS = SSM_D_INNER // SSM_HEAD_DIM
SSM_GROUPS_2 = 8
SSM_HEADS_PER_GROUP = SSM_HEADS // SSM_GROUPS_2
SSM_STATE_2 = 128
SSM_CONV = 4
SSM_CONV_DIM = SSM_D_INNER + 2 * SSM_GROUPS_2 * SSM_STATE_2
SSM_IN_DIM = 2 * SSM_D_INNER + 2 * SSM_GROUPS_2 * SSM_STATE_2 + SSM_HEADS
SSD_CHUNK = CHUNK

DIFF_HEAD_DIM = 64
DIFF_V_DIM = 2 * DIFF_HEAD_DIM
DIFF_HEADS = D_MODEL // DIFF_V_DIM
DIFF_WIDTH = DIFF_HEADS * DIFF_V_DIM
KV_DIM = DIFF_HEADS * 2 * DIFF_HEAD_DIM + DIFF_WIDTH
Q_BLOCK = 128
ALIBI_MAX_EXP = 8.0

EPS = 1e-5


def rms_norm(x, g):
    xf = x.astype(jnp.float32)
    y = xf * lax.rsqrt(jnp.mean(xf * xf, axis=-1, keepdims=True) + EPS)
    return (y * g.astype(jnp.float32)).astype(x.dtype)

def gated_group_rms_norm(y, z, g):
    u = y.astype(jnp.float32) * jax.nn.silu(z.astype(jnp.float32))
    shp = u.shape
    u = u.reshape(shp[:-1] + (SSM_GROUPS_2, SSM_D_INNER // SSM_GROUPS_2))
    u = u * lax.rsqrt(jnp.mean(u * u, axis=-1, keepdims=True) + EPS)
    return u.reshape(shp) * g.astype(jnp.float32)

def causal_depthwise_conv(u, w, bias):
    c = u.shape[-1]
    out = lax.conv_general_dilated(
        u, w[:, None, :].astype(u.dtype), window_strides=(1,),
        padding=[(SSM_CONV - 1, 0)], dimension_numbers=("NWC", "WIO", "NWC"),
        feature_group_count=c)
    return out + bias.astype(u.dtype)

def ssd_chunked_scan(xdt, adt, bm, cm):
    b, s = xdt.shape[:2]
    nc = s // SSD_CHUNK

    def to_chunks(t):
        return jnp.moveaxis(t.reshape((b, nc, SSD_CHUNK) + t.shape[2:]), 1, 0)

    causal = jnp.tril(jnp.ones((SSD_CHUNK, SSD_CHUNK), dtype=bool))[None, :, :, None, None]

    def step(state, inp):
        x_c, a_c, b_c, c_c = inp
        acs = jnp.cumsum(a_c, axis=1)
        seg = acs[:, :, None] - acs[:, None, :]
        decay = jnp.exp(jnp.where(causal, seg, -jnp.inf))
        cb = jnp.einsum("blgn,bsgn->blsg", c_c, b_c)
        y_diag = jnp.einsum("blsgr,bsgrp->blgrp", cb[..., None] * decay, x_c)
        y_off = jnp.einsum("blgn,bgrpn->blgrp", c_c, state) * jnp.exp(acs)[..., None]
        to_end = jnp.exp(acs[:, -1:] - acs)
        new_state = (state * jnp.exp(acs[:, -1])[..., None, None]
                     + jnp.einsum("blgn,blgrp->bgrpn", b_c, x_c * to_end[..., None]))
        return new_state, y_diag + y_off

    state0 = jnp.zeros((b, SSM_GROUPS_2, SSM_HEADS_PER_GROUP, SSM_HEAD_DIM, SSM_STATE_2), jnp.float32)
    _, ys = lax.scan(step, state0, (to_chunks(xdt), to_chunks(adt), to_chunks(bm), to_chunks(cm)))
    return jnp.moveaxis(ys, 0, 1).reshape(xdt.shape)

def mamba2_layer(x, norm_g, w_in, conv_w, conv_b, dt_bias, a_log, d_skip, gate_norm_g, w_out):
    b, s, _ = x.shape
    G, R, P, N = SSM_GROUPS_2, SSM_HEADS_PER_GROUP, SSM_HEAD_DIM, SSM_STATE_2
    h = rms_norm(x, norm_g)
    zxbcdt = h @ w_in
    z = zxbcdt[..., :SSM_D_INNER]
    xbc = zxbcdt[..., SSM_D_INNER:SSM_D_INNER + SSM_CONV_DIM]
    dt_raw = zxbcdt[..., SSM_D_INNER + SSM_CONV_DIM:]
    xbc = jax.nn.silu(causal_depthwise_conv(xbc, conv_w, conv_b))
    gn = G * N
    xs = xbc[..., :SSM_D_INNER].reshape(b, s, G, R, P).astype(jnp.float32)
    bm = xbc[..., SSM_D_INNER:SSM_D_INNER + gn].reshape(b, s, G, N).astype(jnp.float32)
    cm = xbc[..., SSM_D_INNER + gn:].reshape(b, s, G, N).astype(jnp.float32)
    dt = jax.nn.softplus(dt_raw.astype(jnp.float32) + dt_bias.astype(jnp.float32)).reshape(b, s, G, R)
    a = -jnp.exp(a_log.astype(jnp.float32)).reshape(G, R)
    y = ssd_chunked_scan(xs * dt[..., None], a * dt, bm, cm)
    y = y + d_skip.astype(jnp.float32).reshape(G, R, 1) * xs
    y = gated_group_rms_norm(y.reshape(b, s, SSM_D_INNER), z, gate_norm_g).astype(x.dtype)
    return x + y @ w_out

def shared_kv(x, kv_norm_g, w_kv):
    b, s, _ = x.shape
    kv = rms_norm(x, kv_norm_g) @ w_kv
    k = kv[..., :DIFF_HEADS * 2 * DIFF_HEAD_DIM].reshape(b, s, DIFF_HEADS, 2, DIFF_HEAD_DIM)
    v = kv[..., DIFF_HEADS * 2 * DIFF_HEAD_DIM:].reshape(b, s, DIFF_HEADS, DIFF_V_DIM)
    return k.transpose(0, 2, 3, 1, 4), v.transpose(0, 2, 1, 3)

def diff_attention_layer(x, k, v, norm_g, w_in, lam_qk, sub_g, w_out, lambda_init):
    b, s, _ = x.shape
    H, d = DIFF_HEADS, DIFF_HEAD_DIM
    nblk = s // Q_BLOCK
    qg = rms_norm(x, norm_g) @ w_in
    q = qg[..., :DIFF_WIDTH].reshape(b, nblk, Q_BLOCK, H, 2, d).transpose(1, 0, 3, 4, 2, 5)
    gate = qg[..., DIFF_WIDTH:]
    lf = lam_qk.astype(jnp.float32)
    lam = jnp.exp(jnp.sum(lf[0] * lf[1])) - jnp.exp(jnp.sum(lf[2] * lf[3])) + lambda_init
    slopes = 2.0 ** (-ALIBI_MAX_EXP * jnp.arange(1, H + 1, dtype=jnp.float32) / H)
    key_pos = jnp.arange(s)
    scale = 1.0 / math.sqrt(d)

    def attend_block(args):
        qb, blk = args
        qpos = blk * Q_BLOCK + jnp.arange(Q_BLOCK)
        dist = jnp.abs(qpos[:, None] - key_pos[None, :]).astype(jnp.float32)
        allowed = (key_pos // CHUNK)[None, :] <= (qpos // CHUNK)[:, None]
        scores = jnp.einsum("bhiqd,bhikd->bhiqk", qb, k).astype(jnp.float32) * scale
        scores = scores - slopes[None, :, None, None, None] * dist
        probs = jax.nn.softmax(jnp.where(allowed, scores, -jnp.inf), axis=-1)
        weights = probs[:, :, 0] - lam * probs[:, :, 1]
        return jnp.einsum("bhqk,bhke->bqhe", weights.astype(v.dtype), v)

    out = lax.map(attend_block, (q, jnp.arange(nblk)))
    out = jnp.moveaxis(out, 0, 1).reshape(b, s, H, DIFF_V_DIM)
    out = (rms_norm(out, sub_g) * (1.0 - lambda_init)).reshape(b, s, DIFF_WIDTH)
    return x + (out * jax.nn.silu(gate)) @ w_out

def second_inputs(seed: int = 0) -> dict:
    key = jax.random.key(seed)
    ks = jax.random.split(key, 18)
    f32 = jnp.float32

    def nrm(k, shape, scale):
        return jax.random.normal(k, shape, f32) * scale

    def gain(k, shape):
        return 1.0 + 0.05 * jax.random.normal(k, shape, f32)

    x = jax.random.normal(ks[0], (BATCH, SEQ, D_MODEL), f32)
    a_norm_g = gain(ks[1], (N_A_LAYERS_2, D_MODEL))
    a_w_in = nrm(ks[2], (N_A_LAYERS_2, D_MODEL, SSM_IN_DIM), D_MODEL ** -0.5)
    a_conv_w = nrm(ks[3], (N_A_LAYERS_2, SSM_CONV, SSM_CONV_DIM), SSM_CONV ** -0.5)
    a_conv_b = nrm(ks[4], (N_A_LAYERS_2, SSM_CONV_DIM), 0.01)
    u = jax.random.uniform(ks[5], (N_A_LAYERS_2, SSM_HEADS), f32)
    dt0 = jnp.exp(u * (math.log(DT_MAX) - math.log(DT_MIN)) + math.log(DT_MIN))
    a_dt_bias = dt0 + jnp.log(-jnp.expm1(-dt0))
    a_a_log = jnp.log(jax.random.uniform(ks[6], (N_A_LAYERS_2, SSM_HEADS), f32, 1.0, 16.0))
    a_d_skip = gain(ks[7], (N_A_LAYERS_2, SSM_HEADS))
    a_gate_norm_g = gain(ks[8], (N_A_LAYERS_2, SSM_D_INNER))
    a_w_out = nrm(ks[9], (N_A_LAYERS_2, SSM_D_INNER, D_MODEL), SSM_D_INNER ** -0.5)
    kv_norm_g = gain(ks[10], (D_MODEL,))
    w_kv = nrm(ks[11], (D_MODEL, KV_DIM), D_MODEL ** -0.5)
    b_norm_g = gain(ks[12], (N_B_LAYERS_2, D_MODEL))
    b_w_in = nrm(ks[13], (N_B_LAYERS_2, D_MODEL, 2 * DIFF_WIDTH), D_MODEL ** -0.5)
    b_lambda = nrm(ks[14], (N_B_LAYERS_2, 4, DIFF_HEAD_DIM), 0.1)
    b_sub_g = gain(ks[15], (N_B_LAYERS_2, DIFF_V_DIM))
    b_w_out = nrm(ks[16], (N_B_LAYERS_2, DIFF_WIDTH, D_MODEL), DIFF_WIDTH ** -0.5)
    final_norm_g = gain(ks[17], (D_MODEL,))
    return {"x": x, "a_norm_g": a_norm_g, "a_w_in": a_w_in, "a_conv_w": a_conv_w,
            "a_conv_b": a_conv_b, "a_dt_bias": a_dt_bias, "a_a_log": a_a_log,
            "a_d_skip": a_d_skip, "a_gate_norm_g": a_gate_norm_g, "a_w_out": a_w_out,
            "kv_norm_g": kv_norm_g, "w_kv": w_kv, "b_norm_g": b_norm_g, "b_w_in": b_w_in,
            "b_lambda": b_lambda, "b_sub_g": b_sub_g, "b_w_out": b_w_out,
            "final_norm_g": final_norm_g}

def second_block(x, a_norm_g, a_w_in, a_conv_w, a_conv_b, a_dt_bias, a_a_log, a_d_skip,
              a_gate_norm_g, a_w_out, kv_norm_g, w_kv, b_norm_g, b_w_in, b_lambda,
              b_sub_g, b_w_out, final_norm_g):
    k = v = None
    for i in range(DEPTH):
        if i < N_A_LAYERS_2:
            x = mamba2_layer(x, a_norm_g[i], a_w_in[i], a_conv_w[i], a_conv_b[i],
                             a_dt_bias[i], a_a_log[i], a_d_skip[i], a_gate_norm_g[i], a_w_out[i])
            if i == N_A_LAYERS_2 - 1:
                k, v = shared_kv(x, kv_norm_g, w_kv)
        else:
            j = i - N_A_LAYERS_2
            lambda_init = 0.8 - 0.6 * math.exp(-0.3 * i)
            x = diff_attention_layer(x, k, v, b_norm_g[j], b_w_in[j], b_lambda[j],
                                     b_sub_g[j], b_w_out[j], lambda_init)
    return rms_norm(x, final_norm_g)


def setup_inputs(seed=0):
    out = dict(first_inputs(seed))
    for name, value in second_inputs(seed + 1).items():
        if name != "x":
            out[name + "_2"] = value
    return out


def reference(
    x, p, norm_mix, ssm_lambda_re, ssm_lambda_im, ssm_log_dt, ssm_b_re, ssm_b_im, ssm_c_re,
    ssm_c_im, ssm_d, ssm_w_glu, kv_norm, w_k, w_v, w_q, attn_sinks, w_o, norm_mlp, w_up, w_down,
    norm_ple, w_ple_gate, w_ple_proj, norm_final, a_norm_g_2, a_w_in_2, a_conv_w_2, a_conv_b_2,
    a_dt_bias_2, a_a_log_2, a_d_skip_2, a_gate_norm_g_2, a_w_out_2, kv_norm_g_2, w_kv_2,
    b_norm_g_2, b_w_in_2, b_lambda_2, b_sub_g_2, b_w_out_2, final_norm_g_2,
):
    x = first_block(
        x, p, norm_mix, ssm_lambda_re, ssm_lambda_im, ssm_log_dt, ssm_b_re, ssm_b_im, ssm_c_re,
        ssm_c_im, ssm_d, ssm_w_glu, kv_norm, w_k, w_v, w_q, attn_sinks, w_o, norm_mlp, w_up,
        w_down, norm_ple, w_ple_gate, w_ple_proj, norm_final,
    )
    return second_block(
        x, a_norm_g_2, a_w_in_2, a_conv_w_2, a_conv_b_2, a_dt_bias_2, a_a_log_2, a_d_skip_2,
        a_gate_norm_g_2, a_w_out_2, kv_norm_g_2, w_kv_2, b_norm_g_2, b_w_in_2, b_lambda_2,
        b_sub_g_2, b_w_out_2, final_norm_g_2,
    )


_drawn_inputs = setup_inputs


def setup_inputs(seed=0):
    import zlib

    import numpy as np

    out = dict(_drawn_inputs(seed))
    spreads = {}
    factors = {'norm_mix': 4.861,
     'ssm_lambda_re': 8.0,
     'kv_norm': 8.0,
     'attn_sinks': 7.866,
     'norm_ple': 8.0,
     'a_conv_b_2': 5.488,
     'a_d_skip_2': 2.992,
     'kv_norm_g_2': 3.851,
     'b_norm_g_2': 3.664,
     'b_lambda_2': 8.0,
     'b_sub_g_2': 5.775}
    for name, (base, spread) in spreads.items():
        noise = np.random.default_rng([zlib.crc32(name.encode()), seed]).standard_normal(out[name].shape)
        drawn = base * np.exp(spread * noise) if base else spread * noise
        out[name] = __import__('jax').numpy.asarray(drawn.astype(out[name].dtype))
    for name, factor in factors.items():
        out[name] = (out[name] * factor).astype(out[name].dtype)
    return out
```

```python
import math
from contextlib import ExitStack
import numpy as np
import concourse.bass as bass
from concourse import mybir

F32 = mybir.dt.float32
F32R = mybir.dt.float32r
ACT = mybir.ActivationFunctionType
ALU = mybir.AluOpType
AX = mybir.AxisListType

LANES, TOK, DM = 128, 512, 1024
KT = DM // LANES
SG, SH, SN = 64, 16, 64
STEP = 8
NSTEP = TOK // STEP
GB = LANES // SH
NBLK = SG // GB
SIN_SCALE = 6.283185
PI_SAFE = 3.1415925
ROUND = 12582912.0
TWO_PI_HI, TWO_PI_LO = 6.28125, 2.0 * math.pi - 6.28125

CONSTS = [("ident", 128), ("turn", 128), ("ropeswap", 128), ("ones", 128), ("tri", 128), ("sgn", 1), ("nsgn", 1),
          ("sel", 8), ("cidx", 64), ("cnz", 64), ("id16", 16), ("rcos", 512), ("rsin", 512), ("band", 256), ("band0", 256), ("dist", 512), ("slope", 8)]
GAINS = ["mix0", "mix1", "mlp0", "mlp1", "ple0", "ple1", "kv", "final", "a_norm", "kv2", "b_norm", "final2"]
PARAMS = [(g, 8) for g in GAINS] + [("lam_re", 64), ("lam_im", 64), ("log_dt", 64), ("gain_u", 64), ("d_h", 64),
          ("conv_w", 128), ("conv_b", 32), ("d_skip", 16), ("gate_g", 16), ("sub_g", 1), ("sinks", 16),
          ("dt_bias", 32), ("a_log", 32), ("lam_qk", 256)]


def columns(table):
    at, n = {}, 0
    for name, w in table:
        at[name] = (n, n + w)
        n += w
    return at, n


CC, NCONST = columns(CONSTS)
PC, NPARAM = columns(PARAMS)

U_GLU, U_MLP0, U_P0, U_GATE0 = 0, 16, 80, 82
U_KV, U_Q, U_O, U_MLP1, U_P1, U_GATE1 = 90, 94, 102, 110, 174, 176
U_DT, U_MAMBA, U_KV2, U_QG2, U_O2 = 184, 185, 249, 265, 281
UNITS = 289
PAIRS = (UNITS + 1) // 2


class Steps:

    def __init__(self, sem, names, ahead=1):
        self.sem, self.names, self.ahead, self.here = sem, names.split(), ahead, 0

    def open(self, e):
        e.sem_inc(self.sem, self.ahead * len(self.names))

    def count(self, turn, more):
        n = len(self.names)
        loop, t = turn if isinstance(turn, tuple) else (0, turn) if isinstance(turn, int) else (turn, 0)
        more += (t + self.ahead) * n
        assert more >= 0
        return more if isinstance(loop, int) and loop == 0 else loop * n + more

    def at(self, name, turn=0):
        return self.count(turn, self.names.index(name) + 1)

    def before(self, name, turn):
        return self.at(name, turn) - len(self.names) if isinstance(turn, int) else self.count(turn, self.names.index(name) + 1 - len(self.names))

    def next(self, e, turn=0):
        e.wait_ge(self.sem, self.count(turn, self.here % len(self.names)))
        return self

    def took(self, name, ins):
        want = self.names[self.here % len(self.names)]
        assert want == name, (name, want)
        self.here += 1
        ins.then_inc(self.sem, 1)


def program(nc, a):
    ctx = ExitStack()
    with ctx:
        base = [(nc.sbuf_base + 255) // 256 * 256]

        def put(name, shape, dt=F32, at=None):
            size = int(np.prod(shape[1:])) * 4
            if at is None:
                at = base[0]
                base[0] += (size + 31) // 32 * 32
                assert base[0] <= nc.sbuf_usable_end, (name, base[0], nc.sbuf_usable_end)
            return nc.alloc_sbuf_tensor_at(name, shape, dt, offset=at)

        def sem(name):
            return ctx.enter_context(nc.semaphore(name))

        const = put("const", [LANES, NCONST])
        par = put("par", [LANES, NPARAM])
        h = put("h", [LANES, KT, TOK])
        raw = put("raw", [LANES, 2, 2, KT, LANES])
        w_hi = put("w_hi", [LANES, 2, KT, LANES], F32R)
        w_lo = put("w_lo", [LANES, 2, KT, LANES], F32R)
        x0_at = base[0]
        x0h = put("x0h", [LANES, KT, TOK], F32R)
        x0l = put("x0l", [LANES, KT, TOK], F32R)
        x1h = put("x1h", [LANES, KT, TOK], F32R)
        x1l = put("x1l", [LANES, KT, TOK], F32R)
        acc_at = base[0]
        acc = put("acc", [LANES, TOK])
        sq = put("sq", [LANES, TOK])
        sd = put("sd", [LANES, TOK])
        R = put("R", [LANES, TOK])
        t32 = put("t32", [LANES, TOK])
        a32 = put("a32", [LANES, TOK])
        half_pi, eps6, eps5 = put("half_pi", [LANES, 1]), put("eps6", [LANES, 1]), put("eps5", [LANES, 1])
        own = base[0]
        room = nc.sbuf_usable_end - own

        def C(name, lo=0, hi=None, rows=LANES):
            a0, a1 = CC[name]
            return const[0:rows, a0 + lo:(a1 if hi is None else a0 + hi)]

        def V(name, lo=0, hi=None, rows=LANES):
            a0, a1 = PC[name]
            return par[0:rows, a0 + lo:(a1 if hi is None else a0 + hi)]

        def Vd(name, i):
            a0, a1 = PC[name]
            return par[:, a0 + i:a0 + i + 1] if isinstance(i, int) else par[:, bass.ds(i + a0, 1)]

        def tile(t, i):
            return t[:, i:i + 1] if isinstance(i, int) else t[:, bass.ds(i, 1)]

        def one(ap):
            return ap.rearrange("p (o n) -> p o n", o=1)

        bank = [ctx.enter_context(nc.psum_tensor(f"bank{i}", [LANES, TOK], F32)) for i in range(8)]
        bk = [b[:, :] for b in bank]

        loaded = sem("loaded")
        raw_loaded = [sem("raw_loaded_0"), sem("raw_loaded_1")]
        hi_split, w_split = sem("hi_split"), sem("w_split")
        unit_done, bank_free = sem("unit_done"), sem("bank_free")
        h_ready, x_hi, x_ready = sem("h_ready"), sem("x_hi"), sem("x_ready")
        squared, acc_ready, norm_mm, sd_ready, r_ready = (sem(n) for n in ("squared", "acc_ready", "norm_mm", "sd_ready", "r_ready"))
        stored = sem("stored")

        def after(u0, j, n4, more):
            return u0 + j + more + (n4 * 4)

        def pe_unit(e, u0, j, n4, xh, xl, first=None):
            b = bk[(u0 + j) % 4]
            w = (u0 + j) % 2
            e.wait_ge(w_split, after(u0, j, n4, 1))
            e.wait_ge(bank_free, after(u0, j, n4, 1))
            for k in range(KT):
                if first is not None:
                    e.wait_ge(*first(k))
                e.matmul(b, w_hi[:, w, k], xh[:, k], start=(k == 0), stop=False)
                e.matmul(b, w_hi[:, w, k], xl[:, k], start=False, stop=False)
                last = e.matmul(b, w_lo[:, w, k], xh[:, k], start=False, stop=(k == KT - 1))
            last.then_inc(unit_done, 1)

        def act_split(e, v0, n4, lead=False):
            if isinstance(n4, int) and v0 + 4 * n4 >= UNITS:
                return
            e.wait_ge(raw_loaded[(v0 // 2) % 2], n4 * 16 + (v0 // 4 + 1) * 16)
            if not lead:
                e.wait_ge(unit_done, n4 * 4 + (v0 - 1))
            e.activation(w_hi[:, v0 % 2], raw[:, (v0 // 2) % 2, v0 % 2], ACT.Copy).then_inc(hi_split, 1)

        def dve_split(e, v0, n4):
            if isinstance(n4, int) and v0 + 4 * n4 >= UNITS:
                return
            e.wait_ge(hi_split, n4 * 4 + (v0 + 1))
            e.tensor_tensor(w_lo[:, v0 % 2], raw[:, (v0 // 2) % 2, v0 % 2], w_hi[:, v0 % 2].bitcast(F32),
                            ALU.subtract).then_inc(w_split, 1)

        def evac_start(e, u0, j, n4):
            e.wait_ge(unit_done, after(u0, j, n4, 1))
            return bk[(u0 + j) % 4]

        def act_x(e, n, p, m, gain, xh):
            e.wait_ge(h_ready, m + (8 * n + 1))
            e.activation(tile(xh, m), tile(h, m), ACT.Copy, scale=Vd(gain, m)).then_inc(x_hi, 1)

        def dve_x(e, p, m, gain, xh, xl):
            e.wait_ge(x_hi, m + (8 * p + 1))
            e.scalar_tensor_tensor(tile(xl, m), tile(h, m), Vd(gain, m), tile(xh, m).bitcast(F32),
                                   ALU.mult, ALU.subtract).then_inc(x_ready, 1)

        def pool_start(e, n):
            if n:
                e.wait_ge(norm_mm, n)
                e.wait_ge(acc_ready, 8 * n)
            e.memset(acc[:, :], 0.0).then_inc(squared, 1)
            e.wait_ge(squared, 9 * n + 1)

        def pool_square(e, n, m):
            e.wait_ge(h_ready, m + (8 * n + 1))
            e.wait_ge(acc_ready, m + 8 * n)
            e.tensor_tensor(one(sq[:, :]), tile(h, m), tile(h, m), ALU.mult).then_inc(squared, 1)
            e.wait_ge(squared, m + (9 * n + 2))
            e.tensor_tensor(acc[:, :], acc[:, :], sq[:, :], ALU.add).then_inc(acc_ready, 1)

        def pe_norm(e, n):
            e.wait_ge(acc_ready, 8 * n + 8)
            e.matmul(bk[4], C("ones"), acc[:, :], start=True, stop=True).then_inc(norm_mm, 1)

        def act_norm(e, n, eps):
            e.wait_ge(norm_mm, n + 1)
            if n:
                e.wait_ge(r_ready, n)
            e.activation(sd[:, :], bk[4], ACT.Sqrt, bias=eps[:, :], scale=1.0 / DM).then_inc(sd_ready, 1)

        def dve_norm(e, n):
            e.wait_ge(sd_ready, n + 1)
            e.reciprocal(R[:, :], sd[:, :]).then_inc(r_ready, 1)
            e.wait_ge(r_ready, n + 1)

        def turns(e, n, body):
            if n == 4:
                for j in range(4):
                    body(0, j)
                return
            with e.Fori(0, n // 4) as i:
                for j in range(4):
                    body(i, j)

        at = [own]

        def own_buf(name, shape, dt=F32, lanes=LANES):
            at[0] = (at[0] + 31) // 32 * 32
            t = put(name, [lanes] + list(shape), dt, at=at[0])
            at[0] += int(np.prod(shape)) * 4
            assert at[0] <= nc.sbuf_usable_end, name
            return t

        B_st = own_buf("B_st", [2, SG, SH])
        C_st = own_buf("C_st", [2, SG, SH])
        xu = own_buf("xu", [SG, NSTEP])
        psi = own_buf("psi", [SG])
        mag8 = own_buf("mag8", [SG])
        ru = own_buf("ru", [NSTEP])
        TA = own_buf("TA", [2, SG, STEP + 1])
        PB = own_buf("PB", [2, SG, STEP])
        DI = own_buf("DI", [SG, SH], lanes=SH)
        sinb = own_buf("sinb", [GB, NSTEP])
        Vb = own_buf("Vb", [GB, NSTEP])
        Zb = own_buf("Zb", [GB, NSTEP])
        D0 = own_buf("D0", [GB, NSTEP])
        Wb = own_buf("Wb", [GB, NSTEP])
        tA = own_buf("tA", [GB, NSTEP])
        Ksb = own_buf("Ksb", [GB, STEP, SH], lanes=SH)
        Ysb = own_buf("Ysb", [STEP, GB, SH], lanes=NSTEP)
        at = [x0_at + 32768]
        small = {n: own_buf("s5_" + n, [SG]) for n in
                 "dt lrdt th k phi aphi k8 phi8 mag sn cs den rden nr c1 c2 t3 cr ci s2r s2i s4r s4i".split()}
        AR = own_buf("AR", [2, SG, STEP])
        cmA = own_buf("cmA", [SG, STEP])
        cmB = own_buf("cmB", [SG, STEP])
        ru3 = own_buf("ru3", [NSTEP, STEP])
        at = [x0_at]
        TB = own_buf("TB", [GB, STEP, SH])
        TBt = own_buf("TBt", [GB, STEP, SH])
        TC = own_buf("TC", [GB, STEP + 1, SH])
        TCt = own_buf("TCt", [GB, STEP + 1, SH])
        ST = own_buf("ST", [GB, LANES])
        Tm = own_buf("Tm", [GB, STEP, SH])
        Ub = own_buf("Ub", [GB, NSTEP])
        Sx = own_buf("Sx", [GB, NSTEP])
        cosb = own_buf("cosb", [GB, NSTEP])
        assert at[0] <= x0_at + 32768
        grid = lambda t: t[:, :].rearrange("p (g c) -> p g c", g=GB)
        ang, kk, ff, absf, tB, g32 = grid(acc), grid(sq), grid(sd), grid(t32), grid(R), a32

        zeroed, dt_ready, phase_ready, trig_ready, tables_ready, ru_ready = (
            sem(n) for n in ("zeroed", "dt_ready", "phase_ready", "trig_ready", "tables_ready", "ru_ready"))
        vec_chain, t_loaded, g_free = sem("vec_chain"), sem("t_loaded"), sem("g_free")
        D5 = Steps(sem("s5_vector"), "TB1 TB2 TB pr1 pr2 V Kd Z po1 po2 W")
        A5 = Steps(sem("s5_scalar"), "absf sin cos ST1 ST2 Sx K1 K2 Y1 Y2 g hi")
        E5 = Steps(sem("s5_tensor"), "ST1 ST2 S JS K1 K2 JZ Y1 Y2 YT")
        P5 = Steps(sem("s5_pool"), "U1 ang U k f D0 TC1 TC2 TC")
        chain = [0]

        def link(e, ins):
            chain[0] += 1
            ins.then_inc(vec_chain, 1)
            e.wait_ge(vec_chain, chain[0])

        def blkof(t, b):
            return t[:, bass.ds(b * GB, GB)] if not isinstance(b, int) else t[:, b * GB:(b + 1) * GB]

        def s5_loads(e):
            e.dma_start(const[:, :], a["const"]).then_inc(loaded, 16)
            e.dma_start(par[:, :], a["par"]).then_inc(loaded, 16)
            e.dma_start(h[:, :, :], a["xT"].rearrange("(k p) n -> p k n", p=LANES)).then_inc(loaded, 16)
            e.dma_start(B_st[:, :, :, :], a["B"]).then_inc(loaded, 16)
            e.dma_start(C_st[:, :, :, :], a["C"]).then_inc(loaded, 16)
            e.dma_start(xu[:, :, :], a["xu"]).then_inc(loaded, 16)

        def s5_sync(e):
            e.sem_inc(t_loaded, 16 * STEP)
            with e.Fori(0, NBLK) as b:
                e.wait_ge(D5.sem, D5.at("Kd", b))
                e.wait_ge(E5.sem, E5.before("Y2", b))
                for s in range(STEP):
                    e.dma_start(Tm[s * SH:(s + 1) * SH, :, s:STEP, :],
                                Ksb[:, :, 0:STEP - s, :]).then_inc(t_loaded, 16)

        def s5_pool(e):
            e.memset(Tm[:, :, :, :], 0.0).then_inc(zeroed, 1)
            P5.open(e)
            e.wait_ge(loaded, 96)
            pool_start(e, 0)
            for m in range(KT):
                pool_square(e, 0, m)
            e.wait_ge(tables_ready, 1)
            e.wait_ge(ru_ready, 1)
            full = [LANES, GB, NSTEP]
            with e.Fori(0, NBLK) as b:
                e.wait_ge(E5.sem, E5.before("Y2", b))
                P5.next(e, b).took("U1", e.tensor_tensor(Ub[:, :, :], blkof(xu, b), V("gain_u")[:, bass.ds(b * GB, GB)].unsqueeze(2).to_broadcast(full), ALU.mult))
                P5.next(e, b).took("ang", e.tensor_tensor(ang, blkof(psi, b).unsqueeze(2).to_broadcast(full), C("cidx").unsqueeze(1).to_broadcast(full), ALU.mult))
                P5.next(e, b).took("U", e.tensor_tensor(Ub[:, :, :], Ub[:, :, :], ru[:, :].unsqueeze(1).to_broadcast(full), ALU.mult))
                P5.took("k", e.tensor_scalar(kk, ang, ROUND, ROUND, ALU.add, ALU.subtract))
                e.wait_ge(P5.sem, P5.at("k", b))
                e.wait_ge(A5.sem, A5.before("sin", b))
                P5.next(e, b).took("f", e.tensor_tensor(ff, ang, kk, ALU.subtract))
                e.wait_ge(D5.sem, D5.before("Z", b))
                P5.next(e, b).took("D0", e.tensor_tensor(D0[:, :, :], blkof(mag8, b).unsqueeze(2).to_broadcast(full), C("cnz").unsqueeze(1).to_broadcast(full), ALU.mult))
                f4 = [LANES, GB, STEP + 1, SH]
                P5.next(e, b).took("TC1", e.tensor_tensor(TC[:, :, :, :], C_st[:, 0, bass.ds(b * GB, GB), :].unsqueeze(2).to_broadcast(f4), TA[:, 0, bass.ds(b * GB, GB), :].unsqueeze(3).to_broadcast(f4), ALU.mult))
                P5.next(e, b).took("TC2", e.tensor_tensor(TCt[:, :, :, :], C_st[:, 1, bass.ds(b * GB, GB), :].unsqueeze(2).to_broadcast(f4), TA[:, 1, bass.ds(b * GB, GB), :].unsqueeze(3).to_broadcast(f4), ALU.mult))
                e.wait_ge(P5.sem, P5.at("TC2", b))
                P5.next(e, b).took("TC", e.tensor_tensor(TC[:, :, :, :], TC[:, :, :, :], TCt[:, :, :, :], ALU.add))

        def s5_scalar(e):
            s = small
            A5.open(e)
            e.wait_ge(loaded, 96)
            e.activation(s["dt"][:, :], V("log_dt"), ACT.Exp).then_inc(dt_ready, 1)
            e.wait_ge(phase_ready, 1)
            e.activation(s["mag"][:, :], s["lrdt"][:, :], ACT.Exp)
            e.activation(mag8[:, :], s["lrdt"][:, :], ACT.Exp, scale=8.0)
            e.activation(s["sn"][:, :], s["phi"][:, :], ACT.Sin)
            e.activation(s["cs"][:, :], s["aphi"][:, :], ACT.Sin, bias=half_pi[:, :], scale=-1.0).then_inc(trig_ready, 1)
            act_norm(e, 0, eps6)
            with e.Fori(0, NBLK) as b:
                e.wait_ge(P5.sem, P5.at("f", b))
                A5.next(e, b).took("absf", e.activation(absf, ff, ACT.Abs))
                e.wait_ge(D5.sem, D5.before("po2", b))
                A5.next(e, b).took("sin", e.activation(sinb[:, :, :], ff, ACT.Sin, scale=SIN_SCALE))
                e.wait_ge(A5.sem, A5.at("absf", b))
                A5.next(e, b).took("cos", e.activation(cosb[:, :, :], absf, ACT.Sin, bias=half_pi[:, :], scale=-SIN_SCALE))
                for i in (1, 2):
                    e.wait_ge(E5.sem, E5.at(f"ST{i}", b))
                    A5.next(e, b).took(f"ST{i}", e.activation(ST[:, 4 * i - 4:4 * i, :], bk[i - 1].rearrange("p (g n) -> p g n", g=4), ACT.Copy))
                e.wait_ge(E5.sem, E5.at("S", b))
                A5.next(e, b).took("Sx", e.activation(Sx[:, :, :], grid(bank[2]), ACT.Copy))
                e.wait_ge(t_loaded, b * (16 * STEP) + 16 * STEP)
                for i in (1, 2):
                    e.wait_ge(E5.sem, E5.at(f"K{i}", b))
                    A5.next(e, b).took(f"K{i}", e.activation(Ksb[:, 4 * i - 4:4 * i, :, :], bank[4 + i][0:SH, :].rearrange("p (g s h) -> p g s h", g=4, s=STEP), ACT.Copy))
                for i in (1, 2):
                    e.wait_ge(E5.sem, E5.at(f"Y{i}", b))
                    A5.next(e, b).took(f"Y{i}", e.activation(Ysb[:, :, 4 * i - 4:4 * i, :].rearrange("p s g h -> p g s h"), bank[i - 1][0:NSTEP, :].rearrange("p (g s h) -> p g s h", g=4, s=STEP), ACT.Copy))
                e.wait_ge(E5.sem, E5.at("YT", b))
                e.wait_ge(g_free, b + 1)
                tok = bk[7].rearrange("p (s c) -> p s c", s=STEP)
                A5.next(e, b).took("g", e.activation(g32[:, :].rearrange("p (c s) -> p s c", s=STEP), tok, ACT.Gelu_apprx_tanh))
                A5.next(e, b).took("hi", e.activation(x1h[:, bass.ds(b, 1), :].rearrange("p o (c s) -> p (o s) c", s=STEP), tok, ACT.Gelu_apprx_tanh))
            e.sem_inc(x_hi, 8)

        def s5_vector(e):
            s = small
            v = lambda n: s[n][:, :]
            e.memset(half_pi[:, :], math.pi / 2)
            e.memset(eps6[:, :], 1e-6)
            e.memset(eps5[:, :], 1e-5)
            e.memset(Wb[:, :, 0:1], 0.0).then_inc(zeroed, 1)
            e.sem_inc(g_free, 1)
            D5.open(e)
            e.wait_ge(loaded, 96)
            e.sem_inc(h_ready, 8)
            e.wait_ge(dt_ready, 1)
            tt, ts = e.tensor_tensor, e.tensor_scalar
            link(e, tt(v("lrdt"), V("lam_re"), v("dt"), ALU.mult))
            link(e, tt(v("th"), V("lam_im"), v("dt"), ALU.mult))

            def reduced(out, x, k):
                link(e, ts(v(k), v(x), 1.0 / (2 * math.pi), ROUND, ALU.mult, ALU.add))
                link(e, ts(v(k), v(k), ROUND, None, ALU.subtract))
                link(e, e.scalar_tensor_tensor(v(out), v(k), -TWO_PI_HI, v(x), ALU.mult, ALU.add))
                link(e, e.scalar_tensor_tensor(v(out), v(k), -TWO_PI_LO, v(out), ALU.mult, ALU.add))

            reduced("phi", "th", "k")
            link(e, ts(v("th"), v("phi"), 8.0, None, ALU.mult))
            link(e, ts(v("phi"), v("phi"), PI_SAFE, -PI_SAFE, ALU.min, ALU.max))
            link(e, e.scalar_tensor_tensor(v("aphi"), v("phi"), -1.0, v("phi"), ALU.mult, ALU.max))
            e.sem_inc(phase_ready, 1)
            reduced("phi8", "th", "k8")
            link(e, ts(psi[:, :], v("phi8"), 1.0 / (2 * math.pi), None, ALU.mult))
            e.wait_ge(trig_ready, 1)
            ar, ai = TA[:, 0, :, 1], TA[:, 1, :, 1]
            e.memset(TA[:, 0, :, 0:1], 1.0)
            e.memset(TA[:, 1, :, 0:1], 0.0)
            e.memset(AR[:, 0, :, 7:8], 1.0)
            e.memset(AR[:, 1, :, 7:8], 0.0)
            link(e, tt(ar, v("mag"), v("cs"), ALU.mult))
            link(e, tt(ai, v("mag"), v("sn"), ALU.mult))
            link(e, tt(v("den"), V("lam_re"), V("lam_re"), ALU.mult))
            link(e, tt(v("t3"), V("lam_im"), V("lam_im"), ALU.mult))
            link(e, tt(v("den"), v("den"), v("t3"), ALU.add))
            link(e, e.reciprocal(v("rden"), v("den")))
            link(e, ts(v("nr"), ar, -1.0, None, ALU.add))
            link(e, tt(v("c1"), v("nr"), V("lam_re"), ALU.mult))
            link(e, tt(v("c2"), ai, V("lam_im"), ALU.mult))
            link(e, tt(v("c1"), v("c1"), v("c2"), ALU.add))
            link(e, tt(v("cr"), v("c1"), v("rden"), ALU.mult))
            link(e, tt(v("c1"), ai, V("lam_re"), ALU.mult))
            link(e, tt(v("c2"), v("nr"), V("lam_im"), ALU.mult))
            link(e, tt(v("c1"), v("c1"), v("c2"), ALU.subtract))
            link(e, tt(v("ci"), v("c1"), v("rden"), ALU.mult))

            def cmul(o, x, y, n):
                A, B = cmA[:, :, 0:n], cmB[:, :, 0:n]
                yr, yi = (q.unsqueeze(2).to_broadcast([LANES, SG, n]) for q in y)
                link(e, tt(A, x[0], yr, ALU.mult))
                link(e, tt(B, x[1], yi, ALU.mult))
                link(e, tt(o[0], A, B, ALU.subtract))
                link(e, tt(A, x[0], yi, ALU.mult))
                link(e, tt(B, x[1], yr, ALU.mult))
                link(e, tt(o[1], A, B, ALU.add))

            def cols(t, lo, hi):
                return t[:, 0, :, lo:hi], t[:, 1, :, lo:hi]

            a1 = (ar, ai)
            a2 = (v("s2r"), v("s2i"))
            a4 = (v("s4r"), v("s4i"))
            u2 = lambda q: tuple(x.unsqueeze(2) for x in q)
            cmul(u2(a2), u2(a1), a1, 1)
            cmul(u2(a4), u2(a2), a2, 1)
            cmul(cols(TA, 8, 9), u2(a4), a4, 1)
            cmul(cols(TA, 2, 4), cols(TA, 0, 2), a2, 2)
            cmul(cols(TA, 4, 8), cols(TA, 0, 4), a4, 4)
            link(e, e.tensor_copy(AR[:, :, :, 6:7], TA[:, :, :, 1:2]))
            cmul(cols(AR, 4, 6), cols(AR, 6, 8), a2, 2)
            cmul(cols(AR, 0, 4), cols(AR, 4, 8), a4, 4)
            cmul(cols(PB, 0, 8), cols(AR, 0, 8), (v("cr"), v("ci")), 8)
            link(e, ts(PB[:, 1], PB[:, 1], C("sgn"), None, ALU.mult))
            link(e, ts(TA[:, 0], TA[:, 0], C("nsgn"), None, ALU.mult))
            link(e, ts(TA[:, 1], TA[:, 1], -1.0, None, ALU.mult))
            dfull = [SH, SG, SH]
            link(e, tt(DI[:, :, :], V("d_h", rows=SH).unsqueeze(2).to_broadcast(dfull), C("id16", rows=SH).unsqueeze(1).to_broadcast(dfull), ALU.mult))
            e.sem_inc(tables_ready, 1)
            dve_norm(e, 0)
            rf = [LANES, NSTEP, STEP]
            link(e, tt(ru3[:, :, :], R[:, :].rearrange("p (c s) -> p c s", s=STEP), C("sel").unsqueeze(1).to_broadcast(rf), ALU.mult))
            e.reduce_sum(ru[:, :].unsqueeze(2), ru3[:, :, :], axis=AX.X).then_inc(ru_ready, 1)

            f4 = [LANES, GB, STEP, SH]

            def block(b, first):
                w5 = lambda n: e.wait_ge(D5.sem, D5.at(n, b))
                bb = (b * GB, GB)
                cut = (lambda t: t[:, 0:GB]) if first else (lambda t: t[:, bass.ds(*bb)])
                e.wait_ge(E5.sem, E5.before("K2", b))
                D5.next(e, b).took("TB1", tt(TB[:, :, :, :], cut(B_st[:, 0]).unsqueeze(2).to_broadcast(f4), cut(PB[:, 0]).unsqueeze(3).to_broadcast(f4), ALU.mult))
                D5.next(e, b).took("TB2", tt(TBt[:, :, :, :], cut(B_st[:, 1]).unsqueeze(2).to_broadcast(f4), cut(PB[:, 1]).unsqueeze(3).to_broadcast(f4), ALU.mult))
                w5("TB2")
                D5.next(e, b).took("TB", tt(TB[:, :, :, :], TB[:, :, :, :], TBt[:, :, :, :], ALU.add))
                if not first:
                    e.wait_ge(A5.sem, A5.before("hi", b))
                    e.tensor_tensor(x1l[:, bass.ds(b - 1, 1)], one(g32[:, :]), x1h[:, bass.ds(b - 1, 1)].bitcast(F32), ALU.subtract).then_inc(x_ready, 1)
                    e.wait_ge(x_ready, b)
                    e.sem_inc(g_free, 1)
                e.wait_ge(A5.sem, A5.at("Sx", b))
                D5.next(e, b).took("pr1", tt(tA[:, :, :], Sx[:, :, :], cosb[:, :, :], ALU.mult))
                e.wait_ge(E5.sem, E5.at("JS", b))
                D5.next(e, b).took("pr2", tt(tB, grid(bank[3]), sinb[:, :, :], ALU.mult))
                w5("pr2")
                D5.next(e, b).took("V", tt(Vb[:, :, :], tA[:, :, :], tB, ALU.subtract))
                e.wait_ge(A5.sem, A5.at("K2", b))
                D5.next(e, b).took("Kd", tt(Ksb[:, :, 0, :], Ksb[:, :, 0, :], cut(DI), ALU.add))
                e.wait_ge(P5.sem, P5.at("D0", b))
                w5("V")
                flat = lambda t: t[:, :, :].rearrange("p g c -> p (g c)")
                D5.next(e, b).took("Z", e.tensor_tensor_scan(flat(Zb), flat(D0), flat(Vb), 0.0, ALU.mult, ALU.add))
                w5("Z")
                D5.next(e, b).took("po1", tt(tA[:, :, :], Zb[:, :, :], cosb[:, :, :], ALU.mult))
                e.wait_ge(E5.sem, E5.at("JZ", b))
                D5.next(e, b).took("po2", tt(tB, grid(bank[3]), sinb[:, :, :], ALU.mult))
                w5("po2")
                e.wait_ge(E5.sem, E5.before("Y2", b))
                D5.next(e, b).took("W", tt(Wb[:, :, 1:], tA[:, :, :NSTEP - 1], tB[:, :, :NSTEP - 1], ALU.add))

            block(0, True)
            with e.Fori(1, NBLK) as b:
                block(b, False)
            e.wait_ge(A5.sem, A5.at("hi", NBLK - 1))
            e.tensor_tensor(x1l[:, NBLK - 1], g32[:, :], x1h[:, NBLK - 1].bitcast(F32), ALU.subtract).then_inc(x_ready, 1)

        def s5_tensor(e):
            E5.open(e)
            pe_norm(e, 0)
            e.wait_ge(zeroed, 2)
            with e.Fori(0, NBLK) as b:
                e.wait_ge(D5.sem, D5.at("TB", b))
                for i in (1, 2):
                    e.wait_ge(A5.sem, A5.before(f"Y{i}", b))
                    for g in range(4):
                        last = e.transpose(bank[i - 1][:, g * LANES:(g + 1) * LANES], TB[:, 4 * i - 4 + g].rearrange("p s h -> p (s h)"), C("ident"))
                    E5.took(f"ST{i}", last)
                e.wait_ge(P5.sem, P5.at("U", b))
                e.wait_ge(A5.sem, A5.at("ST2", b))
                for g in range(GB):
                    last = e.matmul(bank[2][:, g * NSTEP:(g + 1) * NSTEP], ST[:, g], Ub[:, g], start=True, stop=True)
                E5.took("S", last)
                e.wait_ge(A5.sem, A5.at("Sx", b))
                e.wait_ge(D5.sem, D5.before("po2", b))
                E5.took("JS", e.matmul(bk[3], C("turn"), Sx[:, :, :].rearrange("p g c -> p (g c)"), start=True, stop=True))
                e.wait_ge(P5.sem, P5.at("TC", b))
                for i in (1, 2):
                    e.wait_ge(A5.sem, A5.before(f"K{i}", b))
                    for g in range(4):
                        gg = 4 * i - 4 + g
                        last = e.matmul(bank[4 + i][0:SH, g * LANES:(g + 1) * LANES], TB[:, gg, STEP - 1], TC[:, gg, 0:STEP].rearrange("p s h -> p (s h)"), start=True, stop=True)
                    E5.took(f"K{i}", last)
                e.wait_ge(D5.sem, D5.at("Z", b))
                E5.took("JZ", e.matmul(bk[3], C("turn"), Zb[:, :, :].rearrange("p g c -> p (g c)"), start=True, stop=True))
                e.wait_ge(D5.sem, D5.at("W", b))
                e.wait_ge(t_loaded, b * (16 * STEP) + 32 * STEP)
                for i in (1, 2):
                    for g in range(4):
                        gg = 4 * i - 4 + g
                        o = bank[i - 1][0:NSTEP, g * LANES:(g + 1) * LANES]
                        e.matmul(o, Ub[:, gg], Tm[:, gg].rearrange("p s h -> p (s h)"), start=True, stop=False)
                        last = e.matmul(o, Wb[:, gg], TC[:, gg, 1:].rearrange("p s h -> p (s h)"), start=False, stop=True)
                    E5.took(f"Y{i}", last)
                e.wait_ge(A5.sem, A5.at("Y2", b))
                e.wait_ge(A5.sem, A5.before("hi", b))
                for t in range(STEP):
                    turned = e.transpose if t else e.matmul
                    last = turned(bank[7][:, t * NSTEP:(t + 1) * NSTEP], Ysb[:, t].rearrange("p g h -> p (g h)"), C("ident", hi=NSTEP, rows=NSTEP))
                E5.took("YT", last)

        sg = Zb[:, :, :].rearrange("p g c -> p (g c)")
        sg_ready = sem("sg_ready")

        def glu_scalar(e):
            def body(i, j):
                act_split(e, U_GLU + j + 2, i)
                if j % 2 == 0:
                    e.wait_ge(unit_done, after(U_GLU, j, i, 1))
                    e.wait_ge(bank_free, after(U_GLU, j, i, 4))
                    e.activation(sg, bk[(U_GLU + j) % 4], ACT.Sigmoid).then_inc(sg_ready, 1)
                else:
                    act_x(e, 1, 1, i * 2 + j // 2, "mlp0", x0h)
            turns(e, 16, body)

        def glu_vector(e):
            def body(i, j):
                dve_split(e, U_GLU + j + 2, i)
                m = i * 2 + j // 2
                if j % 2 == 0:
                    e.wait_ge(sg_ready, m + 1)
                    e.sem_inc(bank_free, 1)
                else:
                    b = evac_start(e, U_GLU, j, i)
                    e.tensor_tensor(t32[:, :], b, sg, ALU.mult).then_inc(bank_free, 1)
                    e.wait_ge(bank_free, after(U_GLU, j, i, 5))
                    e.tensor_tensor(tile(h, m), tile(h, m), one(t32[:, :]), ALU.add).then_inc(h_ready, 1)
                    e.wait_ge(h_ready, m + 9)
                    dve_x(e, 1, m, "mlp0", x0h, x0l)
            turns(e, 16, body)

        def ready(s, n):
            return lambda k: (s, n + (k + 1))

        def glu_tensor(e):
            turns(e, 16, lambda i, j: pe_unit(e, U_GLU, j, i, x1h, x1l, ready(x_ready, 0) if j == 0 else None))

        def pool_h(e, n, steps=KT):
            pool_start(e, n)
            with e.Fori(0, steps) as m:
                pool_square(e, n, m)

        a_hi, a_ready = sem("a_hi"), sem("a_ready")

        def mlp_parts(i, n, p_in, p_out, gain):
            u0 = (U_MLP0, U_MLP1)[i]
            a0 = 32 * i

            def up_scalar(e, q):
                def body(t, j):
                    act_split(e, u0 + j + 2, q * 4 + t)
                    m = t * 4 + j
                    e.wait_ge(bank_free, after(u0, j, q * 4 + t, 5))
                    e.activation(tile(x1h, m), one(t32[:, :]), ACT.Square).then_inc(a_hi, 1)
                    e.wait_ge(a_ready, q * 8 + m + (a0 + 1))
                    e.activation(a32[:, :], t32[:, :], ACT.Square).then_inc(a_hi, 1)
                turns(e, 8, body)

            def up_vector(e, q):
                def body(t, j):
                    dve_split(e, u0 + j + 2, q * 4 + t)
                    m = t * 4 + j
                    b = evac_start(e, u0, j, q * 4 + t)
                    e.scalar_tensor_tensor(t32[:, :], b, 0.0, R[:, :], ALU.max, ALU.mult).then_inc(bank_free, 1)
                    e.wait_ge(a_hi, (q * 8 + m) * 2 + (2 * a0 + 2))
                    e.tensor_tensor(tile(x1l, m), one(a32[:, :]), tile(x1h, m).bitcast(F32), ALU.subtract).then_inc(a_ready, 1)
                turns(e, 8, body)

            def up_tensor(e, q):
                turns(e, 8, lambda t, j: pe_unit(e, u0, j, q * 4 + t, x0h, x0l, ready(x_ready, 8 * p_in) if j == 0 else None))

            def down_scalar(e, q, final):
                def body(t, j):
                    act_split(e, u0 + 8 + j + 2, q * 4 + t)
                    if final:
                        act_x(e, n, p_out, t * 4 + j, gain, x0h)
                turns(e, 8, body)

            def down_vector(e, q, final):
                def body(t, j):
                    dve_split(e, u0 + 8 + j + 2, q * 4 + t)
                    m = t * 4 + j
                    b = evac_start(e, u0 + 8, j, q * 4 + t)
                    e.tensor_tensor(tile(h, m), tile(h, m), one(b), ALU.add).then_inc(bank_free, 1)
                    if final:
                        e.wait_ge(bank_free, after(u0 + 8, j, q * 4 + t, 5))
                        e.sem_inc(h_ready, 1)
                        dve_x(e, p_out, m, gain, x0h, x0l)
                turns(e, 8, body)

            def down_tensor(e, q):
                turns(e, 8, lambda t, j: pe_unit(e, u0 + 8, j, q * 4 + t, x1h, x1l, (lambda k: (a_ready, q * 8 + (a0 + k + 2))) if j == 0 else None))

            def vector(e):
                if i == 0:
                    e.sem_inc(a_ready, 1)
                dve_norm(e, n - 1)
                with e.Fori(0, 3) as q:
                    up_vector(e, q)
                    down_vector(e, q, False)
                up_vector(e, 3)
                down_vector(e, 3, True)

            def scalar(e):
                act_norm(e, n - 1, eps6)
                with e.Fori(0, 3) as q:
                    up_scalar(e, q)
                    down_scalar(e, q, False)
                up_scalar(e, 3)
                down_scalar(e, 3, True)

            def tensor(e):
                pe_norm(e, n - 1)
                with e.Fori(0, 3) as q:
                    up_tensor(e, q)
                    down_tensor(e, q)
                up_tensor(e, 3)
                down_tensor(e, 3)

            return scalar, vector, tensor

        at = [own]
        p_in = own_buf("p_in", [2, 2, TOK])
        p_h, p_l = own_buf("p_h", [2, TOK], F32R), own_buf("p_l", [2, TOK], F32R)
        pp_at = at[0]
        Pp = own_buf("Pp", [KT, TOK])
        gs = own_buf("gs", [TOK])
        kept = at[0]
        p_loaded, p_hi, p_ready, p_mm, p_out = (sem(s) for s in ("p_loaded", "p_hi", "p_ready", "p_mm", "p_out"))

        def ple_parts(i, n, p_out_set, gain):
            up, u0 = (U_P0, U_P1)[i], (U_GATE0, U_GATE1)[i]

            def scalar(e):
                if i == 0:
                    e.wait_ge(p_loaded, 16)
                else:
                    e.wait_ge(unit_done, U_P1)
                e.activation(p_h[:, :, :], p_in[:, i], ACT.Copy).then_inc(p_hi, 1)
                for j in range(2):
                    act_split(e, up + j + 2, 0)
                    for mm in range(4):
                        t = 8 * i + 4 * j + mm
                        e.wait_ge(p_mm, t + 1)
                        e.activation(Pp[:, 4 * j + mm], bk[4 + mm], ACT.Copy).then_inc(p_out, 1)
                act_norm(e, n - 1, eps6)

                def body(t, j):
                    act_split(e, u0 + j + 2, t)
                    m = t * 4 + j
                    e.wait_ge(bank_free, after(u0, j, t, 5))
                    e.activation(gs[:, :], t32[:, :], ACT.Sigmoid).then_inc(sg_ready, 1)
                    if gain:
                        act_x(e, n, p_out_set, m, gain, x1h)
                turns(e, 8, body)

            def vector(e):
                e.wait_ge(p_hi, i + 1)
                e.tensor_tensor(p_l[:, :, :], p_in[:, i], p_h[:, :, :].bitcast(F32), ALU.subtract).then_inc(p_ready, 1)
                for j in range(2):
                    dve_split(e, up + j + 2, 0)
                    e.wait_ge(unit_done, up + j + 1)
                    e.sem_inc(bank_free, 1)
                dve_norm(e, n - 1)
                e.wait_ge(p_out, 8 * i + 8)

                def body(t, j):
                    dve_split(e, u0 + j + 2, t)
                    m = t * 4 + j
                    b = evac_start(e, u0, j, t)
                    e.tensor_tensor(t32[:, :], b, R[:, :], ALU.mult).then_inc(bank_free, 1)
                    e.wait_ge(sg_ready, m + (8 + 8 * i + 1))
                    e.tensor_tensor(one(a32[:, :]), one(gs[:, :]), tile(Pp, m), ALU.mult).then_inc(gated, 1)
                    e.wait_ge(gated, m + (8 * i + 1))
                    e.tensor_tensor(tile(h, m), tile(h, m), one(a32[:, :]), ALU.add).then_inc(h_ready, 1)
                    if gain:
                        dve_x(e, p_out_set, m, gain, x1h, x1l)
                turns(e, 8, body)

            def tensor(e):
                e.wait_ge(p_ready, i + 1)
                for j in range(2):
                    e.wait_ge(w_split, up + j + 1)
                    e.wait_ge(bank_free, up + j + 1)
                    for mm in range(4):
                        t = 8 * i + 4 * j + mm
                        if j:
                            e.wait_ge(p_out, t - 3)
                        w = (up + j) % 2
                        for k in range(2):
                            kk = 2 * mm + k
                            e.matmul(bk[4 + mm], w_hi[:, w, kk], p_h[:, k], start=(k == 0), stop=False)
                            e.matmul(bk[4 + mm], w_hi[:, w, kk], p_l[:, k], start=False, stop=False)
                            last = e.matmul(bk[4 + mm], w_lo[:, w, kk], p_h[:, k], start=False, stop=(k == 1))
                        last.then_inc(p_mm, 1)
                    e.wait_ge(p_mm, 8 * i + 4 * j + 4)
                    e.sem_inc(unit_done, 1)
                e.wait_ge(p_out, 8 * i + 8)
                pe_norm(e, n - 1)
                turns(e, 8, lambda t, j: pe_unit(e, u0, j, t, x0h, x0l, ready(x_ready, 8 * (p_out_set - 1)) if j == 0 else None))

            return scalar, vector, tensor

        gated = sem("gated")

        def more_x_scalar(e, n, p, gain, xh):
            with e.Fori(0, KT) as m:
                act_x(e, n, p, m, gain, xh)

        def more_x_vector(e, p, gain, xh, xl):
            with e.Fori(0, KT) as m:
                dve_x(e, p, m, gain, xh, xl)

        at = [kept]
        kdup = own_buf("kdup", [4, TOK])
        kv32 = own_buf("kv32", [4, TOK])
        v_tok = own_buf("v_tok", [4, 256])
        q32 = put("q32", [LANES, KT, TOK], at=pp_at)
        at = [x0_at]
        Ks = own_buf("Ks", [2, LANES + TOK])
        Qs = own_buf("Qs", [2, 2, TOK])
        Vs = own_buf("Vs", [2, 5, 64])
        Sm = own_buf("Sm", [4, 2, 2, 256])
        PT = put("PT", [LANES, 2, 512], at=acc_at)
        st = {n: own_buf("st_" + n, [4, 4]) for n in "mx nm df sm es rc".split()}
        assert at[0] <= x0_at + 32768
        rope_mm, kv_t, kv_tok, k_dup = sem("rope_mm"), sem("kv_t"), sem("kv_tok"), sem("k_dup")
        RO = Steps(sem("rope_steps"), "cos sin sum")

        def rope_tensor(e, u0, j, n4, src, turn):
            e.wait_ge(bank_free, after(u0, j, n4, 5))
            e.wait_ge(RO.sem, RO.at("sin", (turn[0], turn[1] - 2)))
            e.matmul(bk[5 + j % 2], C("ropeswap"), src, start=True, stop=True).then_inc(rope_mm, 1)

        def rope_vector(e, src, j, turn):
            RO.next(e, turn).took("cos", e.tensor_tensor(one(t32[:, :]), src, one(C("rcos")), ALU.mult))
            e.wait_ge(rope_mm, turn + 1 if isinstance(turn, int) else turn[0] + (turn[1] + 1))
            RO.next(e, turn).took("sin", e.tensor_tensor(a32[:, :], bk[5 + j % 2], C("rsin"), ALU.mult))
            RO.next(e, turn).took("sum", e.tensor_tensor(src, one(t32[:, :]), one(a32[:, :]), ALU.add))

        def kv_scalar(e):
            act_norm(e, 3, eps6)
            for j in range(4):
                act_split(e, U_KV + j + 2, 0)
                if j in (2, 3):
                    t = j - 2
                    e.wait_ge(RO.sem, RO.at("sum", t))
                    for half in range(2):
                        for to in range(2):
                            last = e.activation(kdup[64 * to:64 * to + 64, 2 * t + half], kv32[64 * half:64 * half + 64, t], ACT.Copy)
                            last.then_inc(k_dup, 1)
            for t in range(2):
                e.wait_ge(kv_t, t + 1)
                e.activation(v_tok[:, :, LANES * t:LANES * (t + 1)], bk[7 - 2 * t].rearrange("p (c n) -> p c n", c=4), ACT.Copy).then_inc(kv_tok, 1)

        def kv_vector(e):
            dve_norm(e, 3)
            RO.open(e)
            for j in range(4):
                dve_split(e, U_KV + j + 2, 0)
                b = evac_start(e, U_KV, j, 0)
                e.tensor_tensor(kv32[:, j], b, R[:, :], ALU.mult).then_inc(bank_free, 1)
                if j in (1, 2):
                    e.wait_ge(bank_free, U_KV + j + 4)
                    rope_vector(e, kv32[:, j - 1:j], j - 1, j - 1)

        def kv_tensor(e):
            pe_norm(e, 3)
            for j in range(4):
                pe_unit(e, U_KV, j, 0, x1h, x1l, ready(x_ready, 24) if j == 0 else None)
                if j in (1, 2):
                    e.wait_ge(bank_free, U_KV + j + 4)
                    e.matmul(bk[4 + j], C("ropeswap"), kv32[:, j - 1], start=True, stop=True).then_inc(rope_mm, 1)
            for t in range(2):
                e.wait_ge(bank_free, U_KV + 7 + t)
                if t:
                    e.wait_ge(RO.sem, RO.at("sin", 0))
                for c in range(4):
                    last = e.transpose(bank[7 - 2 * t][:, c * LANES:(c + 1) * LANES], kv32[:, 2 + t, c * LANES:(c + 1) * LANES], C("ident"))
                last.then_inc(kv_t, 1)

        def q_scalar(e):
            turns(e, 8, lambda t, j: act_split(e, U_Q + j + 2, t))

        def q_vector(e):
            def body(t, j):
                dve_split(e, U_Q + j + 2, t)
                m = t * 4 + j
                b = evac_start(e, U_Q, j, t)
                e.tensor_tensor(tile(q32, m), one(b), one(R[:, :]), ALU.mult).then_inc(bank_free, 1)
                if j:
                    e.wait_ge(bank_free, after(U_Q, j - 1, t, 5))
                    rope_vector(e, tile(q32, t * 4 + (j - 1)), j - 1, (t * 4, j + 1))
                if j == 3:
                    e.wait_ge(bank_free, after(U_Q, j, t, 5))
                    rope_vector(e, tile(q32, m), j, (t * 4, j + 2))
            turns(e, 8, body)

        def q_tensor(e):
            e.wait_ge(kv_tok, 2)

            def body(t, j):
                pe_unit(e, U_Q, j, t, x0h, x0l, ready(x_ready, 32) if j == 0 else None)
                m = t * 4 + j
                if j:
                    rope_tensor(e, U_Q, j - 1, t, tile(q32, t * 4 + (j - 1)), (t * 4, j + 1))
                if j == 3:
                    rope_tensor(e, U_Q, 3, t, tile(q32, m), (t * 4, j + 2))
            turns(e, 8, body)

        def piped(e, step, total, drain):
            for T in range(8):
                step(0, T)
            with e.Fori(1, total // 8) as i:
                for T in range(8):
                    step(i, T)
            for T in range(drain):
                step(total // 8, T)

        def runs(i, q, total):
            return not isinstance(i, int) or 0 <= 8 * i + q < total

        PKQ = Steps(sem("att_copies"), "K Q V")
        DA = Steps(sem("att_max"), "m0 m1 max sink neg dif", ahead=8)
        AB = Steps(sem("att_exp"), "e0 e1 e2 e3 es", ahead=8)
        DC = Steps(sem("att_scale"), "den rec scale", ahead=8)
        ES = Steps(sem("att_scores"), "s", ahead=8)
        ED = Steps(sem("att_turned"), "t0 t1", ahead=8)
        AE = Steps(sem("att_weights"), "w0 w1", ahead=8)
        EF = Steps(sem("att_out"), "o", ahead=8)
        AG = Steps(sem("att_out_hi"), "hi", ahead=8)
        DH = Steps(sem("att_out_lo"), "lo", ahead=8)
        pads = sem("pads")
        NT = 16

        def att_pool(e):
            PKQ.open(e)
            e.wait_ge(unit_done, U_O)
            for t, cut in ((Ks, Ks[:, :, 0:LANES]), (Vs, Vs[:, :, 0])):
                e.memset(cut, 0.0).then_inc(pads, 1)
            e.wait_ge(RO.sem, RO.at("sum", 9))
            e.wait_ge(k_dup, 8)
            e.wait_ge(kv_tok, 2)
            with e.Fori(0, 2) as i:
                for x in range(2):
                    kh = (i * 2, x)
                    e.wait_ge(ES.sem, ES.at("s", (i * 8, 4 * x - 5)))
                    PKQ.next(e, kh).took("K", e.tensor_copy(Ks[:, x:x + 1, LANES:], tile(kdup, i * 2 + x)))
                    PKQ.next(e, kh).took("Q", e.tensor_copy(Qs[:, x], q32[:, bass.ds(i * 4 + 2 * x, 2)]))
                    e.wait_ge(EF.sem, EF.at("o", (i * 8, 4 * x - 5)))
                    PKQ.next(e, kh).took("V", e.tensor_copy(Vs[:, x, 1:5], v_tok[:, :, bass.ds(i * 128 + 64 * x, 64)]))

        def att_tensor(e):
            for s in (ES, ED, EF):
                s.open(e)
            e.wait_ge(pads, 2)

            def step(i, T):
                if runs(i, T, NT):
                    x, n, b = T // 4, T % 4, 2 * (T % 2)
                    if n == 0:
                        e.wait_ge(PKQ.sem, PKQ.at("Q", (i * 2, x)))
                    e.wait_ge(DA.sem, DA.at("m1", (i * 8, T - 2)))
                    for g in range(4):
                        hf, gg = g % 2, g // 2
                        last = e.matmul(bank[b + hf][:, gg * 256:gg * 256 + 256], Qs[64 * hf:64 * hf + 64, x, gg, n * LANES:(n + 1) * LANES],
                                        Ks[64 * hf:64 * hf + 64, x, n * LANES:(n + 2) * LANES], start=True, stop=True)
                    ES.took("s", last)
                q = T - 3
                if runs(i, q, NT):
                    e.wait_ge(DC.sem, DC.at("scale", (i * 8, q)))
                    for kt in range(2):
                        e.wait_ge(AE.sem, AE.at(f"w{kt}", (i * 8, q - 1)))
                        for g in range(4):
                            last = e.transpose(bank[5 + kt][:, g * LANES:(g + 1) * LANES], Sm[:, q % 4, g // 2, g % 2, kt * LANES:(kt + 1) * LANES], C("ident"))
                        ED.took(f"t{kt}", last)
                q = T - 4
                if runs(i, q, NT):
                    x, n = q % 8 // 4, q % 4
                    if n == 0:
                        e.wait_ge(PKQ.sem, PKQ.at("V", (i * 2, q // 4)))
                    e.wait_ge(AE.sem, AE.at("w1", (i * 8, q)))
                    e.wait_ge(DH.sem, DH.at("lo", (i * 8, q - 2)))
                    for hf in range(2):
                        for kt in range(2):
                            last = e.matmul(bank[7 - 3 * (q % 2)][64 * hf:64 * hf + 64, 0:256], Vs[:, x, n + kt], PT[:, kt, hf * 256:hf * 256 + 256], start=(kt == 0), stop=(kt == 1))
                    EF.took("o", last)
            piped(e, step, NT, 6)

        def att_vector(e):
            for s in (DA, DC, DH):
                s.open(e)

            def step(i, T):
                if runs(i, T, NT):
                    b, z, t = 2 * (T % 2), T % 4, (i * 8, T)
                    e.wait_ge(ES.sem, ES.at("s", t))
                    e.wait_ge(ED.sem, ED.at("t1", (i * 8, T - 4)))
                    mask = C("band0" if T % 4 == 0 else "band").unsqueeze(1).to_broadcast([LANES, 2, 256])
                    for hf in range(2):
                        DA.took(f"m{hf}", e.scalar_tensor_tensor(Sm[:, z, hf], bank[b + hf][:, :].rearrange("p (g k) -> p g k", g=2), 0.125, mask, ALU.mult, ALU.add))
                    flat = Sm[:, z].rearrange("p a b k -> p (a b) k")
                    DA.next(e, t).took("max", e.reduce_max(st["mx"][:, z].unsqueeze(2), flat, axis=AX.X))
                    s0 = PC["sinks"][0]
                    sk = par[:, bass.ds(i * 8 + (s0 + 4 * (T // 4)), 4)].rearrange("p (g f) -> p f g", f=2)
                    v = lambda nm: st[nm][:, z].rearrange("p (f g) -> p f g", f=2)
                    DA.next(e, t).took("sink", e.tensor_tensor(v("mx"), v("mx"), sk, ALU.max))
                    DA.next(e, t).took("neg", e.tensor_scalar(st["nm"][:, z], st["mx"][:, z], -1.0, None, ALU.mult))
                    DA.next(e, t).took("dif", e.tensor_tensor(v("df"), sk, v("mx"), ALU.subtract))
                q = T - 2
                if runs(i, q, NT):
                    t, z = (i * 8, q), q % 4
                    e.wait_ge(AB.sem, AB.at("es", t))
                    DC.next(e, t).took("den", e.tensor_tensor(st["rc"][:, z], st["sm"][:, z], st["es"][:, z], ALU.add))
                    DC.next(e, t).took("rec", e.reciprocal(st["rc"][:, z], st["rc"][:, z]))
                    flat = Sm[:, z].rearrange("p a b k -> p (a b) k")
                    DC.next(e, t).took("scale", e.tensor_tensor(flat, flat, st["rc"][:, z].unsqueeze(2).to_broadcast([LANES, 4, 256]), ALU.mult))
                q = T - 5
                if runs(i, q, NT):
                    e.wait_ge(AG.sem, AG.at("hi", (i * 8, q)))
                    DH.took("lo", e.tensor_tensor(o_tiles(x1l, i, q), o_bank(q), o_tiles(x1h, i, q).bitcast(F32), ALU.subtract))
            piped(e, step, NT, 6)

        def o_tiles(x1, i, q):
            n, k = q % 4, 2 * (q // 4)
            return x1[:, i * 4 + k:i * 4 + k + 2, n * LANES:(n + 1) * LANES] if isinstance(i, int) else x1[:, bass.ds(i * 4 + k, 2), n * LANES:(n + 1) * LANES]

        def o_bank(q):
            return bank[7 - 3 * (q % 2)][:, 0:256].rearrange("p (g q) -> p g q", g=2)

        def att_scalar(e):
            for s in (AB, AE, AG):
                s.open(e)

            def step(i, T):
                q = T - 1
                if runs(i, q, NT):
                    z = q % 4
                    e.wait_ge(DA.sem, DA.at("dif", (i * 8, q)))
                    for g in range(4):
                        s = Sm[:, z, g // 2, g % 2]
                        AB.took(f"e{g}", e.activation(s, s, ACT.Exp, bias=st["nm"][:, z, g:g + 1], accum_out=st["sm"][:, z, g:g + 1]))
                    AB.took("es", e.activation(st["es"][:, z], st["df"][:, z], ACT.Exp))
                q = T - 3
                if runs(i, q, NT):
                    e.wait_ge(EF.sem, EF.at("o", (i * 8, q - 1)))
                    for kt in range(2):
                        e.wait_ge(ED.sem, ED.at(f"t{kt}", (i * 8, q)))
                        AE.took(f"w{kt}", e.activation(PT[:, kt], bk[5 + kt], ACT.Copy))
                q = T - 4
                if runs(i, q, NT):
                    e.wait_ge(EF.sem, EF.at("o", (i * 8, q)))
                    AG.took("hi", e.activation(o_tiles(x1h, i, q), o_bank(q), ACT.Copy))
            piped(e, step, NT, 6)

        def wo_scalar(e):
            def body(t, j):
                act_split(e, U_O + j + 2, t)
                act_x(e, 4, 5, t * 4 + j, "mlp1", x0h)
            turns(e, 8, body)

        def wo_vector(e):
            def body(t, j):
                dve_split(e, U_O + j + 2, t)
                m = t * 4 + j
                b = evac_start(e, U_O, j, t)
                e.tensor_tensor(tile(h, m), tile(h, m), one(b), ALU.add).then_inc(bank_free, 1)
                e.wait_ge(bank_free, after(U_O, j, t, 5))
                e.sem_inc(h_ready, 1)
                dve_x(e, 5, m, "mlp1", x0h, x0l)
            turns(e, 8, body)

        def wo_tensor(e):
            def there(k):
                return DH.sem, DH.at("lo", 4 * (k // 2) + 3)
            turns(e, 8, lambda t, j: pe_unit(e, U_O, j, t, x1h, x1l, there if j == 0 else None))

        def final1_scalar(e):
            act_norm(e, 6, eps6)
            more_x_scalar(e, 7, 7, "a_norm", x1h)

        def final1_vector(e):
            dve_norm(e, 6)
            with e.Fori(0, KT) as m:
                e.scalar_tensor_tensor(tile(h, m), tile(h, m), Vd("final", m), one(R[:, :]), ALU.mult, ALU.mult).then_inc(h_ready, 1)
                e.wait_ge(h_ready, m + 57)
                dve_x(e, 7, m, "a_norm", x1h, x1l)

        def final1_tensor(e):
            pe_norm(e, 6)

        NC_, HEADS, HG, HP = 4, 32, 4, 64
        at = [kept]
        at = [own]
        T4 = own_buf("T4", [4, NC_, HEADS])
        G4 = own_buf("G4", [4, NC_, HG])
        zd = own_buf("zd", [NC_, HEADS]); az = own_buf("az", [NC_, HEADS]); s1 = own_buf("s1", [NC_, HEADS])
        s2_ = own_buf("s2_", [NC_, HEADS]); pq = own_buf("pq", [NC_, HEADS]); ea = own_buf("ea", [HEADS])
        dtr = own_buf("dtr", [TOK], lanes=HEADS)
        pre = own_buf("pre", [2, TOK + 3])
        cv = own_buf("cv", [2, TOK])
        at[0] = (at[0] + 31) // 32 * 32
        xt = own_buf("xt", [4, TOK])
        bct = own_buf("bct", [4, TOK])
        zs = own_buf("zs", [4, TOK])
        xdt = own_buf("xdt", [NC_, HG, HP]); xw = own_buf("xw", [NC_, HG, HP])
        btok = own_buf("btok", [NC_, LANES]); cbm = own_buf("cbm", [NC_, LANES])
        dec = own_buf("dec", [2, HG, LANES]); ecs = own_buf("ecs", [2, HG, LANES]); cs = own_buf("cs", [2, HG, LANES])
        state = own_buf("state", [HG, HP])
        uu = own_buf("uu", [2, TOK])
        usq = put("usq", [LANES, 2, TOK], at=acc_at)
        dts, dtx, dtt, dta = (sem(n) for n in ("dt_turned", "dt_exp", "dt_cumulated", "dt_act"))
        DM1 = Steps(sem("dt_steps"), "raw z az den r s s2 p17 p15 p13 p11 p9 p7 p5 p3 l mz dt adt nacs dif")

        def dt_scalar(e):
            act_norm(e, 7, eps5)
            act_split(e, U_DT + 2, 0)
            e.activation(ea[:, :], V("a_log"), ACT.Exp)
            e.wait_ge(DM1.sem, DM1.at("az"))
            e.activation(s1[:, :, :], az[:, :, :], ACT.Exp, scale=-1.0).then_inc(dtx, 1)
            e.wait_ge(DM1.sem, DM1.at("dif"))
            e.activation(T4[:, 3], zd[:, :, :], ACT.Exp).then_inc(dta, 1)

        def dt_vector(e):
            tt, ts, stt = e.tensor_tensor, e.tensor_scalar, e.scalar_tensor_tensor
            d = lambda name, ins: DM1.took(name, ins)
            n = lambda: DM1.next(e)
            DM1.open(e)
            dve_norm(e, 7)
            dve_split(e, U_DT + 2, 0)
            b = evac_start(e, U_DT, 0, 0)
            d("raw", tt(dtr[:, :], bank[U_DT % 4][0:HEADS, :], R[0:HEADS, :], ALU.mult))
            n()
            e.sem_inc(bank_free, 1)
            for t in (pre,):
                e.memset(t[:, :, 0:3], 0.0)
            e.wait_ge(dts, 1)
            full = [LANES, NC_, HEADS]
            n(); d("z", tt(zd[:, :, :], bank[5][:, 0:128].rearrange("p (c h) -> p c h", c=NC_), V("dt_bias").unsqueeze(1).to_broadcast(full), ALU.add))
            n(); d("az", stt(az[:, :, :], zd[:, :, :], -1.0, zd[:, :, :], ALU.mult, ALU.max))
            e.wait_ge(dtx, 1)
            n(); d("den", ts(pq[:, :, :], s1[:, :, :], 2.0, None, ALU.add))
            n(); d("r", e.reciprocal(pq[:, :, :], pq[:, :, :]))
            n(); d("s", tt(s1[:, :, :], s1[:, :, :], pq[:, :, :], ALU.mult))
            n(); d("s2", tt(s2_[:, :, :], s1[:, :, :], s1[:, :, :], ALU.mult))
            n(); d("p17", ts(pq[:, :, :], s2_[:, :, :], 1 / 17, None, ALU.mult))
            for k in (15, 13, 11, 9, 7, 5, 3):
                n(); d(f"p{k}", stt(pq[:, :, :], pq[:, :, :], 1 / k, s2_[:, :, :], ALU.add, ALU.mult))
            n(); d("l", stt(pq[:, :, :], pq[:, :, :], 1.0, s1[:, :, :], ALU.add, ALU.mult))
            n(); d("mz", ts(zd[:, :, :], zd[:, :, :], 0.0, None, ALU.max))
            n(); d("dt", stt(T4[:, 0], pq[:, :, :], 2.0, zd[:, :, :], ALU.mult, ALU.add))
            n(); d("adt", stt(T4[:, 1], T4[:, 0], -1.0, ea[:, :].unsqueeze(1).to_broadcast(full), ALU.mult, ALU.mult))
            e.wait_ge(dtt, 1)
            cum = bank[6][:, 0:128].rearrange("p (c h) -> p c h", c=NC_)
            end = bank[6][:, 128:256].rearrange("p (c h) -> p c h", c=NC_)
            n(); d("nacs", ts(T4[:, 2], cum, -1.0, None, ALU.mult))
            n(); d("dif", tt(zd[:, :, :], end, T4[:, 2], ALU.add))

        def dt_tensor(e):
            pe_norm(e, 7)
            pe_unit(e, U_DT, 0, 0, x1h, x1l, ready(x_ready, 56))
            e.wait_ge(DM1.sem, DM1.at("raw"))
            for c in range(NC_):
                last = e.transpose(bank[5][:, c * HEADS:(c + 1) * HEADS], dtr[:, c * LANES:(c + 1) * LANES], C("ident", hi=HEADS, rows=HEADS))
            last.then_inc(dts, 1)
            e.wait_ge(DM1.sem, DM1.at("adt"))
            adt = T4[:, 1].rearrange("p c h -> p (c h)")
            e.matmul(bank[6][:, 0:128], C("tri"), adt, start=True, stop=True)
            e.matmul(bank[6][:, 128:256], C("ones"), adt, start=True, stop=True).then_inc(dtt, 1)

        conv, silued = sem("conv"), sem("silued")
        SE = Steps(sem("ssd_tensor"), "tx0 tx1 tb cb a0 a1 y0 n0 a2 y1 n1 a3 y2 n2 y3 sum")
        SD = Steps(sem("ssd_vector"), "xd0 xd1 cbm g0 M0 S0 g1 M1 Sm1 S1 g2 M2 Sm2 S2 g3 M3 ud0 uz0 ud1 uz1 rg yg0 lo0 yg1 lo1")
        SA = Steps(sem("ssd_scalar"), "bt e0 x0 e1 x1 e2 x2 e3 x3 q0 q1 sg hi0 hi1")
        SP = Steps(sem("ssd_pool"), "G xw c1 c2 c3")

        def mamba_units(j):
            return ("x", j) if j < 4 else ("bc", j - 4) if j < 8 else ("z", j - 8)

        def in_scalar(e, hf, pr):
            n4 = hf * 8 + pr * 3
            turn = hf * 2 + pr
            for j in range(12):
                act_split(e, U_MAMBA + j + 2, n4)
                kind, i = mamba_units(j)
                if kind == "z":
                    e.wait_ge(bank_free, after(U_MAMBA, j, n4, 5))
                    e.activation(zs[:, i], t32[:, :] if i % 2 == 0 else a32[:, :], ACT.Silu).then_inc(silued, 1)
                else:
                    e.wait_ge(conv, turn * 32 + 4 * j + 4)
                    dst = xt[:, i] if kind == "x" else bct[:, i]
                    e.activation(dst, cv[:, j % 2], ACT.Silu).then_inc(silued, 1)

        def in_vector(e, hf, pr):
            n4 = hf * 8 + pr * 3
            turn = hf * 2 + pr
            for j in range(12):
                dve_split(e, U_MAMBA + j + 2, n4)
                kind, i = mamba_units(j)
                b = evac_start(e, U_MAMBA, j, n4)
                if kind == "z":
                    e.tensor_tensor(t32[:, :] if i % 2 == 0 else a32[:, :], b, R[:, :], ALU.mult).then_inc(bank_free, 1)
                    if i >= 1:
                        e.wait_ge(silued, turn * 12 + j)
                    continue
                z = j % 2
                e.tensor_tensor(pre[:, z, 3:], b, R[:, :], ALU.mult).then_inc(bank_free, 1)
                if kind == "x":
                    ct = hf * 8 + pr * 4 + i
                else:
                    ct = hf * 4 + pr * 2 + (16 + 8 * (i // 2) + i % 2)
                w = lambda k: par[:, bass.ds(ct + (PC["conv_w"][0] + 32 * k), 1)]
                e.wait_ge(bank_free, after(U_MAMBA, j, n4, 5))
                if j >= 2:
                    e.wait_ge(silued, turn * 12 + (j - 1))
                e.tensor_scalar(cv[:, z], pre[:, z, 3:], w(3), par[:, bass.ds(ct + PC["conv_b"][0], 1)], ALU.mult, ALU.add).then_inc(conv, 1)
                for k in range(3):
                    e.wait_ge(conv, turn * 32 + (4 * j + 1 + k))
                    e.scalar_tensor_tensor(cv[:, z], pre[:, z, k:k + TOK], w(k), cv[:, z], ALU.mult, ALU.add).then_inc(conv, 1)

        def in_tensor(e, hf, pr):
            n4 = hf * 8 + pr * 3
            for j in range(12):
                pe_unit(e, U_MAMBA, j, n4, x1h, x1l)

        def ssd_tensor(e, t, gl):
            n = lambda name: None
            e.wait_ge(silued, t[2])
            for c2 in range(2):
                e.wait_ge(SD.sem, SD.before("rg" if c2 else "S2", t[:2]))
                for c in (2 * c2, 2 * c2 + 1):
                    for i in range(2):
                        last = e.transpose(bank[5 + c2][:, (c % 2) * 256 + i * 128:(c % 2) * 256 + (i + 1) * 128], xt[:, 2 * gl + i, c * LANES:(c + 1) * LANES], C("ident"))
                SE.took(f"tx{c2}", last)
            e.wait_ge(SA.sem, SA.before("bt", t[:2]))
            for c in range(NC_):
                last = e.transpose(bank[7][:, c * LANES:(c + 1) * LANES], bct[:, gl, c * LANES:(c + 1) * LANES], C("ident"))
            SE.took("tb", last)
            e.wait_ge(SD.sem, SD.before("cbm", t[:2]))
            for c in range(NC_):
                cc = slice(c * LANES, (c + 1) * LANES)
                last = e.matmul(bank[4][:, cc], bct[:, gl, cc], bct[:, 2 + gl, cc], start=True, stop=True)
            SE.took("cb", last)
            e.wait_ge(SP.sem, SP.at("G", t[:2]))

            def cums(c):
                if c >= 2:
                    e.wait_ge(SD.sem, SD.at(f"g{c - 2}", t[:2]))
                    e.wait_ge(SA.sem, SA.at(f"x{c - 2}", t[:2]))
                for r in range(HG):
                    last = e.matmul(bank[c % 2][:, r * LANES:(r + 1) * LANES], G4[:, 1, c, r:r + 1].to_broadcast([LANES, LANES]), C("tri"), start=True, stop=True)
                SE.took(f"a{c}", last)

            def outs(c):
                e.wait_ge(SD.sem, SD.at(f"M{c}", t[:2]))
                if c == 0:
                    e.wait_ge(SD.sem, SD.before("uz1", t[:2]))
                else:
                    e.wait_ge(SD.sem, SD.at(f"S{c - 1}", t[:2]))
                    e.wait_ge(SP.sem, SP.at(f"c{c}", t[:2]))
                for r in range(HG):
                    o = bank[2 + r // 2][(r % 2) * HP:(r % 2 + 1) * HP, c * LANES:(c + 1) * LANES]
                    last = e.matmul(o, xdt[:, c, r], dec[:, c % 2, r], start=True, stop=(c == 0))
                    if c:
                        last = e.matmul(o, state[:, r], cs[:, c % 2, r], start=False, stop=True)
                SE.took(f"y{c}", last)

            def news(c):
                if c == 0:
                    e.wait_ge(SP.sem, SP.at("xw", t[:2]))
                    e.wait_ge(SA.sem, SA.at("bt", t[:2]))
                    e.wait_ge(SD.sem, SD.at("xd1", t[:2]))
                else:
                    e.wait_ge(SD.sem, SD.at(f"S{c - 1}", t[:2]))
                SE.took(f"n{c}", e.matmul(bank[5][:, 0:256], btok[:, c], xw[:, c].rearrange("p r w -> p (r w)"), start=True, stop=True))

            cums(0); cums(1)
            outs(0); news(0); cums(2)
            outs(1); news(1); cums(3)
            outs(2); news(2)
            outs(3)
            e.wait_ge(SA.sem, SA.at("q1", t[:2]))
            e.matmul(bk[6], C("ones"), usq[:, 0], start=True, stop=False)
            SE.took("sum", e.matmul(bk[6], C("ones"), usq[:, 1], start=False, stop=True))

        def ssd_vector(e, t, gl, o_tile, dtile):
            tt, ts, stt = e.tensor_tensor, e.tensor_scalar, e.scalar_tensor_tensor
            T = t[:2]
            n = lambda: SD.next(e, T)
            e.wait_ge(SP.sem, SP.at("G", T))
            e.wait_ge(SE.sem, SE.before("y3", T))
            for c2 in range(2):
                e.wait_ge(SE.sem, SE.at(f"tx{c2}", T))
                if c2 == 0:
                    e.wait_ge(SP.sem, SP.before("xw", T))
                SD.took(f"xd{c2}", tt(xdt[:, 2 * c2:2 * c2 + 2], bank[5 + c2][:, :].rearrange("p (c r w) -> p c r w", c=2, r=HG),
                                     G4[:, 0, 2 * c2:2 * c2 + 2].unsqueeze(3).to_broadcast([LANES, 2, HG, HP]), ALU.mult))
            e.wait_ge(SE.sem, SE.at("cb", T))
            SD.took("cbm", tt(cbm[:, :, :], bk[4].rearrange("p (c l) -> p c l", c=NC_), C("tri").unsqueeze(1).to_broadcast([LANES, NC_, LANES]), ALU.mult))
            for c in range(NC_):
                z = c % 2
                e.wait_ge(SE.sem, SE.at(f"a{c}", T))
                if c >= 2:
                    e.wait_ge(SE.sem, SE.at(f"y{c - 2}", T))
                for r in range(HG):
                    last = ts(dec[:, z, r], bank[z][:, r * LANES:(r + 1) * LANES], G4[:, 2, c, r:r + 1], 0.0, ALU.add, ALU.min)
                SD.took(f"g{c}", last)
                e.wait_ge(SA.sem, SA.at(f"e{c}", T))
                n(); SD.took(f"M{c}", tt(dec[:, z], dec[:, z], cbm[:, c].unsqueeze(1).to_broadcast([LANES, HG, LANES]), ALU.mult))
                if c == NC_ - 1:
                    continue
                e.wait_ge(SE.sem, SE.at(f"n{c}", T))
                new = bank[5][:, 0:256].rearrange("p (r w) -> p r w", r=HG)
                if c == 0:
                    SD.took("S0", e.tensor_copy(state[:, :, :], new))
                else:
                    e.wait_ge(SE.sem, SE.at(f"y{c}", T))
                    e.wait_ge(SA.sem, SA.at(f"x{c}", T))
                    n(); SD.took(f"Sm{c}", tt(state[:, :, :], state[:, :, :], ecs[:, z, :, LANES - 1:].to_broadcast([LANES, HG, HP]), ALU.mult))
                    n(); SD.took(f"S{c}", tt(state[:, :, :], state[:, :, :], new, ALU.add))
            e.wait_ge(SE.sem, SE.at("y3", T))
            for i in range(2):
                dsk = par[:, bass.ds(dtile + (PC["d_skip"][0] + i), 1)]
                if i == 0:
                    e.wait_ge(SA.sem, SA.before("q1", T))
                n(); SD.took(f"ud{i}", stt(uu[:, i], xt[:, 2 * gl + i], dsk, bk[2 + i], ALU.mult, ALU.add))
                n(); SD.took(f"uz{i}", tt(uu[:, i], uu[:, i], zs[:, 2 * gl + i], ALU.mult))
            e.wait_ge(SA.sem, SA.at("sg", T))
            n(); SD.took("rg", e.reciprocal(sd[:, :], sd[:, :]))
            for i in range(2):
                gg = par[:, bass.ds(dtile + (PC["gate_g"][0] + i), 1)]
                n(); SD.took(f"yg{i}", stt(uu[:, i], uu[:, i], gg, sd[:, :], ALU.mult, ALU.mult))
                e.wait_ge(SA.sem, SA.at(f"hi{i}", T))
                SD.took(f"lo{i}", tt(tile(x0l, o_tile + i), uu[:, i:i + 1], tile(x0h, o_tile + i).bitcast(F32), ALU.subtract))

        def ssd_scalar(e, t, gl, o_tile):
            T = t[:2]
            e.wait_ge(SE.sem, SE.at("tb", T))
            SA.took("bt", e.activation(btok[:, :, :], bk[7].rearrange("p (c n) -> p c n", c=NC_), ACT.Copy))
            for c in range(NC_):
                z = c % 2
                e.wait_ge(SD.sem, SD.at(f"g{c}", T))
                SA.took(f"e{c}", e.activation(dec[:, z], dec[:, z], ACT.Exp))
                if c >= 2:
                    e.wait_ge(SP.sem, SP.at(f"c{c - 2}", T) if c > 2 else SP.at("xw", T))
                    if c == 3:
                        e.wait_ge(SD.sem, SD.at("S1", T))
                else:
                    e.wait_ge(SP.sem, SP.before(f"c{c + 2}" if c == 0 else "c3", T))
                SA.took(f"x{c}", e.activation(ecs[:, z], bk[z].rearrange("p (r l) -> p r l", r=HG), ACT.Exp))
            for i in range(2):
                e.wait_ge(SD.sem, SD.at(f"uz{i}", T))
                SA.took(f"q{i}", e.activation(usq[:, i], uu[:, i], ACT.Square))
            e.wait_ge(SE.sem, SE.at("sum", T))
            SA.took("sg", e.activation(sd[:, :], bk[6], ACT.Sqrt, bias=eps5[:, :], scale=1.0 / 256))
            for i in range(2):
                e.wait_ge(SD.sem, SD.at(f"yg{i}", T))
                SA.took(f"hi{i}", e.activation(tile(x0h, o_tile + i), uu[:, i:i + 1], ACT.Copy))

        def ssd_pool(e, t, gl, g):
            T = t[:2]
            e.wait_ge(SE.sem, SE.before("a3", T))
            e.wait_ge(SD.sem, SD.before("g3", T))
            SP.next(e, T).took("G", e.tensor_copy(G4[:, :, :, :], T4[:, :, :, bass.ds(g * 4, 4)]))
            e.wait_ge(SE.sem, SE.before("n2", T))
            e.wait_ge(SD.sem, SD.at("xd1", T))
            SP.next(e, T).took("xw", e.tensor_tensor(xw[:, :, :, :], xdt[:, :, :, :], G4[:, 3].unsqueeze(3).to_broadcast([LANES, NC_, HG, HP]), ALU.mult))
            for c in (1, 2, 3):
                e.wait_ge(SA.sem, SA.at(f"x{c}", T))
                e.wait_ge(SE.sem, SE.at(f"y{c - 2}", T) if c == 3 else SE.before("y3", T))
                ccol = bct[:, 2 + gl, c * LANES:(c + 1) * LANES].unsqueeze(1).to_broadcast([LANES, HG, LANES])
                SP.next(e, T).took(f"c{c}", e.tensor_tensor(cs[:, c % 2], ccol, ecs[:, c % 2], ALU.mult))

        def mamba(e, units, ssd, out):
            with e.Fori(0, 2) as hf:
                with e.Fori(0, 2) as pr:
                    if units:
                        units(e, hf, pr)
                    for gl in range(2):
                        ssd(e, (hf * 4 + pr * 2, gl, hf * 24 + pr * 12 + 12), gl, hf, pr)
                if out:
                    out(e, hf)

        def mamba_tensor(e):
            SE.open(e)

            def out(e, hf):
                def there(k):
                    return SD.sem, SD.at(f"lo{k % 2}", (hf * 4, k // 2))
                turns(e, 8, lambda t, j: pe_unit(e, U_MAMBA + 24, j, hf * 8 + t, x0h, x0l, there if j == 0 else None))
            mamba(e, in_tensor, lambda e, t, gl, hf, pr: ssd_tensor(e, t, gl), out)

        def mamba_vector(e):
            SD.open(e)

            def out(e, hf):
                def body(t, j):
                    dve_split(e, U_MAMBA + 24 + j + 2, hf * 8 + t)
                    b = evac_start(e, U_MAMBA + 24, j, hf * 8 + t)
                    m = t * 4 + j
                    e.tensor_tensor(tile(h, m), tile(h, m), one(b), ALU.add).then_inc(bank_free, 1)
                turns(e, 8, body)
            mamba(e, in_vector, lambda e, t, gl, hf, pr: ssd_vector(e, t, gl, pr * 4 + 2 * gl, hf * 8 + pr * 4 + 2 * gl), out)
            e.wait_ge(bank_free, U_KV2 + 4)
            e.sem_inc(h_ready, 8)
            more_x_vector(e, 8, "kv2", x1h, x1l)
            more_x_vector(e, 9, "b_norm", x0h, x0l)

        def mamba_scalar(e):
            SA.open(e)
            mamba(e, in_scalar, lambda e, t, gl, hf, pr: ssd_scalar(e, t, gl, pr * 4 + 2 * gl),
                  lambda e, hf: turns(e, 8, lambda t, j: act_split(e, U_MAMBA + 24 + j + 2, hf * 8 + t)))
            more_x_scalar(e, 8, 8, "kv2", x1h)
            more_x_scalar(e, 8, 9, "b_norm", x0h)

        def mamba_pool(e):
            SP.open(e)
            e.wait_ge(dta, 1)
            e.wait_ge(DM1.sem, DM1.at("dif"))
            mamba(e, None, lambda e, t, gl, hf, pr: ssd_pool(e, t, gl, hf * 4 + pr * 2 + gl), None)

        DH_, LAMBDA_INIT = 8, 0.8 - 0.6 * math.exp(-0.3)
        at = [own]
        K2 = own_buf("K2", [DH_, TOK])
        V2tok = own_buf("V2tok", [4, DM])
        q2 = own_buf("q2", [DH_, TOK])
        gate = own_buf("gate", [DH_, TOK])
        v32 = own_buf("v32", [2, TOK])
        lprod, lsum, lexp = own_buf("lprod", [2, 64]), own_buf("lsum", [2]), own_buf("lexp", [2])
        nlam, sub_gl = own_buf("nlam", [1]), own_buf("sub_gl", [1])
        s2t = {n: own_buf("s2t_" + n, [4, 2]) for n in "mx nm sm rc".split()}
        at = [x0_at]
        Q2s = own_buf("Q2s", [2, TOK])
        K2s = own_buf("K2s", [2, TOK])
        V2s = own_buf("V2s", [2, 4, LANES])
        S2 = own_buf("S2", [4, 2, TOK])
        W2T = own_buf("W2T", [2, TOK])
        O32 = put("O32", [LANES, 2, TOK], at=acc_at)
        assert at[0] <= x0_at + 32768
        VT2 = Steps(sem("v2_turned"), "t", ahead=2)
        VK2 = Steps(sem("v2_kept"), "k", ahead=2)
        GS2 = Steps(sem("gate_silu"), "g", ahead=2)
        LM = Steps(sem("lambda_steps"), "pr sum nlam0 nlam sub")
        lam_exp = sem("lambda_exp")

        def kv2_scalar(e):
            act_norm(e, 8, eps5)
            e.wait_ge(LM.sem, LM.at("sum"))
            e.activation(lexp[:, :], lsum[:, :], ACT.Exp).then_inc(lam_exp, 1)
            VK2.open(e)
            turns(e, 8, lambda t, j: act_split(e, U_KV2 + j + 2, t))

            def keep(t, j):
                T = (t * 4, j)
                e.wait_ge(VT2.sem, VT2.at("t", T))
                VK2.took("k", e.activation(V2tok[:, :, bass.ds(t * LANES * 4 + j * LANES, LANES)], bk[5 + j % 2].rearrange("p (c n) -> p c n", c=4), ACT.Copy))

            def body(t, j):
                act_split(e, U_KV2 + 8 + j + 2, t)
                if j:
                    keep(t, j - 1)
                if j == 3:
                    keep(t, 3)
            turns(e, 8, body)

        def kv2_vector(e):
            dve_norm(e, 8)
            LM.open(e)
            l4 = V("lam_qk").rearrange("p (a b d) -> p a b d", a=2, b=2)
            LM.took("pr", e.tensor_tensor(lprod[:, :, :], l4[:, :, 0], l4[:, :, 1], ALU.mult))
            LM.next(e).took("sum", e.reduce_sum(lsum[:, :].unsqueeze(2), lprod[:, :, :], axis=AX.X))
            e.wait_ge(lam_exp, 1)
            LM.next(e).took("nlam0", e.tensor_tensor(nlam[:, :], lexp[:, 1:2], lexp[:, 0:1], ALU.subtract))
            LM.next(e).took("nlam", e.tensor_scalar(nlam[:, :], nlam[:, :], -LAMBDA_INIT, None, ALU.add))
            LM.next(e).took("sub", e.tensor_scalar(sub_gl[:, :], V("sub_g"), 1.0 - LAMBDA_INIT, None, ALU.mult))

            def k_body(t, j):
                dve_split(e, U_KV2 + j + 2, t)
                b = evac_start(e, U_KV2, j, t)
                e.tensor_tensor(tile(K2, t * 4 + j), one(b), one(R[:, :]), ALU.mult).then_inc(bank_free, 1)
            turns(e, 8, k_body)

            def v_body(t, j):
                dve_split(e, U_KV2 + 8 + j + 2, t)
                b = evac_start(e, U_KV2 + 8, j, t)
                e.wait_ge(VT2.sem, VT2.at("t", (t * 4, j - 2)))
                e.tensor_tensor(v32[:, j % 2], b, R[:, :], ALU.mult).then_inc(bank_free, 1)
            turns(e, 8, v_body)

        def kv2_tensor(e):
            VT2.open(e)
            pe_norm(e, 8)
            turns(e, 8, lambda t, j: pe_unit(e, U_KV2, j, t, x1h, x1l, ready(x_ready, 64) if j == 0 else None))

            def turn(t, j):
                e.wait_ge(bank_free, after(U_KV2 + 8, j, t, 5))
                e.wait_ge(VK2.sem, VK2.at("k", (t * 4, j - 2)))
                for c in range(4):
                    last = e.transpose(bank[5 + j % 2][:, c * LANES:(c + 1) * LANES], v32[:, j % 2, c * LANES:(c + 1) * LANES], C("ident"))
                VT2.took("t", last)

            def body(t, j):
                pe_unit(e, U_KV2 + 8, j, t, x1h, x1l)
                if j:
                    turn(t, j - 1)
                if j == 3:
                    turn(t, 3)
            turns(e, 8, body)

        def qg2_scalar(e):
            GS2.open(e)
            turns(e, 8, lambda t, j: act_split(e, U_QG2 + j + 2, t))

            def body(t, j):
                act_split(e, U_QG2 + 8 + j + 2, t)
                e.wait_ge(bank_free, after(U_QG2 + 8, j, t, 5))
                GS2.took("g", e.activation(tile(gate, t * 4 + j), one((a32 if j % 2 else t32)[:, :]), ACT.Silu))
            turns(e, 8, body)

        def qg2_vector(e):
            def q_body(t, j):
                dve_split(e, U_QG2 + j + 2, t)
                b = evac_start(e, U_QG2, j, t)
                e.scalar_tensor_tensor(tile(q2, t * 4 + j), one(b), 0.125, one(R[:, :]), ALU.mult, ALU.mult).then_inc(bank_free, 1)
            turns(e, 8, q_body)

            def g_body(t, j):
                dve_split(e, U_QG2 + 8 + j + 2, t)
                b = evac_start(e, U_QG2 + 8, j, t)
                e.wait_ge(GS2.sem, GS2.at("g", (t * 4, j - 2)))
                e.tensor_tensor((a32 if j % 2 else t32)[:, :], b, R[:, :], ALU.mult).then_inc(bank_free, 1)
            turns(e, 8, g_body)

        def qg2_tensor(e):
            turns(e, 16, lambda t, j: pe_unit(e, U_QG2, j, t, x0h, x0l, ready(x_ready, 72) if j == 0 else None))

        DT = 4 * DH_
        FP = Steps(sem("diff_copies"), "K Q V")
        FM = Steps(sem("diff_max"), "m0 m1 max neg", ahead=8)
        FE = Steps(sem("diff_exp"), "e0 e1", ahead=8)
        FW = Steps(sem("diff_weights"), "rec lrec w0 w1", ahead=8)
        FS = Steps(sem("diff_scores"), "s", ahead=8)
        FT = Steps(sem("diff_turned"), "t", ahead=8)
        FC = Steps(sem("diff_kept"), "w", ahead=8)
        FO = Steps(sem("diff_out"), "o", ahead=8)
        FK = Steps(sem("diff_out_kept"), "k", ahead=8)
        HA = Steps(sem("head_scalar"), "sq sd hi", ahead=4)
        HD = Steps(sem("head_vector"), "rc y yg lo", ahead=4)
        HE = Steps(sem("head_sum"), "sum", ahead=4)

        def diff_pool(e):
            FP.open(e)
            e.wait_ge(unit_done, U_O2)
            e.wait_ge(bank_free, U_O2 + 4)
            e.wait_ge(VK2.sem, VK2.at("k", 7))
            with e.Fori(0, DH_ // 2) as i:
                for x in range(2):
                    e.wait_ge(FS.sem, FS.at("s", (i * 8, 4 * x - 5)))
                    FP.next(e, (i * 2, x)).took("K", e.tensor_copy(K2s[:, x:x + 1], tile(K2, i * 2 + x)))
                    FP.next(e, (i * 2, x)).took("Q", e.tensor_copy(Q2s[:, x:x + 1], tile(q2, i * 2 + x)))
                    e.wait_ge(FO.sem, FO.at("o", (i * 8, 4 * x - 5)))
                    FP.next(e, (i * 2, x)).took("V", e.tensor_copy(V2s[:, x], V2tok[:, :, bass.ds(i * (2 * LANES) + x * LANES, LANES)]))

        def ended(i, T, lag):
            q = T - lag
            return (i * 2, q // 4) if q % 4 == 3 and runs(i, q, DT) else None

        def diff_tensor(e):
            for s in (FS, FT, FO, HE):
                s.open(e)

            def step(i, T):
                if runs(i, T, DT):
                    x, n, b = T // 4, T % 4, 2 * (T % 2)
                    if n == 0:
                        e.wait_ge(FP.sem, FP.at("Q", (i * 2, x)))
                    e.wait_ge(FM.sem, FM.at("m1", (i * 8, T - 2)))
                    for s in range(2):
                        last = e.matmul(bank[b + s][:, 0:LANES * (n + 1)], Q2s[64 * s:64 * s + 64, x, n * LANES:(n + 1) * LANES],
                                        K2s[64 * s:64 * s + 64, x, 0:LANES * (n + 1)], start=True, stop=True)
                    FS.took("s", last)
                q = T - 3
                if runs(i, q, DT):
                    n = q % 4
                    e.wait_ge(FW.sem, FW.at("w1", (i * 8, q)))
                    e.wait_ge(FC.sem, FC.at("w", (i * 8, q - 2)))
                    for c in range(n + 1):
                        last = e.transpose(bank[5 + q % 2][:, c * LANES:(c + 1) * LANES], S2[:, q % 4, 0, c * LANES:(c + 1) * LANES], C("ident"))
                    FT.took("t", last)
                q = T - 4
                if runs(i, q, DT):
                    x, n = q % 8 // 4, q % 4
                    if n == 0:
                        e.wait_ge(FP.sem, FP.at("V", (i * 2, q // 4)))
                    e.wait_ge(FC.sem, FC.at("w", (i * 8, q)))
                    e.wait_ge(FK.sem, FK.at("k", (i * 8, q - 1)))
                    for c in range(n + 1):
                        last = e.matmul(bank[7][:, n * LANES:(n + 1) * LANES], V2s[:, x, c], W2T[:, q % 2, c * LANES:(c + 1) * LANES], start=(c == 0), stop=(c == n))
                    FO.took("o", last)
                H = ended(i, T, 5)
                if H:
                    e.wait_ge(HA.sem, HA.at("sq", H))
                    HE.took("sum", e.matmul(bk[4], C("ones"), t32[:, :], start=True, stop=True))
            piped(e, step, DT, 8)

        def diff_vector(e):
            for s in (FM, FW, HD):
                s.open(e)

            def step(i, T):
                if runs(i, T, DT):
                    x, n, b, z = T // 4, T % 4, 2 * (T % 2), T % 4
                    t, N = (i * 8, T), LANES * (T % 4 + 1)
                    e.wait_ge(FS.sem, FS.at("s", t))
                    e.wait_ge(FT.sem, FT.at("t", (i * 8, T - 4)))
                    s0 = CC["slope"][0] + x
                    slope = const[:, s0:s0 + 1] if isinstance(i, int) and i == 0 else const[:, bass.ds(i * 2 + s0, 1)]
                    for s in range(2):
                        FM.took(f"m{s}", e.scalar_tensor_tensor(S2[:, z, s, 0:N], C("dist", lo=TOK - N), slope, bank[b + s][:, 0:N], ALU.mult, ALU.add))
                    FM.next(e, t).took("max", e.reduce_max(s2t["mx"][:, z].unsqueeze(2), S2[:, z, :, 0:N], axis=AX.X))
                    FM.next(e, t).took("neg", e.tensor_scalar(s2t["nm"][:, z], s2t["mx"][:, z], -1.0, None, ALU.mult))
                q = T - 2
                if runs(i, q, DT):
                    t, z, N = (i * 8, q), q % 4, LANES * (q % 4 + 1)
                    e.wait_ge(FE.sem, FE.at("e1", t))
                    FW.next(e, t).took("rec", e.reciprocal(s2t["rc"][:, z], s2t["sm"][:, z]))
                    FW.next(e, t).took("lrec", e.tensor_tensor(s2t["rc"][:, z, 1:2], s2t["rc"][:, z, 1:2], nlam[:, :], ALU.mult))
                    FW.next(e, t).took("w0", e.tensor_scalar(S2[:, z, 0, 0:N], S2[:, z, 0, 0:N], s2t["rc"][:, z, 0:1], None, ALU.mult))
                    FW.next(e, t).took("w1", e.scalar_tensor_tensor(S2[:, z, 0, 0:N], S2[:, z, 1, 0:N], s2t["rc"][:, z, 1:2], S2[:, z, 0, 0:N], ALU.mult, ALU.add))
                H = ended(i, T, 7)
                if H:
                    y = H[1] % 2
                    e.wait_ge(HA.sem, HA.at("sd", H))
                    HD.next(e, H).took("rc", e.reciprocal(R[:, :], sd[:, :]))
                    e.wait_ge(FK.sem, FK.at("k", (i * 8, T - 7)))
                    HD.next(e, H).took("y", e.scalar_tensor_tensor(O32[:, y], O32[:, y], sub_gl[:, :], R[:, :], ALU.mult, ALU.mult))
                    HD.next(e, H).took("yg", e.tensor_tensor(O32[:, y:y + 1], O32[:, y:y + 1], tile(gate, i * 2 + H[1]), ALU.mult))
                H = ended(i, T, 8)
                if H:
                    y = H[1] % 2
                    e.wait_ge(HA.sem, HA.at("hi", H))
                    HD.took("lo", e.tensor_tensor(tile(x1l, i * 2 + H[1]), O32[:, y:y + 1], tile(x1h, i * 2 + H[1]).bitcast(F32), ALU.subtract))
            piped(e, step, DT, 8)

        def diff_scalar(e):
            for s in (FE, FC, FK, HA):
                s.open(e)

            def step(i, T):
                q = T - 1
                if runs(i, q, DT):
                    t, z, N = (i * 8, q), q % 4, LANES * (q % 4 + 1)
                    e.wait_ge(FM.sem, FM.at("neg", t))
                    e.wait_ge(FW.sem, FW.at("w1", (i * 8, q - 4)))
                    for s in range(2):
                        FE.took(f"e{s}", e.activation(S2[:, z, s, 0:N], S2[:, z, s, 0:N], ACT.Exp, bias=s2t["nm"][:, z, s:s + 1], accum_out=s2t["sm"][:, z, s:s + 1]))
                q = T - 3
                if runs(i, q, DT):
                    N = LANES * (q % 4 + 1)
                    e.wait_ge(FT.sem, FT.at("t", (i * 8, q)))
                    e.wait_ge(FO.sem, FO.at("o", (i * 8, q - 2)))
                    FC.took("w", e.activation(W2T[:, q % 2, 0:N], bank[5 + q % 2][:, 0:N], ACT.Copy))
                q = T - 4
                if runs(i, q, DT):
                    n = q % 4
                    e.wait_ge(FO.sem, FO.at("o", (i * 8, q)))
                    if n == 0:
                        e.wait_ge(HD.sem, HD.at("lo", (i * 2, q // 4 - 2)))
                    FK.took("k", e.activation(O32[:, q % 8 // 4, n * LANES:(n + 1) * LANES], bank[7][:, n * LANES:(n + 1) * LANES], ACT.Copy))
                H = ended(i, T, 8)
                if H:
                    e.wait_ge(HD.sem, HD.at("yg", H))
                    HA.took("hi", e.activation(tile(x1h, i * 2 + H[1]), O32[:, H[1] % 2:H[1] % 2 + 1], ACT.Copy))
                H = ended(i, T, 4)
                if H:
                    e.wait_ge(FK.sem, FK.at("k", (i * 8, T - 4)))
                    e.wait_ge(HE.sem, HE.at("sum", (H[0], H[1] - 1)))
                    HA.took("sq", e.activation(t32[:, :], O32[:, H[1] % 2], ACT.Square))
                H = ended(i, T, 6)
                if H:
                    e.wait_ge(HE.sem, HE.at("sum", H))
                    e.wait_ge(HD.sem, HD.at("rc", (H[0], H[1] - 1)))
                    HA.took("sd", e.activation(sd[:, :], bk[4], ACT.Sqrt, bias=eps5[:, :], scale=1.0 / LANES))
            piped(e, step, DT, 8)

        def wo2_scalar(e):
            for m in range(8):
                act_split(e, U_O2 + m + 2, 0)
            act_norm(e, 9, eps5)

        def wo2_vector(e):
            for m in range(8):
                dve_split(e, U_O2 + m + 2, 0)
                b = evac_start(e, U_O2, m, 0)
                e.tensor_tensor(h[:, m], h[:, m], b, ALU.add).then_inc(bank_free, 1)
                e.wait_ge(bank_free, U_O2 + m + 5)
                e.sem_inc(h_ready, 1)
            dve_norm(e, 9)
            with e.Fori(0, KT) as m:
                e.scalar_tensor_tensor(tile(h, m), tile(h, m), Vd("final2", m), one(R[:, :]), ALU.mult, ALU.mult).then_inc(h_ready, 1)

        def wo2_tensor(e):
            for m in range(8):
                pe_unit(e, U_O2, m, 0, x1h, x1l, (lambda k: (HD.sem, HD.at("lo", k))) if m == 0 else None)
            pe_norm(e, 9)

        def store(e):
            for m in range(KT):
                e.wait_ge(h_ready, 8 * 10 + m + 1)
                e.dma_start(a["out"][m * LANES:(m + 1) * LANES, :], h[:, m]).then_inc(stored, 16)
            e.wait_ge(stored, 16 * KT)

        mlp0, mlp1 = mlp_parts(0, 2, 1, 2, "ple0"), mlp_parts(1, 5, 5, 6, "ple1")
        ple0, ple1 = ple_parts(0, 3, 3, "kv"), ple_parts(1, 6, 7, None)
        block = ctx.enter_context(nc.Block())

        @block.sync
        def _(e):
            s5_loads(e)
            for i in range(2):
                e.dma_start(raw[:, i], a["w"][i]).then_inc(raw_loaded[i], 16)
            s5_sync(e)
            e.wait_ge(h_ready, 9)
            e.dma_start(p_in[:, :, :, :], a["pT"]).then_inc(p_loaded, 16)
            with e.Fori(1, PAIRS // 2) as i:
                for s in range(2):
                    e.wait_ge(w_split, i * 4 + (2 * s - 2))
                    e.dma_start(raw[:, s], a["w"][bass.ds(i * 2 + s, 1)].rearrange("o p a k m -> p (o a) k m")).then_inc(raw_loaded[s], 16)
            if PAIRS % 2:
              e.wait_ge(w_split, 2 * PAIRS - 4)
              e.dma_start(raw[:, 0], a["w"][PAIRS - 1]).then_inc(raw_loaded[0], 16)
            store(e)

        @block.gpsimd
        def _(e):
            s5_pool(e)
            for n in (1, 2, 3):
                pool_h(e, n)
            att_pool(e)
            e.wait_ge(h_ready, 33)
            for n in (4, 5, 6, 7):
                pool_h(e, n)
            mamba_pool(e)
            e.wait_ge(h_ready, 65)
            pool_h(e, 8)
            diff_pool(e)
            e.wait_ge(h_ready, 73)
            pool_h(e, 9)

        @block.scalar
        def _(e):
            act_split(e, 0, 0, True)
            act_split(e, 1, 0, True)
            s5_scalar(e)
            glu_scalar(e)
            mlp0[0](e)
            ple0[0](e)
            more_x_scalar(e, 3, 4, "mix1", x0h)
            kv_scalar(e)
            q_scalar(e)
            att_scalar(e)
            wo_scalar(e)
            mlp1[0](e)
            ple1[0](e)
            final1_scalar(e)
            dt_scalar(e)
            mamba_scalar(e)
            kv2_scalar(e)
            qg2_scalar(e)
            diff_scalar(e)
            wo2_scalar(e)

        @block.vector
        def _(e):
            e.sem_inc(bank_free, 4)
            dve_split(e, 0, 0)
            dve_split(e, 1, 0)
            s5_vector(e)
            glu_vector(e)
            mlp0[1](e)
            ple0[1](e)
            more_x_vector(e, 4, "mix1", x0h, x0l)
            kv_vector(e)
            q_vector(e)
            att_vector(e)
            wo_vector(e)
            mlp1[1](e)
            ple1[1](e)
            final1_vector(e)
            dt_vector(e)
            mamba_vector(e)
            kv2_vector(e)
            qg2_vector(e)
            diff_vector(e)
            wo2_vector(e)

        @block.tensor
        def _(e):
            s5_tensor(e)
            glu_tensor(e)
            mlp0[2](e)
            ple0[2](e)
            kv_tensor(e)
            q_tensor(e)
            att_tensor(e)
            wo_tensor(e)
            mlp1[2](e)
            ple1[2](e)
            final1_tensor(e)
            dt_tensor(e)
            mamba_tensor(e)
            kv2_tensor(e)
            qg2_tensor(e)
            diff_tensor(e)
            wo2_tensor(e)


def constants():
    f = np.float32
    c = {}
    eye = np.eye(128, dtype=f)
    c["ident"] = eye
    turn = np.zeros((128, 128), f)
    turn[64:, :64], turn[:64, 64:] = -np.eye(64), np.eye(64)
    c["turn"] = turn
    swap = np.zeros((128, 128), f)
    for base in (0, 64):
        for d in range(8):
            swap[base + d + 8, base + d] = -1
            swap[base + d, base + d + 8] = 1
    c["ropeswap"] = swap
    c["ones"] = np.ones((128, 128), f)
    k, q = np.arange(128)[:, None], np.arange(128)[None, :]
    c["tri"] = (k <= q).astype(f)
    sgn = np.where(np.arange(128) < 64, -1, 1).astype(f)[:, None]
    c["sgn"], c["nsgn"] = sgn, -sgn
    c["sel"] = (np.arange(128)[:, None] // 16 == np.arange(8)[None]).astype(f)
    c["cidx"] = np.tile(np.arange(64, dtype=f), (128, 1))
    c["cnz"] = np.tile((np.arange(64) > 0).astype(f), (128, 1))
    c["id16"] = np.pad(np.eye(16, dtype=f), ((0, 112), (0, 0)))
    inv = f(500000.0) ** (-np.arange(0, 16, 2, dtype=f) / f(16))
    ang = np.arange(512, dtype=f)[None] * inv[:, None]
    rc, rs = np.ones((64, 512), f), np.zeros((64, 512), f)
    rc[0:8] = rc[8:16] = np.cos(ang)
    rs[0:8] = rs[8:16] = np.sin(ang)
    c["rcos"], c["rsin"] = np.tile(rc, (2, 1)), np.tile(rs, (2, 1))
    qi, kj = np.arange(128)[:, None] + 128, np.arange(256)[None]
    c["band"] = np.where((kj <= qi) & (qi - kj < 128), 0, -1e30).astype(f)
    c["band0"] = np.where(kj < 128, f(-1e30), c["band"])
    qi, kj = np.arange(128)[:, None], np.arange(512)[None] - 384
    c["dist"] = np.where(kj // 64 <= qi // 64, np.abs(qi - kj), 1e30).astype(f)
    c["slope"] = np.tile(-f(2.0) ** (-f(8.0) * np.arange(1, 9, dtype=f) / f(8.0)), (128, 1))
    return np.ascontiguousarray(np.concatenate([c[n] for n, _ in CONSTS], axis=1).astype(f))


def lay_out(x, p, norm_mix, ssm_lambda_re, ssm_lambda_im, ssm_log_dt, ssm_b_re, ssm_b_im, ssm_c_re,
            ssm_c_im, ssm_d, ssm_w_glu, kv_norm, w_k, w_v, w_q, attn_sinks, w_o, norm_mlp, w_up, w_down,
            norm_ple, w_ple_gate, w_ple_proj, norm_final, a_norm_g_2, a_w_in_2, a_conv_w_2, a_conv_b_2,
            a_dt_bias_2, a_a_log_2, a_d_skip_2, a_gate_norm_g_2, a_w_out_2, kv_norm_g_2, w_kv_2,
            b_norm_g_2, b_w_in_2, b_lambda_2, b_sub_g_2, b_w_out_2, final_norm_g_2):
    f = np.float32
    units = []

    def unit(w, r0, c0):
        units.append(w[r0:r0 + DM, c0:c0 + 128].reshape(KT, 128, 128).transpose(1, 0, 2))

    def cols(w, n, c0=0, r0=0):
        for m in range(n):
            unit(w, r0, c0 + 128 * m)

    def ple(w):
        w = w.reshape(2, 128, 2, 4, 128)
        for j in range(2):
            units.append(w[:, :, j].transpose(1, 2, 0, 3).reshape(128, KT, 128))

    def mlp(i):
        for q in range(4):
            cols(w_up[i], 8, q * DM)
            cols(w_down[i], 8, 0, q * DM)

    for m in range(8):
        unit(ssm_w_glu[0], 0, DM + 128 * m)
        unit(ssm_w_glu[0], 0, 128 * m)
    mlp(0)
    ple(w_ple_proj[0])
    cols(w_ple_gate[0], 8)
    cols(w_k, 2)
    cols(w_v, 2)
    cols(w_q[0], 8)
    cols(w_o[0], 8)
    mlp(1)
    ple(w_ple_proj[1])
    cols(w_ple_gate[1], 8)
    win = a_w_in_2[0]
    units.append(np.pad(win[:, 6144:6176].reshape(KT, 128, 32).transpose(1, 0, 2), ((0, 0), (0, 0), (0, 96))))
    for half in range(2):
        for pair in range(2):
            g = 4 * half + 2 * pair
            cols(win, 4, 2048 + 256 * g)
            cols(win, 2, 4096 + 128 * g)
            cols(win, 2, 5120 + 128 * g)
            cols(win, 4, 256 * g)
        cols(a_w_out_2[0], 8, 0, half * DM)
    cols(w_kv_2, 16)
    cols(b_w_in_2[0], 16)
    cols(b_w_out_2[0], 8)
    assert len(units) == UNITS
    units.append(np.zeros((128, KT, 128), f))
    w = np.ascontiguousarray(np.stack(units).reshape(PAIRS, 2, 128, KT, 128).transpose(0, 2, 1, 3, 4))

    v = {}
    vec = lambda t: t.reshape(-1, 128).T
    gains = [norm_mix[0], norm_mix[1], norm_mlp[0], norm_mlp[1], norm_ple[0], norm_ple[1], kv_norm, norm_final,
             a_norm_g_2[0], kv_norm_g_2, b_norm_g_2[0], final_norm_g_2]
    for n, g in zip(GAINS, gains):
        v[n] = vec(g)
    over = lambda t: np.tile(t.reshape(1, -1), (128, 1))
    v["lam_re"] = np.tile(ssm_lambda_re[0].T, (2, 1))
    v["lam_im"] = np.tile(ssm_lambda_im[0].T, (2, 1))
    v["log_dt"] = over(ssm_log_dt[0])
    v["gain_u"] = np.tile(norm_mix[0].reshape(64, 16).T, (8, 1))
    v["d_h"] = np.pad(ssm_d[0].reshape(64, 16).T, ((0, 112), (0, 0)))
    v["conv_w"] = a_conv_w_2[0].reshape(4, 32, 128).transpose(2, 0, 1).reshape(128, 128)
    v["conv_b"] = vec(a_conv_b_2[0])
    v["d_skip"] = vec(np.repeat(a_d_skip_2[0], 64))
    v["gate_g"] = vec(a_gate_norm_g_2[0])
    v["sub_g"] = vec(b_sub_g_2[0])
    v["sinks"] = over(attn_sinks[0])
    v["dt_bias"] = over(a_dt_bias_2[0])
    v["a_log"] = over(a_a_log_2[0])
    v["lam_qk"] = over(b_lambda_2[0])
    par = np.concatenate([v[n] for n, _ in PARAMS], axis=1)

    B = np.stack([np.concatenate([ssm_b_re[0], ssm_b_im[0]], 1), np.concatenate([ssm_b_im[0], ssm_b_re[0]], 1)])
    Cc = np.stack([np.concatenate([ssm_c_re[0], ssm_c_im[0]], 2), np.concatenate([ssm_c_im[0], ssm_c_re[0]], 2)])
    out = {
        "w": w, "const": constants(), "par": par,
        "xT": x[0].T,
        "xu": x[0].reshape(64, 8, 64, 16).transpose(1, 3, 2, 0).reshape(128, 64, 64),
        "B": B.transpose(2, 0, 1, 3),
        "C": Cc.transpose(3, 0, 1, 2),
        "pT": p[:, 0].reshape(2, 512, 2, 128).transpose(3, 0, 2, 1),
    }
    return {k: np.ascontiguousarray(t) for k, t in out.items()}


def kernel(**inputs):
    import concourse.bacc as bacc
    from concourse.bass_utils import run_bass_kernel_spmd

    nc = bacc.Bacc("TRN2", target_bir_lowering=False, num_devices=1)
    arrays = {f"in_{n}_dram": t for n, t in lay_out(**inputs).items()}
    a = {n: nc.dram_tensor(f"in_{n}_dram", arrays[f"in_{n}_dram"].shape, F32, kind="ExternalInput").ap()
         for n in ("w", "const", "par", "xT", "xu", "B", "C", "pT")}
    a["out"] = nc.dram_tensor("out_dram", (DM, TOK), F32, kind="ExternalOutput").ap()
    program(nc, a)
    result = run_bass_kernel_spmd(nc, [arrays], core_ids=[0])
    return np.ascontiguousarray(result.results[0]["out_dram"].T).reshape(1, TOK, DM)
```

```python
import math
from contextlib import ExitStack
import numpy as np
import concourse.bass as bass
from concourse import mybir

F32 = mybir.dt.float32
F32R = mybir.dt.float32r
ACT = mybir.ActivationFunctionType
ALU = mybir.AluOpType
AX = mybir.AxisListType

LANES, TOK, DM = 128, 512, 1024
KT = DM // LANES
SG, SH, SN = 64, 16, 64
STEP = 8
NSTEP = TOK // STEP
GB = LANES // SH
NBLK = SG // GB
SIN_SCALE = 6.283185
PI_SAFE = 3.1415925
ROUND = 12582912.0
TWO_PI_HI, TWO_PI_LO = 6.28125, 2.0 * math.pi - 6.28125

CONSTS = [("ident", 128), ("turn", 128), ("ropeswap", 128), ("ones", 128), ("tri", 128), ("sgn", 1), ("nsgn", 1),
          ("sel", 8), ("cidx", 64), ("cnz", 64), ("id16", 16), ("rcos", 512), ("rsin", 512), ("band", 256), ("band0", 256), ("dist", 512), ("slope", 8)]
GAINS = ["mix0", "mix1", "mlp0", "mlp1", "ple0", "ple1", "kv", "final", "a_norm", "kv2", "b_norm", "final2"]
PARAMS = [(g, 8) for g in GAINS] + [("lam_re", 64), ("lam_im", 64), ("log_dt", 64), ("gain_u", 64), ("d_h", 64),
          ("conv_w", 128), ("conv_b", 32), ("d_skip", 16), ("gate_g", 16), ("sub_g", 1), ("sinks", 16),
          ("dt_bias", 32), ("a_log", 32), ("lam_qk", 256)]


def columns(table):
    at, n = {}, 0
    for name, w in table:
        at[name] = (n, n + w)
        n += w
    return at, n


CC, NCONST = columns(CONSTS)
PC, NPARAM = columns(PARAMS)

U_GLU, U_MLP0, U_P0, U_GATE0 = 0, 16, 80, 82
U_KV, U_Q, U_O, U_MLP1, U_P1, U_GATE1 = 90, 94, 102, 110, 174, 176
U_DT, U_MAMBA, U_KV2, U_QG2, U_O2 = 184, 185, 249, 265, 281
UNITS = 289
PAIRS = (UNITS + 1) // 2


class Steps:

    def __init__(self, sem, names, ahead=1):
        self.sem, self.names, self.ahead, self.here = sem, names.split(), ahead, 0

    def open(self, e):
        e.sem_inc(self.sem, self.ahead * len(self.names))

    def count(self, turn, more):
        n = len(self.names)
        loop, t = turn if isinstance(turn, tuple) else (0, turn) if isinstance(turn, int) else (turn, 0)
        more += (t + self.ahead) * n
        assert more >= 0
        return more if isinstance(loop, int) and loop == 0 else loop * n + more

    def at(self, name, turn=0):
        return self.count(turn, self.names.index(name) + 1)

    def before(self, name, turn):
        return self.at(name, turn) - len(self.names) if isinstance(turn, int) else self.count(turn, self.names.index(name) + 1 - len(self.names))

    def next(self, e, turn=0):
        e.wait_ge(self.sem, self.count(turn, self.here % len(self.names)))
        return self

    def took(self, name, ins):
        want = self.names[self.here % len(self.names)]
        assert want == name, (name, want)
        self.here += 1
        ins.then_inc(self.sem, 1)


def program(nc, a):
    ctx = ExitStack()
    with ctx:
        base = [(nc.sbuf_base + 255) // 256 * 256]

        def put(name, shape, dt=F32, at=None):
            size = int(np.prod(shape[1:])) * 4
            if at is None:
                at = base[0]
                base[0] += (size + 31) // 32 * 32
                assert base[0] <= nc.sbuf_usable_end, (name, base[0], nc.sbuf_usable_end)
            return nc.alloc_sbuf_tensor_at(name, shape, dt, offset=at)

        def sem(name):
            return ctx.enter_context(nc.semaphore(name))

        const = put("const", [LANES, NCONST])
        par = put("par", [LANES, NPARAM])
        h = put("h", [LANES, KT, TOK])
        raw = put("raw", [LANES, 2, 2, KT, LANES])
        w_hi = put("w_hi", [LANES, 2, KT, LANES], F32R)
        w_lo = put("w_lo", [LANES, 2, KT, LANES], F32R)
        x0_at = base[0]
        x0h = put("x0h", [LANES, KT, TOK], F32R)
        x0l = put("x0l", [LANES, KT, TOK], F32R)
        x1h = put("x1h", [LANES, KT, TOK], F32R)
        x1l = put("x1l", [LANES, KT, TOK], F32R)
        acc_at = base[0]
        acc = put("acc", [LANES, TOK])
        sq = put("sq", [LANES, TOK])
        sd = put("sd", [LANES, TOK])
        R = put("R", [LANES, TOK])
        t32 = put("t32", [LANES, TOK])
        a32 = put("a32", [LANES, TOK])
        half_pi, eps6, eps5 = put("half_pi", [LANES, 1]), put("eps6", [LANES, 1]), put("eps5", [LANES, 1])
        own = base[0]
        room = nc.sbuf_usable_end - own

        def C(name, lo=0, hi=None, rows=LANES):
            a0, a1 = CC[name]
            return const[0:rows, a0 + lo:(a1 if hi is None else a0 + hi)]

        def V(name, lo=0, hi=None, rows=LANES):
            a0, a1 = PC[name]
            return par[0:rows, a0 + lo:(a1 if hi is None else a0 + hi)]

        def Vd(name, i):
            a0, a1 = PC[name]
            return par[:, a0 + i:a0 + i + 1] if isinstance(i, int) else par[:, bass.ds(i + a0, 1)]

        def tile(t, i):
            return t[:, i:i + 1] if isinstance(i, int) else t[:, bass.ds(i, 1)]

        def one(ap):
            return ap.rearrange("p (o n) -> p o n", o=1)

        bank = [ctx.enter_context(nc.psum_tensor(f"bank{i}", [LANES, TOK], F32)) for i in range(8)]
        bk = [b[:, :] for b in bank]

        loaded = sem("loaded")
        raw_loaded = [sem("raw_loaded_0"), sem("raw_loaded_1")]
        hi_split, w_split = sem("hi_split"), sem("w_split")
        unit_done, bank_free = sem("unit_done"), sem("bank_free")
        h_ready, x_hi, x_ready = sem("h_ready"), sem("x_hi"), sem("x_ready")
        squared, acc_ready, norm_mm, sd_ready, r_ready = (sem(n) for n in ("squared", "acc_ready", "norm_mm", "sd_ready", "r_ready"))
        stored = sem("stored")

        def after(u0, j, n4, more):
            return u0 + j + more + (n4 * 4)

        def pe_unit(e, u0, j, n4, xh, xl, first=None):
            b = bk[(u0 + j) % 4]
            w = (u0 + j) % 2
            e.wait_ge(w_split, after(u0, j, n4, 1))
            e.wait_ge(bank_free, after(u0, j, n4, 1))
            for k in range(KT):
                if first is not None:
                    e.wait_ge(*first(k))
                e.matmul(b, w_hi[:, w, k], xh[:, k], start=(k == 0), stop=False)
                e.matmul(b, w_hi[:, w, k], xl[:, k], start=False, stop=False)
                last = e.matmul(b, w_lo[:, w, k], xh[:, k], start=False, stop=(k == KT - 1))
            last.then_inc(unit_done, 1)

        def act_split(e, v0, n4, lead=False):
            if isinstance(n4, int) and v0 + 4 * n4 >= UNITS:
                return
            e.wait_ge(raw_loaded[(v0 // 2) % 2], n4 * 16 + (v0 // 4 + 1) * 16)
            if not lead:
                e.wait_ge(unit_done, n4 * 4 + (v0 - 1))
            e.activation(w_hi[:, v0 % 2], raw[:, (v0 // 2) % 2, v0 % 2], ACT.Copy).then_inc(hi_split, 1)

        def dve_split(e, v0, n4):
            if isinstance(n4, int) and v0 + 4 * n4 >= UNITS:
                return
            e.wait_ge(hi_split, n4 * 4 + (v0 + 1))
            e.tensor_tensor(w_lo[:, v0 % 2], raw[:, (v0 // 2) % 2, v0 % 2], w_hi[:, v0 % 2].bitcast(F32),
                            ALU.subtract).then_inc(w_split, 1)

        def evac_start(e, u0, j, n4):
            e.wait_ge(unit_done, after(u0, j, n4, 1))
            return bk[(u0 + j) % 4]

        def act_x(e, n, p, m, gain, xh):
            e.wait_ge(h_ready, m + (8 * n + 1))
            e.activation(tile(xh, m), tile(h, m), ACT.Copy, scale=Vd(gain, m)).then_inc(x_hi, 1)

        def dve_x(e, p, m, gain, xh, xl):
            e.wait_ge(x_hi, m + (8 * p + 1))
            e.scalar_tensor_tensor(tile(xl, m), tile(h, m), Vd(gain, m), tile(xh, m).bitcast(F32),
                                   ALU.mult, ALU.subtract).then_inc(x_ready, 1)

        def pool_start(e, n):
            if n:
                e.wait_ge(norm_mm, n)
                e.wait_ge(acc_ready, 8 * n)
            e.memset(acc[:, :], 0.0).then_inc(squared, 1)
            e.wait_ge(squared, 9 * n + 1)

        def pool_square(e, n, m):
            e.wait_ge(h_ready, m + (8 * n + 1))
            e.wait_ge(acc_ready, m + 8 * n)
            e.tensor_tensor(one(sq[:, :]), tile(h, m), tile(h, m), ALU.mult).then_inc(squared, 1)
            e.wait_ge(squared, m + (9 * n + 2))
            e.tensor_tensor(acc[:, :], acc[:, :], sq[:, :], ALU.add).then_inc(acc_ready, 1)

        def pe_norm(e, n):
            e.wait_ge(acc_ready, 8 * n + 8)
            e.matmul(bk[4], C("ones"), acc[:, :], start=True, stop=True).then_inc(norm_mm, 1)

        def act_norm(e, n, eps):
            e.wait_ge(norm_mm, n + 1)
            if n:
                e.wait_ge(r_ready, n)
            e.activation(sd[:, :], bk[4], ACT.Sqrt, bias=eps[:, :], scale=1.0 / DM).then_inc(sd_ready, 1)

        def dve_norm(e, n):
            e.wait_ge(sd_ready, n + 1)
            e.reciprocal(R[:, :], sd[:, :]).then_inc(r_ready, 1)
            e.wait_ge(r_ready, n + 1)

        def turns(e, n, body):
            if n == 4:
                for j in range(4):
                    body(0, j)
                return
            with e.Fori(0, n // 4) as i:
                for j in range(4):
                    body(i, j)

        at = [own]

        def own_buf(name, shape, dt=F32, lanes=LANES):
            at[0] = (at[0] + 31) // 32 * 32
            t = put(name, [lanes] + list(shape), dt, at=at[0])
            at[0] += int(np.prod(shape)) * 4
            assert at[0] <= nc.sbuf_usable_end, name
            return t

        B_st = own_buf("B_st", [2, SG, SH])
        C_st = own_buf("C_st", [2, SG, SH])
        psi = own_buf("psi", [SG])
        mag8 = own_buf("mag8", [SG])
        ru = own_buf("ru", [NSTEP])
        TA = own_buf("TA", [2, SG, STEP + 1])
        PB = own_buf("PB", [2, SG, STEP])
        sinb = own_buf("sinb", [2, GB, NSTEP])
        cosb = own_buf("cosb", [2, GB, NSTEP])
        Sx = own_buf("Sx", [2, GB, NSTEP])
        Zb = own_buf("Zb", [GB, NSTEP])
        D0 = own_buf("D0", [2, GB, NSTEP])
        Wb = own_buf("Wb", [GB, NSTEP])
        tA = own_buf("tA", [GB, NSTEP])
        Ksb = own_buf("Ksb", [2, GB, STEP, SH], lanes=SH)
        Ysb = own_buf("Ysb", [STEP, GB, SH], lanes=NSTEP)
        Tm = own_buf("Tm", [2, GB, STEP, SH])
        at = [x0_at + 32768]
        small = {n: own_buf("s5_" + n, [SG]) for n in
                 "dt lrdt th k phi aphi k8 phi8 mag sn cs den rden nr c1 c2 t3 cr ci s2r s2i s4r s4i".split()}
        AR = own_buf("AR", [2, SG, STEP])
        cmA = own_buf("cmA", [SG, STEP])
        cmB = own_buf("cmB", [SG, STEP])
        ru3 = own_buf("ru3", [NSTEP, STEP])
        at = [x0_at + 32768 + 16384 + 12288]
        DI = own_buf("DI", [SG, SH], lanes=SH)
        at = [x0_at]
        TB = own_buf("TB", [GB, STEP, SH])
        TBt = own_buf("TBt", [GB, STEP, SH])
        TC = own_buf("TC", [2, GB, STEP + 1, SH])
        TCt = own_buf("TCt", [GB, STEP + 1, SH])
        ST = own_buf("ST", [GB, LANES])
        Ub = own_buf("Ub", [2, GB, NSTEP])
        Ur = own_buf("Ur", [GB, NSTEP])
        assert at[0] <= x0_at + 32768
        grid = lambda t: t[:, :].rearrange("p (g c) -> p g c", g=GB)
        ang, kk, ff, absf, tB, g32 = grid(acc), grid(sq), grid(sd), grid(t32), grid(R), a32

        zeroed, dt_ready, phase_ready, trig_ready, tables_ready, ru_ready = (
            sem(n) for n in ("zeroed", "dt_ready", "phase_ready", "trig_ready", "tables_ready", "ru_ready"))
        vec_chain, u_loaded = sem("vec_chain"), sem("u_loaded")
        t_loaded = [sem("t_loaded_even"), sem("t_loaded_odd")]
        DB = Steps(sem("s5_in_tables"), "TB1 TB2 TB", ahead=4)
        DV = Steps(sem("s5_states"), "pr1 pr2 V Z po1 po2 W", ahead=4)
        DK = Steps(sem("s5_direct"), "Kd", ahead=4)
        AS = Steps(sem("s5_kept"), "ST1 ST2 K1 K2 Sx", ahead=4)
        AN = Steps(sem("s5_angles"), "absf sin cos", ahead=4)
        AY = Steps(sem("s5_y_kept"), "Y1 Y2", ahead=4)
        AX5 = Steps(sem("s5_gelu"), "g hi", ahead=4)
        EA = Steps(sem("s5_step_sums"), "ST1 ST2 K1 K2 S", ahead=4)
        EB = Steps(sem("s5_outputs"), "JS JZ Y1 Y2", ahead=4)
        DL = Steps(sem("s5_y_low"), "lo", ahead=4)
        ET = Steps(sem("s5_y_turned"), "YT", ahead=4)
        P5 = Steps(sem("s5_pool"), "ang D0 k f TC1 TC2 TC U1 U", ahead=4)
        chain = [0]

        def link(e, ins):
            chain[0] += 1
            ins.then_inc(vec_chain, 1)
            e.wait_ge(vec_chain, chain[0])

        def piped(e, step, total, drain, per=8):
            for T in range(per):
                step(0, T)
            with e.Fori(1, total // per) as i:
                for T in range(per):
                    step(i, T)
            for T in range(drain):
                step(total // per, T)

        def runs(i, q, total, per=8):
            return not isinstance(i, int) or 0 <= per * i + q < total

        def cut(t, i, q, width=GB, axis=1):
            d = slice((i * 2 + q) * width, (i * 2 + q + 1) * width) if isinstance(i, int) else bass.ds(i * (2 * width) + q * width, width)
            return t[:, d] if axis == 1 else t[:, :, d]

        def s5_loads(e):
            e.dma_start(const[:, :], a["const"]).then_inc(loaded, 16)
            e.dma_start(par[:, :], a["par"]).then_inc(loaded, 16)
            e.dma_start(h[:, :, :], a["xT"].rearrange("(k p) n -> p k n", p=LANES)).then_inc(loaded, 16)
            e.dma_start(B_st[:, :, :, :], a["B"]).then_inc(loaded, 16)
            e.dma_start(C_st[:, :, :, :], a["C"]).then_inc(loaded, 16)
            e.dma_start(Ur[:, :, :], a["xu"][:, 0:GB]).then_inc(u_loaded, 16)

        def s5_sync(e):
            for z in range(2):
                e.sem_inc(t_loaded[z], 16 * STEP)

            def block(i, q):
                if runs(i, q + 1, NBLK, 2):
                    e.wait_ge(P5.sem, P5.at("U1", (i * 2, q)))
                    e.dma_start(Ur[:, :, :], cut(a["xu"], i, q + 1)).then_inc(u_loaded, 16)
                e.wait_ge(DK.sem, DK.at("Kd", (i * 2, q)))
                for s in range(STEP):
                    e.dma_start(Tm[s * SH:(s + 1) * SH, q, :, s:STEP, :],
                                Ksb[:, q, :, 0:STEP - s, :]).then_inc(t_loaded[q], 16)
            with e.Fori(0, NBLK // 2 - 1) as i:
                for q in range(2):
                    block(i, q)
            for q in range(2):
                block(NBLK // 2 - 1, q)

        def s5_pool(e):
            e.memset(Tm[:, :, :, :, :], 0.0).then_inc(zeroed, 1)
            P5.open(e)
            e.wait_ge(loaded, 80)
            pool_start(e, 0)
            for m in range(KT):
                pool_square(e, 0, m)
            e.wait_ge(tables_ready, 1)
            e.wait_ge(ru_ready, 1)
            full = [LANES, GB, NSTEP]
            f4 = [LANES, GB, STEP + 1, SH]
            tt = e.tensor_tensor
            with e.Fori(0, NBLK // 2) as i:
                for q in range(2):
                    t = (i * 2, q)
                    P5.next(e, t).took("ang", tt(ang, cut(psi, i, q).unsqueeze(2).to_broadcast(full), C("cidx").unsqueeze(1).to_broadcast(full), ALU.mult))
                    e.wait_ge(DV.sem, DV.at("Z", (i * 2, q - 2)))
                    e.wait_ge(P5.sem, P5.at("ang", t))
                    P5.took("D0", tt(D0[:, q], cut(mag8, i, q).unsqueeze(2).to_broadcast(full), C("cnz").unsqueeze(1).to_broadcast(full), ALU.mult))
                    P5.took("k", e.tensor_scalar(kk, ang, ROUND, ROUND, ALU.add, ALU.subtract))
                    e.wait_ge(P5.sem, P5.at("k", t))
                    e.wait_ge(AN.sem, AN.at("sin", (i * 2, q - 1)))
                    P5.took("f", tt(ff, ang, kk, ALU.subtract))
                    e.wait_ge(EB.sem, EB.at("Y2", (i * 2, q - 2)))
                    P5.took("TC1", tt(TC[:, q], cut(C_st[:, 0], i, q).unsqueeze(2).to_broadcast(f4), cut(TA[:, 0], i, q).unsqueeze(3).to_broadcast(f4), ALU.mult))
                    P5.next(e, t).took("TC2", tt(TCt[:, :, :, :], cut(C_st[:, 1], i, q).unsqueeze(2).to_broadcast(f4), cut(TA[:, 1], i, q).unsqueeze(3).to_broadcast(f4), ALU.mult))
                    P5.next(e, t).took("TC", tt(TC[:, q], TC[:, q], TCt[:, :, :, :], ALU.add))
                    e.wait_ge(u_loaded, i * 32 + (16 * q + 16))
                    P5.took("U1", tt(Ub[:, q], Ur[:, :, :], cut(V("gain_u"), i, q).unsqueeze(2).to_broadcast(full), ALU.mult))
                    P5.next(e, t).took("U", tt(Ub[:, q], Ub[:, q], ru[:, :].unsqueeze(1).to_broadcast(full), ALU.mult))

        def s5_scalar(e):
            s = small
            e.wait_ge(loaded, 80)
            e.activation(s["dt"][:, :], V("log_dt"), ACT.Exp).then_inc(dt_ready, 1)
            e.wait_ge(phase_ready, 1)
            e.activation(s["mag"][:, :], s["lrdt"][:, :], ACT.Exp)
            e.activation(mag8[:, :], s["lrdt"][:, :], ACT.Exp, scale=8.0)
            e.activation(s["sn"][:, :], s["phi"][:, :], ACT.Sin)
            e.activation(s["cs"][:, :], s["aphi"][:, :], ACT.Sin, bias=half_pi[:, :], scale=-1.0).then_inc(trig_ready, 1)
            act_norm(e, 0, eps6)

            def step(i, T):
                if runs(i, T, NBLK, 2):
                    q, t = T, (i * 2, T)
                    e.wait_ge(P5.sem, P5.at("f", t))
                    e.wait_ge(AN.sem, AN.at("cos", (i * 2, q - 1)))
                    AN.took("absf", e.activation(absf, ff, ACT.Abs))
                    e.wait_ge(DV.sem, DV.at("po2", (i * 2, q - 2)))
                    AN.took("sin", e.activation(sinb[:, q], ff, ACT.Sin, scale=SIN_SCALE))
                    e.wait_ge(AN.sem, AN.at("absf", t))
                    AN.took("cos", e.activation(cosb[:, q], absf, ACT.Sin, bias=half_pi[:, :], scale=-SIN_SCALE))
                    e.wait_ge(EA.sem, EA.at("S", (i * 2, q - 1)))
                    for k in (1, 2):
                        e.wait_ge(EA.sem, EA.at(f"ST{k}", t))
                        AS.took(f"ST{k}", e.activation(ST[:, 4 * k - 4:4 * k, :], bk[k - 1].rearrange("p (g n) -> p g n", g=4), ACT.Copy))
                    e.wait_ge(t_loaded[q], i * (16 * STEP) + 16 * STEP)
                    for k in (1, 2):
                        e.wait_ge(EA.sem, EA.at(f"K{k}", t))
                        AS.took(f"K{k}", e.activation(Ksb[:, q, 4 * k - 4:4 * k, :, :], bank[4 + k][0:SH, :].rearrange("p (g s h) -> p g s h", g=4, s=STEP), ACT.Copy))
                    e.wait_ge(EA.sem, EA.at("S", t))
                    e.wait_ge(EB.sem, EB.at("JS", (i * 2, q - 2)))
                    AS.took("Sx", e.activation(Sx[:, q], grid(bank[2]), ACT.Copy))
                q = T - 2
                if runs(i, q, NBLK, 2):
                    t = (i * 2, q)
                    e.wait_ge(ET.sem, ET.at("YT", t))
                    e.wait_ge(DL.sem, DL.at("lo", (i * 2, q - 1)))
                    tok = bk[7].rearrange("p (s c) -> p s c", s=STEP)
                    AX5.took("g", e.activation(g32[:, :].rearrange("p (c s) -> p s c", s=STEP), tok, ACT.Gelu_apprx_tanh))
                    AX5.took("hi", e.activation(cut(x1h, i, q, 1).rearrange("p o (c s) -> p (o s) c", s=STEP), tok, ACT.Gelu_apprx_tanh))
                q = T - 1
                if runs(i, q, NBLK, 2):
                    e.wait_ge(ET.sem, ET.at("YT", (i * 2, q - 1)))
                    for k in (1, 2):
                        e.wait_ge(EB.sem, EB.at(f"Y{k}", (i * 2, q)))
                        AY.took(f"Y{k}", e.activation(Ysb[:, :, 4 * k - 4:4 * k, :].rearrange("p s g h -> p g s h"), ybank(k)[0:NSTEP, :].rearrange("p (g s h) -> p g s h", g=4, s=STEP), ACT.Copy))
            for s_ in (AS, AN, AY, AX5):
                s_.open(e)
            piped(e, step, NBLK, 2, 2)
            e.sem_inc(x_hi, 8)

        def ybank(k):
            return bank[4 if k == 1 else 2]

        def s5_vector(e):
            s = small
            v = lambda n: s[n][:, :]
            e.memset(half_pi[:, :], math.pi / 2)
            e.memset(eps6[:, :], 1e-6)
            e.memset(eps5[:, :], 1e-5)
            e.memset(Wb[:, :, 0:1], 0.0).then_inc(zeroed, 1)
            for s_ in (DB, DV, DK, DL):
                s_.open(e)
            e.wait_ge(loaded, 80)
            e.sem_inc(h_ready, 8)
            e.wait_ge(dt_ready, 1)
            tt, ts = e.tensor_tensor, e.tensor_scalar
            link(e, tt(v("lrdt"), V("lam_re"), v("dt"), ALU.mult))
            link(e, tt(v("th"), V("lam_im"), v("dt"), ALU.mult))

            def reduced(out, x, k):
                link(e, ts(v(k), v(x), 1.0 / (2 * math.pi), ROUND, ALU.mult, ALU.add))
                link(e, ts(v(k), v(k), ROUND, None, ALU.subtract))
                link(e, e.scalar_tensor_tensor(v(out), v(k), -TWO_PI_HI, v(x), ALU.mult, ALU.add))
                link(e, e.scalar_tensor_tensor(v(out), v(k), -TWO_PI_LO, v(out), ALU.mult, ALU.add))

            reduced("phi", "th", "k")
            link(e, ts(v("th"), v("phi"), 8.0, None, ALU.mult))
            link(e, ts(v("phi"), v("phi"), PI_SAFE, -PI_SAFE, ALU.min, ALU.max))
            link(e, e.scalar_tensor_tensor(v("aphi"), v("phi"), -1.0, v("phi"), ALU.mult, ALU.max))
            e.sem_inc(phase_ready, 1)
            reduced("phi8", "th", "k8")
            link(e, ts(psi[:, :], v("phi8"), 1.0 / (2 * math.pi), None, ALU.mult))
            e.wait_ge(trig_ready, 1)
            ar, ai = TA[:, 0, :, 1], TA[:, 1, :, 1]
            e.memset(TA[:, 0, :, 0:1], 1.0)
            e.memset(TA[:, 1, :, 0:1], 0.0)
            e.memset(AR[:, 0, :, 7:8], 1.0)
            e.memset(AR[:, 1, :, 7:8], 0.0)
            link(e, tt(ar, v("mag"), v("cs"), ALU.mult))
            link(e, tt(ai, v("mag"), v("sn"), ALU.mult))
            link(e, tt(v("den"), V("lam_re"), V("lam_re"), ALU.mult))
            link(e, tt(v("t3"), V("lam_im"), V("lam_im"), ALU.mult))
            link(e, tt(v("den"), v("den"), v("t3"), ALU.add))
            link(e, e.reciprocal(v("rden"), v("den")))
            link(e, ts(v("nr"), ar, -1.0, None, ALU.add))
            link(e, tt(v("c1"), v("nr"), V("lam_re"), ALU.mult))
            link(e, tt(v("c2"), ai, V("lam_im"), ALU.mult))
            link(e, tt(v("c1"), v("c1"), v("c2"), ALU.add))
            link(e, tt(v("cr"), v("c1"), v("rden"), ALU.mult))
            link(e, tt(v("c1"), ai, V("lam_re"), ALU.mult))
            link(e, tt(v("c2"), v("nr"), V("lam_im"), ALU.mult))
            link(e, tt(v("c1"), v("c1"), v("c2"), ALU.subtract))
            link(e, tt(v("ci"), v("c1"), v("rden"), ALU.mult))

            def cmul(o, x, y, n):
                A, B = cmA[:, :, 0:n], cmB[:, :, 0:n]
                yr, yi = (q.unsqueeze(2).to_broadcast([LANES, SG, n]) for q in y)
                link(e, tt(A, x[0], yr, ALU.mult))
                link(e, tt(B, x[1], yi, ALU.mult))
                link(e, tt(o[0], A, B, ALU.subtract))
                link(e, tt(A, x[0], yi, ALU.mult))
                link(e, tt(B, x[1], yr, ALU.mult))
                link(e, tt(o[1], A, B, ALU.add))

            def cols(t, lo, hi):
                return t[:, 0, :, lo:hi], t[:, 1, :, lo:hi]

            a1 = (ar, ai)
            a2 = (v("s2r"), v("s2i"))
            a4 = (v("s4r"), v("s4i"))
            u2 = lambda q: tuple(x.unsqueeze(2) for x in q)
            cmul(u2(a2), u2(a1), a1, 1)
            cmul(u2(a4), u2(a2), a2, 1)
            cmul(cols(TA, 8, 9), u2(a4), a4, 1)
            cmul(cols(TA, 2, 4), cols(TA, 0, 2), a2, 2)
            cmul(cols(TA, 4, 8), cols(TA, 0, 4), a4, 4)
            link(e, e.tensor_copy(AR[:, :, :, 6:7], TA[:, :, :, 1:2]))
            cmul(cols(AR, 4, 6), cols(AR, 6, 8), a2, 2)
            cmul(cols(AR, 0, 4), cols(AR, 4, 8), a4, 4)
            cmul(cols(PB, 0, 8), cols(AR, 0, 8), (v("cr"), v("ci")), 8)
            link(e, ts(PB[:, 1], PB[:, 1], C("sgn"), None, ALU.mult))
            link(e, ts(TA[:, 0], TA[:, 0], C("nsgn"), None, ALU.mult))
            link(e, ts(TA[:, 1], TA[:, 1], -1.0, None, ALU.mult))
            dfull = [SH, SG, SH]
            link(e, tt(DI[:, :, :], V("d_h", rows=SH).unsqueeze(2).to_broadcast(dfull), C("id16", rows=SH).unsqueeze(1).to_broadcast(dfull), ALU.mult))
            e.sem_inc(tables_ready, 1)
            dve_norm(e, 0)
            rf = [LANES, NSTEP, STEP]
            link(e, tt(ru3[:, :, :], R[:, :].rearrange("p (c s) -> p c s", s=STEP), C("sel").unsqueeze(1).to_broadcast(rf), ALU.mult))
            e.reduce_sum(ru[:, :].unsqueeze(2), ru3[:, :, :], axis=AX.X).then_inc(ru_ready, 1)

            f4 = [LANES, GB, STEP, SH]

            def tables(i, q):
                t = (i * 2, q)
                e.wait_ge(EA.sem, EA.at("K2", (i * 2, q - 1)))
                DB.took("TB1", tt(TB[:, :, :, :], cut(B_st[:, 0], i, q).unsqueeze(2).to_broadcast(f4), cut(PB[:, 0], i, q).unsqueeze(3).to_broadcast(f4), ALU.mult))
                DB.took("TB2", tt(TBt[:, :, :, :], cut(B_st[:, 1], i, q).unsqueeze(2).to_broadcast(f4), cut(PB[:, 1], i, q).unsqueeze(3).to_broadcast(f4), ALU.mult))
                DB.next(e, t).took("TB", tt(TB[:, :, :, :], TB[:, :, :, :], TBt[:, :, :, :], ALU.add))

            flat = lambda t: t.rearrange("p g c -> p (g c)")

            def step(i, T):
                q = T - 1
                if runs(i, q, NBLK, 2):
                    t, z = (i * 2, q), q % 2
                    n = lambda: DV.next(e, t)
                    e.wait_ge(AS.sem, AS.at("Sx", t))
                    DV.took("pr1", tt(tA[:, :, :], Sx[:, z], cosb[:, z], ALU.mult))
                    e.wait_ge(EB.sem, EB.at("JS", t))
                    DV.took("pr2", tt(tB, grid(bank[3]), sinb[:, z], ALU.mult))
                    n().took("V", tt(tA[:, :, :], tA[:, :, :], tB, ALU.subtract))
                    e.wait_ge(P5.sem, P5.at("D0", t))
                    n().took("Z", e.tensor_tensor_scan(flat(Zb[:, :, :]), flat(D0[:, z]), flat(tA[:, :, :]), 0.0, ALU.mult, ALU.add))
                    n().took("po1", tt(tA[:, :, :], Zb[:, :, :], cosb[:, z], ALU.mult))
                    e.wait_ge(EB.sem, EB.at("JZ", t))
                    DV.took("po2", tt(tB, grid(bank[3]), sinb[:, z], ALU.mult))
                    e.wait_ge(EB.sem, EB.at("Y2", (i * 2, q - 1)))
                    n().took("W", tt(Wb[:, :, 1:], tA[:, :, :NSTEP - 1], tB[:, :, :NSTEP - 1], ALU.add))
                if runs(i, T, NBLK, 2):
                    e.wait_ge(AS.sem, AS.at("K2", (i * 2, T)))
                    DK.took("Kd", tt(Ksb[:, T % 2, :, 0, :], Ksb[:, T % 2, :, 0, :], cut(DI, i, T), ALU.add))
                if runs(i, T + 1, NBLK, 2):
                    tables(i, T + 1)
                q = T - 2
                if runs(i, q, NBLK, 2):
                    e.wait_ge(AX5.sem, AX5.at("hi", (i * 2, q)))
                    DL.took("lo", e.tensor_tensor(cut(x1l, i, q, 1), one(g32[:, :]), cut(x1h, i, q, 1).bitcast(F32), ALU.subtract))
                    e.wait_ge(DL.sem, DL.at("lo", (i * 2, q)))
                    e.sem_inc(x_ready, 1)

            tables(0, 0)
            for q in range(2):
                step(0, q)
            with e.Fori(1, NBLK // 2 - 1) as i:
                for q in range(2):
                    step(i, q)
            for q in range(4):
                step(NBLK // 2 - 1, q)

        def s5_tensor(e):
            for s_ in (EA, EB, ET):
                s_.open(e)
            pe_norm(e, 0)
            e.wait_ge(zeroed, 2)

            def step(i, T):
                q = T - 1
                if runs(i, q, NBLK, 2):
                    e.wait_ge(AS.sem, AS.at("Sx", (i * 2, q)))
                    e.wait_ge(DV.sem, DV.at("po2", (i * 2, q - 1)))
                    EB.took("JS", e.matmul(bk[3], C("turn"), Sx[:, q % 2].rearrange("p g c -> p (g c)"), start=True, stop=True))
                q = T - 2
                if runs(i, q, NBLK, 2):
                    e.wait_ge(AY.sem, AY.at("Y2", (i * 2, q)))
                    e.wait_ge(AX5.sem, AX5.at("hi", (i * 2, q - 1)))
                    for t in range(STEP):
                        turned = e.transpose if t else e.matmul
                        last = turned(bank[7][:, t * NSTEP:(t + 1) * NSTEP], Ysb[:, t].rearrange("p g h -> p (g h)"), C("ident", hi=NSTEP, rows=NSTEP))
                    ET.took("YT", last)
                if runs(i, T, NBLK, 2):
                    q, t = T, (i * 2, T)
                    z = q % 2
                    e.wait_ge(DB.sem, DB.at("TB", t))
                    for k in (1, 2):
                        e.wait_ge(AS.sem, AS.at(f"ST{k}", (i * 2, q - 1)))
                        for g in range(4):
                            last = e.transpose(bank[k - 1][:, g * LANES:(g + 1) * LANES], TB[:, 4 * k - 4 + g].rearrange("p s h -> p (s h)"), C("ident"))
                        EA.took(f"ST{k}", last)
                    e.wait_ge(P5.sem, P5.at("TC", t))
                    for k in (1, 2):
                        e.wait_ge(AS.sem, AS.at(f"K{k}", (i * 2, q - 1)))
                        for g in range(4):
                            gg = 4 * k - 4 + g
                            last = e.matmul(bank[4 + k][0:SH, g * LANES:(g + 1) * LANES], TB[:, gg, STEP - 1], TC[:, z, gg, 0:STEP].rearrange("p s h -> p (s h)"), start=True, stop=True)
                        EA.took(f"K{k}", last)
                    e.wait_ge(P5.sem, P5.at("U", t))
                    e.wait_ge(AS.sem, AS.at("ST2", t))
                    e.wait_ge(AY.sem, AY.at("Y2", (i * 2, q - 2)))
                    for g in range(GB):
                        last = e.matmul(bank[2][:, g * NSTEP:(g + 1) * NSTEP], ST[:, g], Ub[:, z, g], start=True, stop=True)
                    EA.took("S", last)
                q = T - 1
                if runs(i, q, NBLK, 2):
                    t, z = (i * 2, q), q % 2
                    e.wait_ge(DV.sem, DV.at("Z", t))
                    EB.took("JZ", e.matmul(bk[3], C("turn"), Zb[:, :, :].rearrange("p g c -> p (g c)"), start=True, stop=True))
                    e.wait_ge(DV.sem, DV.at("W", t))
                    e.wait_ge(t_loaded[z], i * (16 * STEP) + 16 * STEP * (2 + q // 2))
                    for k in (1, 2):
                        if k == 1:
                            e.wait_ge(AY.sem, AY.at("Y1", (i * 2, q - 1)))
                        elif runs(i, T, NBLK, 2):
                            e.wait_ge(AS.sem, AS.at("Sx", (i * 2, q + 1)))
                        for g in range(4):
                            gg = 4 * k - 4 + g
                            o = ybank(k)[0:NSTEP, g * LANES:(g + 1) * LANES]
                            e.matmul(o, Ub[:, z, gg], Tm[:, z, gg].rearrange("p s h -> p (s h)"), start=True, stop=False)
                            last = e.matmul(o, Wb[:, gg], TC[:, z, gg, 1:].rearrange("p s h -> p (s h)"), start=False, stop=True)
                        EB.took(f"Y{k}", last)
            piped(e, step, NBLK, 2, 2)

        sg = Zb[:, :, :].rearrange("p g c -> p (g c)")
        sg_ready = sem("sg_ready")

        def glu_scalar(e):
            def body(i, j):
                act_split(e, U_GLU + j + 2, i)
                if j % 2 == 0:
                    e.wait_ge(unit_done, after(U_GLU, j, i, 1))
                    e.wait_ge(bank_free, after(U_GLU, j, i, 4))
                    e.activation(sg, bk[(U_GLU + j) % 4], ACT.Sigmoid).then_inc(sg_ready, 1)
                else:
                    act_x(e, 1, 1, i * 2 + j // 2, "mlp0", x0h)
            turns(e, 16, body)

        def glu_vector(e):
            def body(i, j):
                dve_split(e, U_GLU + j + 2, i)
                m = i * 2 + j // 2
                if j % 2 == 0:
                    e.wait_ge(sg_ready, m + 1)
                    e.sem_inc(bank_free, 1)
                else:
                    b = evac_start(e, U_GLU, j, i)
                    e.tensor_tensor(t32[:, :], b, sg, ALU.mult).then_inc(bank_free, 1)
                    e.wait_ge(bank_free, after(U_GLU, j, i, 5))
                    e.tensor_tensor(tile(h, m), tile(h, m), one(t32[:, :]), ALU.add).then_inc(h_ready, 1)
                    e.wait_ge(h_ready, m + 9)
                    dve_x(e, 1, m, "mlp0", x0h, x0l)
            turns(e, 16, body)

        def ready(s, n):
            return lambda k: (s, n + (k + 1))

        def glu_tensor(e):
            turns(e, 16, lambda i, j: pe_unit(e, U_GLU, j, i, x1h, x1l, ready(x_ready, 0) if j == 0 else None))

        def pool_h(e, n, steps=KT):
            pool_start(e, n)
            with e.Fori(0, steps) as m:
                pool_square(e, n, m)

        a_hi, a_ready = sem("a_hi"), sem("a_ready")

        def mlp_parts(i, n, p_in, p_out, gain):
            u0 = (U_MLP0, U_MLP1)[i]
            a0 = 32 * i

            def up_scalar(e, q):
                def body(t, j):
                    act_split(e, u0 + j + 2, q * 4 + t)
                    m = t * 4 + j
                    e.wait_ge(bank_free, after(u0, j, q * 4 + t, 5))
                    e.activation(tile(x1h, m), one(t32[:, :]), ACT.Square).then_inc(a_hi, 1)
                    e.wait_ge(a_ready, q * 8 + m + (a0 + 1))
                    e.activation(a32[:, :], t32[:, :], ACT.Square).then_inc(a_hi, 1)
                turns(e, 8, body)

            def up_vector(e, q):
                def body(t, j):
                    dve_split(e, u0 + j + 2, q * 4 + t)
                    m = t * 4 + j
                    b = evac_start(e, u0, j, q * 4 + t)
                    e.scalar_tensor_tensor(t32[:, :], b, 0.0, R[:, :], ALU.max, ALU.mult).then_inc(bank_free, 1)
                    e.wait_ge(a_hi, (q * 8 + m) * 2 + (2 * a0 + 2))
                    e.tensor_tensor(tile(x1l, m), one(a32[:, :]), tile(x1h, m).bitcast(F32), ALU.subtract).then_inc(a_ready, 1)
                turns(e, 8, body)

            def up_tensor(e, q):
                turns(e, 8, lambda t, j: pe_unit(e, u0, j, q * 4 + t, x0h, x0l, ready(x_ready, 8 * p_in) if j == 0 else None))

            def down_scalar(e, q, final):
                def body(t, j):
                    act_split(e, u0 + 8 + j + 2, q * 4 + t)
                    if final:
                        act_x(e, n, p_out, t * 4 + j, gain, x0h)
                turns(e, 8, body)

            def down_vector(e, q, final):
                def body(t, j):
                    dve_split(e, u0 + 8 + j + 2, q * 4 + t)
                    m = t * 4 + j
                    b = evac_start(e, u0 + 8, j, q * 4 + t)
                    e.tensor_tensor(tile(h, m), tile(h, m), one(b), ALU.add).then_inc(bank_free, 1)
                    if final:
                        e.wait_ge(bank_free, after(u0 + 8, j, q * 4 + t, 5))
                        e.sem_inc(h_ready, 1)
                        dve_x(e, p_out, m, gain, x0h, x0l)
                turns(e, 8, body)

            def down_tensor(e, q):
                turns(e, 8, lambda t, j: pe_unit(e, u0 + 8, j, q * 4 + t, x1h, x1l, (lambda k: (a_ready, q * 8 + (a0 + k + 2))) if j == 0 else None))

            def vector(e):
                if i == 0:
                    e.sem_inc(a_ready, 1)
                dve_norm(e, n - 1)
                with e.Fori(0, 3) as q:
                    up_vector(e, q)
                    down_vector(e, q, False)
                up_vector(e, 3)
                down_vector(e, 3, True)

            def scalar(e):
                act_norm(e, n - 1, eps6)
                with e.Fori(0, 3) as q:
                    up_scalar(e, q)
                    down_scalar(e, q, False)
                up_scalar(e, 3)
                down_scalar(e, 3, True)

            def tensor(e):
                pe_norm(e, n - 1)
                with e.Fori(0, 3) as q:
                    up_tensor(e, q)
                    down_tensor(e, q)
                up_tensor(e, 3)
                down_tensor(e, 3)

            return scalar, vector, tensor

        at = [own]
        p_in = own_buf("p_in", [2, 2, TOK])
        p_h, p_l = own_buf("p_h", [2, TOK], F32R), own_buf("p_l", [2, TOK], F32R)
        pp_at = at[0]
        Pp = own_buf("Pp", [KT, TOK])
        gs = own_buf("gs", [TOK])
        kept = at[0]
        p_loaded, p_hi, p_ready, p_mm, p_out = (sem(s) for s in ("p_loaded", "p_hi", "p_ready", "p_mm", "p_out"))

        def ple_parts(i, n, p_out_set, gain):
            up, u0 = (U_P0, U_P1)[i], (U_GATE0, U_GATE1)[i]

            def scalar(e):
                if i == 0:
                    e.wait_ge(p_loaded, 16)
                else:
                    e.wait_ge(unit_done, U_P1)
                e.activation(p_h[:, :, :], p_in[:, i], ACT.Copy).then_inc(p_hi, 1)
                for j in range(2):
                    act_split(e, up + j + 2, 0)
                    for mm in range(4):
                        t = 8 * i + 4 * j + mm
                        e.wait_ge(p_mm, t + 1)
                        e.activation(Pp[:, 4 * j + mm], bk[4 + mm], ACT.Copy).then_inc(p_out, 1)
                act_norm(e, n - 1, eps6)

                def body(t, j):
                    act_split(e, u0 + j + 2, t)
                    m = t * 4 + j
                    e.wait_ge(bank_free, after(u0, j, t, 5))
                    e.activation(gs[:, :], t32[:, :], ACT.Sigmoid).then_inc(sg_ready, 1)
                    if gain:
                        act_x(e, n, p_out_set, m, gain, x1h)
                turns(e, 8, body)

            def vector(e):
                e.wait_ge(p_hi, i + 1)
                e.tensor_tensor(p_l[:, :, :], p_in[:, i], p_h[:, :, :].bitcast(F32), ALU.subtract).then_inc(p_ready, 1)
                for j in range(2):
                    dve_split(e, up + j + 2, 0)
                    e.wait_ge(unit_done, up + j + 1)
                    e.sem_inc(bank_free, 1)
                dve_norm(e, n - 1)
                e.wait_ge(p_out, 8 * i + 8)

                def body(t, j):
                    dve_split(e, u0 + j + 2, t)
                    m = t * 4 + j
                    b = evac_start(e, u0, j, t)
                    e.tensor_tensor(t32[:, :], b, R[:, :], ALU.mult).then_inc(bank_free, 1)
                    e.wait_ge(sg_ready, m + (8 + 8 * i + 1))
                    e.tensor_tensor(one(a32[:, :]), one(gs[:, :]), tile(Pp, m), ALU.mult).then_inc(gated, 1)
                    e.wait_ge(gated, m + (8 * i + 1))
                    e.tensor_tensor(tile(h, m), tile(h, m), one(a32[:, :]), ALU.add).then_inc(h_ready, 1)
                    if gain:
                        dve_x(e, p_out_set, m, gain, x1h, x1l)
                turns(e, 8, body)

            def tensor(e):
                e.wait_ge(p_ready, i + 1)
                for j in range(2):
                    e.wait_ge(w_split, up + j + 1)
                    e.wait_ge(bank_free, up + j + 1)
                    for mm in range(4):
                        t = 8 * i + 4 * j + mm
                        if j:
                            e.wait_ge(p_out, t - 3)
                        w = (up + j) % 2
                        for k in range(2):
                            kk = 2 * mm + k
                            e.matmul(bk[4 + mm], w_hi[:, w, kk], p_h[:, k], start=(k == 0), stop=False)
                            e.matmul(bk[4 + mm], w_hi[:, w, kk], p_l[:, k], start=False, stop=False)
                            last = e.matmul(bk[4 + mm], w_lo[:, w, kk], p_h[:, k], start=False, stop=(k == 1))
                        last.then_inc(p_mm, 1)
                    e.wait_ge(p_mm, 8 * i + 4 * j + 4)
                    e.sem_inc(unit_done, 1)
                e.wait_ge(p_out, 8 * i + 8)
                pe_norm(e, n - 1)
                turns(e, 8, lambda t, j: pe_unit(e, u0, j, t, x0h, x0l, ready(x_ready, 8 * (p_out_set - 1)) if j == 0 else None))

            return scalar, vector, tensor

        gated = sem("gated")

        def more_x_scalar(e, n, p, gain, xh):
            with e.Fori(0, KT) as m:
                act_x(e, n, p, m, gain, xh)

        def more_x_vector(e, p, gain, xh, xl):
            with e.Fori(0, KT) as m:
                dve_x(e, p, m, gain, xh, xl)

        at = [kept]
        kdup = own_buf("kdup", [4, TOK])
        kv32 = own_buf("kv32", [4, TOK])
        v_tok = own_buf("v_tok", [4, 256])
        q32 = put("q32", [LANES, KT, TOK], at=pp_at)
        at = [x0_at]
        Ks = own_buf("Ks", [2, LANES + TOK])
        Qs = own_buf("Qs", [2, 2, TOK])
        Vs = own_buf("Vs", [2, 5, 64])
        Sm = own_buf("Sm", [4, 2, 2, 256])
        PT = put("PT", [LANES, 2, 512], at=acc_at)
        st = {n: own_buf("st_" + n, [4, 4]) for n in "mx nm df sm es rc".split()}
        assert at[0] <= x0_at + 32768
        rope_mm, kv_t, kv_tok, k_dup = sem("rope_mm"), sem("kv_t"), sem("kv_tok"), sem("k_dup")
        RO = Steps(sem("rope_steps"), "cos sin sum")

        def rope_tensor(e, u0, j, n4, src, turn):
            e.wait_ge(bank_free, after(u0, j, n4, 5))
            e.wait_ge(RO.sem, RO.at("sin", (turn[0], turn[1] - 2)))
            e.matmul(bk[5 + j % 2], C("ropeswap"), src, start=True, stop=True).then_inc(rope_mm, 1)

        def rope_vector(e, src, j, turn):
            RO.next(e, turn).took("cos", e.tensor_tensor(one(t32[:, :]), src, one(C("rcos")), ALU.mult))
            e.wait_ge(rope_mm, turn + 1 if isinstance(turn, int) else turn[0] + (turn[1] + 1))
            RO.next(e, turn).took("sin", e.tensor_tensor(a32[:, :], bk[5 + j % 2], C("rsin"), ALU.mult))
            RO.next(e, turn).took("sum", e.tensor_tensor(src, one(t32[:, :]), one(a32[:, :]), ALU.add))

        def kv_scalar(e):
            act_norm(e, 3, eps6)
            for j in range(4):
                act_split(e, U_KV + j + 2, 0)
                if j in (2, 3):
                    t = j - 2
                    e.wait_ge(RO.sem, RO.at("sum", t))
                    for half in range(2):
                        for to in range(2):
                            last = e.activation(kdup[64 * to:64 * to + 64, 2 * t + half], kv32[64 * half:64 * half + 64, t], ACT.Copy)
                            last.then_inc(k_dup, 1)
            for t in range(2):
                e.wait_ge(kv_t, t + 1)
                e.activation(v_tok[:, :, LANES * t:LANES * (t + 1)], bk[7 - 2 * t].rearrange("p (c n) -> p c n", c=4), ACT.Copy).then_inc(kv_tok, 1)

        def kv_vector(e):
            dve_norm(e, 3)
            RO.open(e)
            for j in range(4):
                dve_split(e, U_KV + j + 2, 0)
                b = evac_start(e, U_KV, j, 0)
                e.tensor_tensor(kv32[:, j], b, R[:, :], ALU.mult).then_inc(bank_free, 1)
                if j in (1, 2):
                    e.wait_ge(bank_free, U_KV + j + 4)
                    rope_vector(e, kv32[:, j - 1:j], j - 1, j - 1)

        def kv_tensor(e):
            pe_norm(e, 3)
            for j in range(4):
                pe_unit(e, U_KV, j, 0, x1h, x1l, ready(x_ready, 24) if j == 0 else None)
                if j in (1, 2):
                    e.wait_ge(bank_free, U_KV + j + 4)
                    e.matmul(bk[4 + j], C("ropeswap"), kv32[:, j - 1], start=True, stop=True).then_inc(rope_mm, 1)
            for t in range(2):
                e.wait_ge(bank_free, U_KV + 7 + t)
                if t:
                    e.wait_ge(RO.sem, RO.at("sin", 0))
                for c in range(4):
                    last = e.transpose(bank[7 - 2 * t][:, c * LANES:(c + 1) * LANES], kv32[:, 2 + t, c * LANES:(c + 1) * LANES], C("ident"))
                last.then_inc(kv_t, 1)

        def q_scalar(e):
            turns(e, 8, lambda t, j: act_split(e, U_Q + j + 2, t))

        def q_vector(e):
            def body(t, j):
                dve_split(e, U_Q + j + 2, t)
                m = t * 4 + j
                b = evac_start(e, U_Q, j, t)
                e.tensor_tensor(tile(q32, m), one(b), one(R[:, :]), ALU.mult).then_inc(bank_free, 1)
                if j:
                    e.wait_ge(bank_free, after(U_Q, j - 1, t, 5))
                    rope_vector(e, tile(q32, t * 4 + (j - 1)), j - 1, (t * 4, j + 1))
                if j == 3:
                    e.wait_ge(bank_free, after(U_Q, j, t, 5))
                    rope_vector(e, tile(q32, m), j, (t * 4, j + 2))
            turns(e, 8, body)

        def q_tensor(e):
            e.wait_ge(kv_tok, 2)

            def body(t, j):
                pe_unit(e, U_Q, j, t, x0h, x0l, ready(x_ready, 32) if j == 0 else None)
                m = t * 4 + j
                if j:
                    rope_tensor(e, U_Q, j - 1, t, tile(q32, t * 4 + (j - 1)), (t * 4, j + 1))
                if j == 3:
                    rope_tensor(e, U_Q, 3, t, tile(q32, m), (t * 4, j + 2))
            turns(e, 8, body)

        PKQ = Steps(sem("att_copies"), "K Q V")
        DA = Steps(sem("att_max"), "m0 m1 max sink neg dif", ahead=8)
        AB = Steps(sem("att_exp"), "e0 e1 e2 e3 es", ahead=8)
        DC = Steps(sem("att_scale"), "den rec scale", ahead=8)
        ES = Steps(sem("att_scores"), "s", ahead=8)
        ED = Steps(sem("att_turned"), "t0 t1", ahead=8)
        AE = Steps(sem("att_weights"), "w0 w1", ahead=8)
        EF = Steps(sem("att_out"), "o", ahead=8)
        AG = Steps(sem("att_out_hi"), "hi", ahead=8)
        DH = Steps(sem("att_out_lo"), "lo", ahead=8)
        pads = sem("pads")
        NT = 16

        def att_pool(e):
            PKQ.open(e)
            e.wait_ge(unit_done, U_O)
            for t, cut in ((Ks, Ks[:, :, 0:LANES]), (Vs, Vs[:, :, 0])):
                e.memset(cut, 0.0).then_inc(pads, 1)
            e.wait_ge(RO.sem, RO.at("sum", 9))
            e.wait_ge(k_dup, 8)
            e.wait_ge(kv_tok, 2)
            with e.Fori(0, 2) as i:
                for x in range(2):
                    kh = (i * 2, x)
                    e.wait_ge(ES.sem, ES.at("s", (i * 8, 4 * x - 5)))
                    PKQ.next(e, kh).took("K", e.tensor_copy(Ks[:, x:x + 1, LANES:], tile(kdup, i * 2 + x)))
                    PKQ.next(e, kh).took("Q", e.tensor_copy(Qs[:, x], q32[:, bass.ds(i * 4 + 2 * x, 2)]))
                    e.wait_ge(EF.sem, EF.at("o", (i * 8, 4 * x - 5)))
                    PKQ.next(e, kh).took("V", e.tensor_copy(Vs[:, x, 1:5], v_tok[:, :, bass.ds(i * 128 + 64 * x, 64)]))

        def att_tensor(e):
            for s in (ES, ED, EF):
                s.open(e)
            e.wait_ge(pads, 2)

            def step(i, T):
                if runs(i, T, NT):
                    x, n, b = T // 4, T % 4, 2 * (T % 2)
                    if n == 0:
                        e.wait_ge(PKQ.sem, PKQ.at("Q", (i * 2, x)))
                    e.wait_ge(DA.sem, DA.at("m1", (i * 8, T - 2)))
                    for g in range(4):
                        hf, gg = g % 2, g // 2
                        last = e.matmul(bank[b + hf][:, gg * 256:gg * 256 + 256], Qs[64 * hf:64 * hf + 64, x, gg, n * LANES:(n + 1) * LANES],
                                        Ks[64 * hf:64 * hf + 64, x, n * LANES:(n + 2) * LANES], start=True, stop=True)
                    ES.took("s", last)
                q = T - 3
                if runs(i, q, NT):
                    e.wait_ge(DC.sem, DC.at("scale", (i * 8, q)))
                    for kt in range(2):
                        e.wait_ge(AE.sem, AE.at(f"w{kt}", (i * 8, q - 1)))
                        for g in range(4):
                            last = e.transpose(bank[5 + kt][:, g * LANES:(g + 1) * LANES], Sm[:, q % 4, g // 2, g % 2, kt * LANES:(kt + 1) * LANES], C("ident"))
                        ED.took(f"t{kt}", last)
                q = T - 4
                if runs(i, q, NT):
                    x, n = q % 8 // 4, q % 4
                    if n == 0:
                        e.wait_ge(PKQ.sem, PKQ.at("V", (i * 2, q // 4)))
                    e.wait_ge(AE.sem, AE.at("w1", (i * 8, q)))
                    e.wait_ge(DH.sem, DH.at("lo", (i * 8, q - 2)))
                    for hf in range(2):
                        for kt in range(2):
                            last = e.matmul(bank[7 - 3 * (q % 2)][64 * hf:64 * hf + 64, 0:256], Vs[:, x, n + kt], PT[:, kt, hf * 256:hf * 256 + 256], start=(kt == 0), stop=(kt == 1))
                    EF.took("o", last)
            piped(e, step, NT, 6)

        def att_vector(e):
            for s in (DA, DC, DH):
                s.open(e)

            def step(i, T):
                if runs(i, T, NT):
                    b, z, t = 2 * (T % 2), T % 4, (i * 8, T)
                    e.wait_ge(ES.sem, ES.at("s", t))
                    e.wait_ge(ED.sem, ED.at("t1", (i * 8, T - 4)))
                    mask = C("band0" if T % 4 == 0 else "band").unsqueeze(1).to_broadcast([LANES, 2, 256])
                    for hf in range(2):
                        DA.took(f"m{hf}", e.scalar_tensor_tensor(Sm[:, z, hf], bank[b + hf][:, :].rearrange("p (g k) -> p g k", g=2), 0.125, mask, ALU.mult, ALU.add))
                    flat = Sm[:, z].rearrange("p a b k -> p (a b) k")
                    DA.next(e, t).took("max", e.reduce_max(st["mx"][:, z].unsqueeze(2), flat, axis=AX.X))
                    s0 = PC["sinks"][0]
                    sk = par[:, bass.ds(i * 8 + (s0 + 4 * (T // 4)), 4)].rearrange("p (g f) -> p f g", f=2)
                    v = lambda nm: st[nm][:, z].rearrange("p (f g) -> p f g", f=2)
                    DA.next(e, t).took("sink", e.tensor_tensor(v("mx"), v("mx"), sk, ALU.max))
                    DA.next(e, t).took("neg", e.tensor_scalar(st["nm"][:, z], st["mx"][:, z], -1.0, None, ALU.mult))
                    DA.next(e, t).took("dif", e.tensor_tensor(v("df"), sk, v("mx"), ALU.subtract))
                q = T - 2
                if runs(i, q, NT):
                    t, z = (i * 8, q), q % 4
                    e.wait_ge(AB.sem, AB.at("es", t))
                    DC.next(e, t).took("den", e.tensor_tensor(st["rc"][:, z], st["sm"][:, z], st["es"][:, z], ALU.add))
                    DC.next(e, t).took("rec", e.reciprocal(st["rc"][:, z], st["rc"][:, z]))
                    flat = Sm[:, z].rearrange("p a b k -> p (a b) k")
                    DC.next(e, t).took("scale", e.tensor_tensor(flat, flat, st["rc"][:, z].unsqueeze(2).to_broadcast([LANES, 4, 256]), ALU.mult))
                q = T - 5
                if runs(i, q, NT):
                    e.wait_ge(AG.sem, AG.at("hi", (i * 8, q)))
                    DH.took("lo", e.tensor_tensor(o_tiles(x1l, i, q), o_bank(q), o_tiles(x1h, i, q).bitcast(F32), ALU.subtract))
            piped(e, step, NT, 6)

        def o_tiles(x1, i, q):
            n, k = q % 4, 2 * (q // 4)
            return x1[:, i * 4 + k:i * 4 + k + 2, n * LANES:(n + 1) * LANES] if isinstance(i, int) else x1[:, bass.ds(i * 4 + k, 2), n * LANES:(n + 1) * LANES]

        def o_bank(q):
            return bank[7 - 3 * (q % 2)][:, 0:256].rearrange("p (g q) -> p g q", g=2)

        def att_scalar(e):
            for s in (AB, AE, AG):
                s.open(e)

            def step(i, T):
                q = T - 1
                if runs(i, q, NT):
                    z = q % 4
                    e.wait_ge(DA.sem, DA.at("dif", (i * 8, q)))
                    for g in range(4):
                        s = Sm[:, z, g // 2, g % 2]
                        AB.took(f"e{g}", e.activation(s, s, ACT.Exp, bias=st["nm"][:, z, g:g + 1], accum_out=st["sm"][:, z, g:g + 1]))
                    AB.took("es", e.activation(st["es"][:, z], st["df"][:, z], ACT.Exp))
                q = T - 3
                if runs(i, q, NT):
                    e.wait_ge(EF.sem, EF.at("o", (i * 8, q - 1)))
                    for kt in range(2):
                        e.wait_ge(ED.sem, ED.at(f"t{kt}", (i * 8, q)))
                        AE.took(f"w{kt}", e.activation(PT[:, kt], bk[5 + kt], ACT.Copy))
                q = T - 4
                if runs(i, q, NT):
                    e.wait_ge(EF.sem, EF.at("o", (i * 8, q)))
                    AG.took("hi", e.activation(o_tiles(x1h, i, q), o_bank(q), ACT.Copy))
            piped(e, step, NT, 6)

        def wo_scalar(e):
            def body(t, j):
                act_split(e, U_O + j + 2, t)
                act_x(e, 4, 5, t * 4 + j, "mlp1", x0h)
            turns(e, 8, body)

        def wo_vector(e):
            def body(t, j):
                dve_split(e, U_O + j + 2, t)
                m = t * 4 + j
                b = evac_start(e, U_O, j, t)
                e.tensor_tensor(tile(h, m), tile(h, m), one(b), ALU.add).then_inc(bank_free, 1)
                e.wait_ge(bank_free, after(U_O, j, t, 5))
                e.sem_inc(h_ready, 1)
                dve_x(e, 5, m, "mlp1", x0h, x0l)
            turns(e, 8, body)

        def wo_tensor(e):
            def there(k):
                return DH.sem, DH.at("lo", 4 * (k // 2) + 3)
            turns(e, 8, lambda t, j: pe_unit(e, U_O, j, t, x1h, x1l, there if j == 0 else None))

        def final1_scalar(e):
            act_norm(e, 6, eps6)
            more_x_scalar(e, 7, 7, "a_norm", x1h)

        def final1_vector(e):
            dve_norm(e, 6)
            with e.Fori(0, KT) as m:
                e.scalar_tensor_tensor(tile(h, m), tile(h, m), Vd("final", m), one(R[:, :]), ALU.mult, ALU.mult).then_inc(h_ready, 1)
                e.wait_ge(h_ready, m + 57)
                dve_x(e, 7, m, "a_norm", x1h, x1l)

        def final1_tensor(e):
            pe_norm(e, 6)

        NC_, HEADS, HG, HP = 4, 32, 4, 64
        at = [kept]
        at = [own]
        T4 = own_buf("T4", [4, NC_, HEADS])
        G4 = own_buf("G4", [4, NC_, HG])
        zd = own_buf("zd", [NC_, HEADS]); az = own_buf("az", [NC_, HEADS]); s1 = own_buf("s1", [NC_, HEADS])
        s2_ = own_buf("s2_", [NC_, HEADS]); pq = own_buf("pq", [NC_, HEADS]); ea = own_buf("ea", [HEADS])
        dtr = own_buf("dtr", [TOK], lanes=HEADS)
        pre = own_buf("pre", [2, TOK + 3])
        cv = own_buf("cv", [2, TOK])
        at[0] = (at[0] + 31) // 32 * 32
        xt = own_buf("xt", [4, TOK])
        bct = own_buf("bct", [4, TOK])
        zs = own_buf("zs", [4, TOK])
        xdt = own_buf("xdt", [NC_, HG, HP]); xw = own_buf("xw", [NC_, HG, HP])
        btok = own_buf("btok", [NC_, LANES]); cbm = own_buf("cbm", [NC_, LANES])
        dec = own_buf("dec", [2, HG, LANES]); ecs = own_buf("ecs", [2, HG, LANES]); cs = own_buf("cs", [2, HG, LANES])
        state = own_buf("state", [HG, HP])
        uu = own_buf("uu", [2, TOK])
        usq = put("usq", [LANES, 2, TOK], at=acc_at)
        dts, dtx, dtt, dta = (sem(n) for n in ("dt_turned", "dt_exp", "dt_cumulated", "dt_act"))
        DM1 = Steps(sem("dt_steps"), "raw z az den r s s2 p17 p15 p13 p11 p9 p7 p5 p3 l mz dt adt nacs dif")

        def dt_scalar(e):
            act_norm(e, 7, eps5)
            act_split(e, U_DT + 2, 0)
            e.activation(ea[:, :], V("a_log"), ACT.Exp)
            e.wait_ge(DM1.sem, DM1.at("az"))
            e.activation(s1[:, :, :], az[:, :, :], ACT.Exp, scale=-1.0).then_inc(dtx, 1)
            e.wait_ge(DM1.sem, DM1.at("dif"))
            e.activation(T4[:, 3], zd[:, :, :], ACT.Exp).then_inc(dta, 1)

        def dt_vector(e):
            tt, ts, stt = e.tensor_tensor, e.tensor_scalar, e.scalar_tensor_tensor
            d = lambda name, ins: DM1.took(name, ins)
            n = lambda: DM1.next(e)
            DM1.open(e)
            dve_norm(e, 7)
            dve_split(e, U_DT + 2, 0)
            b = evac_start(e, U_DT, 0, 0)
            d("raw", tt(dtr[:, :], bank[U_DT % 4][0:HEADS, :], R[0:HEADS, :], ALU.mult))
            n()
            e.sem_inc(bank_free, 1)
            for t in (pre,):
                e.memset(t[:, :, 0:3], 0.0)
            e.wait_ge(dts, 1)
            full = [LANES, NC_, HEADS]
            n(); d("z", tt(zd[:, :, :], bank[5][:, 0:128].rearrange("p (c h) -> p c h", c=NC_), V("dt_bias").unsqueeze(1).to_broadcast(full), ALU.add))
            n(); d("az", stt(az[:, :, :], zd[:, :, :], -1.0, zd[:, :, :], ALU.mult, ALU.max))
            e.wait_ge(dtx, 1)
            n(); d("den", ts(pq[:, :, :], s1[:, :, :], 2.0, None, ALU.add))
            n(); d("r", e.reciprocal(pq[:, :, :], pq[:, :, :]))
            n(); d("s", tt(s1[:, :, :], s1[:, :, :], pq[:, :, :], ALU.mult))
            n(); d("s2", tt(s2_[:, :, :], s1[:, :, :], s1[:, :, :], ALU.mult))
            n(); d("p17", ts(pq[:, :, :], s2_[:, :, :], 1 / 17, None, ALU.mult))
            for k in (15, 13, 11, 9, 7, 5, 3):
                n(); d(f"p{k}", stt(pq[:, :, :], pq[:, :, :], 1 / k, s2_[:, :, :], ALU.add, ALU.mult))
            n(); d("l", stt(pq[:, :, :], pq[:, :, :], 1.0, s1[:, :, :], ALU.add, ALU.mult))
            n(); d("mz", ts(zd[:, :, :], zd[:, :, :], 0.0, None, ALU.max))
            n(); d("dt", stt(T4[:, 0], pq[:, :, :], 2.0, zd[:, :, :], ALU.mult, ALU.add))
            n(); d("adt", stt(T4[:, 1], T4[:, 0], -1.0, ea[:, :].unsqueeze(1).to_broadcast(full), ALU.mult, ALU.mult))
            e.wait_ge(dtt, 1)
            cum = bank[6][:, 0:128].rearrange("p (c h) -> p c h", c=NC_)
            end = bank[6][:, 128:256].rearrange("p (c h) -> p c h", c=NC_)
            n(); d("nacs", ts(T4[:, 2], cum, -1.0, None, ALU.mult))
            n(); d("dif", tt(zd[:, :, :], end, T4[:, 2], ALU.add))

        def dt_tensor(e):
            pe_norm(e, 7)
            pe_unit(e, U_DT, 0, 0, x1h, x1l, ready(x_ready, 56))
            e.wait_ge(DM1.sem, DM1.at("raw"))
            for c in range(NC_):
                last = e.transpose(bank[5][:, c * HEADS:(c + 1) * HEADS], dtr[:, c * LANES:(c + 1) * LANES], C("ident", hi=HEADS, rows=HEADS))
            last.then_inc(dts, 1)
            e.wait_ge(DM1.sem, DM1.at("adt"))
            adt = T4[:, 1].rearrange("p c h -> p (c h)")
            e.matmul(bank[6][:, 0:128], C("tri"), adt, start=True, stop=True)
            e.matmul(bank[6][:, 128:256], C("ones"), adt, start=True, stop=True).then_inc(dtt, 1)

        conv, silued = sem("conv"), sem("silued")
        SE = Steps(sem("ssd_tensor"), "tx0 tx1 tb cb a0 a1 y0 n0 a2 y1 n1 a3 y2 n2 y3 sum")
        SD = Steps(sem("ssd_vector"), "xd0 xd1 cbm g0 M0 S0 g1 M1 Sm1 S1 g2 M2 Sm2 S2 g3 M3 ud0 uz0 ud1 uz1 rg yg0 lo0 yg1 lo1")
        SA = Steps(sem("ssd_scalar"), "bt e0 x0 e1 x1 e2 x2 e3 x3 q0 q1 sg hi0 hi1")
        SP = Steps(sem("ssd_pool"), "G xw c1 c2 c3")

        def mamba_units(j):
            return ("x", j) if j < 4 else ("bc", j - 4) if j < 8 else ("z", j - 8)

        def in_scalar(e, hf, pr):
            n4 = hf * 8 + pr * 3
            turn = hf * 2 + pr
            for j in range(12):
                act_split(e, U_MAMBA + j + 2, n4)
                kind, i = mamba_units(j)
                if kind == "z":
                    e.wait_ge(bank_free, after(U_MAMBA, j, n4, 5))
                    e.activation(zs[:, i], t32[:, :] if i % 2 == 0 else a32[:, :], ACT.Silu).then_inc(silued, 1)
                else:
                    e.wait_ge(conv, turn * 32 + 4 * j + 4)
                    dst = xt[:, i] if kind == "x" else bct[:, i]
                    e.activation(dst, cv[:, j % 2], ACT.Silu).then_inc(silued, 1)

        def in_vector(e, hf, pr):
            n4 = hf * 8 + pr * 3
            turn = hf * 2 + pr
            for j in range(12):
                dve_split(e, U_MAMBA + j + 2, n4)
                kind, i = mamba_units(j)
                b = evac_start(e, U_MAMBA, j, n4)
                if kind == "z":
                    e.tensor_tensor(t32[:, :] if i % 2 == 0 else a32[:, :], b, R[:, :], ALU.mult).then_inc(bank_free, 1)
                    if i >= 1:
                        e.wait_ge(silued, turn * 12 + j)
                    continue
                z = j % 2
                e.tensor_tensor(pre[:, z, 3:], b, R[:, :], ALU.mult).then_inc(bank_free, 1)
                if kind == "x":
                    ct = hf * 8 + pr * 4 + i
                else:
                    ct = hf * 4 + pr * 2 + (16 + 8 * (i // 2) + i % 2)
                w = lambda k: par[:, bass.ds(ct + (PC["conv_w"][0] + 32 * k), 1)]
                e.wait_ge(bank_free, after(U_MAMBA, j, n4, 5))
                if j >= 2:
                    e.wait_ge(silued, turn * 12 + (j - 1))
                e.tensor_scalar(cv[:, z], pre[:, z, 3:], w(3), par[:, bass.ds(ct + PC["conv_b"][0], 1)], ALU.mult, ALU.add).then_inc(conv, 1)
                for k in range(3):
                    e.wait_ge(conv, turn * 32 + (4 * j + 1 + k))
                    e.scalar_tensor_tensor(cv[:, z], pre[:, z, k:k + TOK], w(k), cv[:, z], ALU.mult, ALU.add).then_inc(conv, 1)

        def in_tensor(e, hf, pr):
            n4 = hf * 8 + pr * 3
            for j in range(12):
                pe_unit(e, U_MAMBA, j, n4, x1h, x1l)

        def ssd_tensor(e, t, gl):
            n = lambda name: None
            e.wait_ge(silued, t[2])
            for c2 in range(2):
                e.wait_ge(SD.sem, SD.before("rg" if c2 else "S2", t[:2]))
                for c in (2 * c2, 2 * c2 + 1):
                    for i in range(2):
                        last = e.transpose(bank[5 + c2][:, (c % 2) * 256 + i * 128:(c % 2) * 256 + (i + 1) * 128], xt[:, 2 * gl + i, c * LANES:(c + 1) * LANES], C("ident"))
                SE.took(f"tx{c2}", last)
            e.wait_ge(SA.sem, SA.before("bt", t[:2]))
            for c in range(NC_):
                last = e.transpose(bank[7][:, c * LANES:(c + 1) * LANES], bct[:, gl, c * LANES:(c + 1) * LANES], C("ident"))
            SE.took("tb", last)
            e.wait_ge(SD.sem, SD.before("cbm", t[:2]))
            for c in range(NC_):
                cc = slice(c * LANES, (c + 1) * LANES)
                last = e.matmul(bank[4][:, cc], bct[:, gl, cc], bct[:, 2 + gl, cc], start=True, stop=True)
            SE.took("cb", last)
            e.wait_ge(SP.sem, SP.at("G", t[:2]))

            def cums(c):
                if c >= 2:
                    e.wait_ge(SD.sem, SD.at(f"g{c - 2}", t[:2]))
                    e.wait_ge(SA.sem, SA.at(f"x{c - 2}", t[:2]))
                for r in range(HG):
                    last = e.matmul(bank[c % 2][:, r * LANES:(r + 1) * LANES], G4[:, 1, c, r:r + 1].to_broadcast([LANES, LANES]), C("tri"), start=True, stop=True)
                SE.took(f"a{c}", last)

            def outs(c):
                e.wait_ge(SD.sem, SD.at(f"M{c}", t[:2]))
                if c == 0:
                    e.wait_ge(SD.sem, SD.before("uz1", t[:2]))
                else:
                    e.wait_ge(SD.sem, SD.at(f"S{c - 1}", t[:2]))
                    e.wait_ge(SP.sem, SP.at(f"c{c}", t[:2]))
                for r in range(HG):
                    o = bank[2 + r // 2][(r % 2) * HP:(r % 2 + 1) * HP, c * LANES:(c + 1) * LANES]
                    last = e.matmul(o, xdt[:, c, r], dec[:, c % 2, r], start=True, stop=(c == 0))
                    if c:
                        last = e.matmul(o, state[:, r], cs[:, c % 2, r], start=False, stop=True)
                SE.took(f"y{c}", last)

            def news(c):
                if c == 0:
                    e.wait_ge(SP.sem, SP.at("xw", t[:2]))
                    e.wait_ge(SA.sem, SA.at("bt", t[:2]))
                    e.wait_ge(SD.sem, SD.at("xd1", t[:2]))
                else:
                    e.wait_ge(SD.sem, SD.at(f"S{c - 1}", t[:2]))
                SE.took(f"n{c}", e.matmul(bank[5][:, 0:256], btok[:, c], xw[:, c].rearrange("p r w -> p (r w)"), start=True, stop=True))

            cums(0); cums(1)
            outs(0); news(0); cums(2)
            outs(1); news(1); cums(3)
            outs(2); news(2)
            outs(3)
            e.wait_ge(SA.sem, SA.at("q1", t[:2]))
            e.matmul(bk[6], C("ones"), usq[:, 0], start=True, stop=False)
            SE.took("sum", e.matmul(bk[6], C("ones"), usq[:, 1], start=False, stop=True))

        def ssd_vector(e, t, gl, o_tile, dtile):
            tt, ts, stt = e.tensor_tensor, e.tensor_scalar, e.scalar_tensor_tensor
            T = t[:2]
            n = lambda: SD.next(e, T)
            e.wait_ge(SP.sem, SP.at("G", T))
            e.wait_ge(SE.sem, SE.before("y3", T))
            for c2 in range(2):
                e.wait_ge(SE.sem, SE.at(f"tx{c2}", T))
                if c2 == 0:
                    e.wait_ge(SP.sem, SP.before("xw", T))
                SD.took(f"xd{c2}", tt(xdt[:, 2 * c2:2 * c2 + 2], bank[5 + c2][:, :].rearrange("p (c r w) -> p c r w", c=2, r=HG),
                                     G4[:, 0, 2 * c2:2 * c2 + 2].unsqueeze(3).to_broadcast([LANES, 2, HG, HP]), ALU.mult))
            e.wait_ge(SE.sem, SE.at("cb", T))
            SD.took("cbm", tt(cbm[:, :, :], bk[4].rearrange("p (c l) -> p c l", c=NC_), C("tri").unsqueeze(1).to_broadcast([LANES, NC_, LANES]), ALU.mult))
            for c in range(NC_):
                z = c % 2
                e.wait_ge(SE.sem, SE.at(f"a{c}", T))
                if c >= 2:
                    e.wait_ge(SE.sem, SE.at(f"y{c - 2}", T))
                for r in range(HG):
                    last = ts(dec[:, z, r], bank[z][:, r * LANES:(r + 1) * LANES], G4[:, 2, c, r:r + 1], 0.0, ALU.add, ALU.min)
                SD.took(f"g{c}", last)
                e.wait_ge(SA.sem, SA.at(f"e{c}", T))
                n(); SD.took(f"M{c}", tt(dec[:, z], dec[:, z], cbm[:, c].unsqueeze(1).to_broadcast([LANES, HG, LANES]), ALU.mult))
                if c == NC_ - 1:
                    continue
                e.wait_ge(SE.sem, SE.at(f"n{c}", T))
                new = bank[5][:, 0:256].rearrange("p (r w) -> p r w", r=HG)
                if c == 0:
                    SD.took("S0", e.tensor_copy(state[:, :, :], new))
                else:
                    e.wait_ge(SE.sem, SE.at(f"y{c}", T))
                    e.wait_ge(SA.sem, SA.at(f"x{c}", T))
                    n(); SD.took(f"Sm{c}", tt(state[:, :, :], state[:, :, :], ecs[:, z, :, LANES - 1:].to_broadcast([LANES, HG, HP]), ALU.mult))
                    n(); SD.took(f"S{c}", tt(state[:, :, :], state[:, :, :], new, ALU.add))
            e.wait_ge(SE.sem, SE.at("y3", T))
            for i in range(2):
                dsk = par[:, bass.ds(dtile + (PC["d_skip"][0] + i), 1)]
                if i == 0:
                    e.wait_ge(SA.sem, SA.before("q1", T))
                n(); SD.took(f"ud{i}", stt(uu[:, i], xt[:, 2 * gl + i], dsk, bk[2 + i], ALU.mult, ALU.add))
                n(); SD.took(f"uz{i}", tt(uu[:, i], uu[:, i], zs[:, 2 * gl + i], ALU.mult))
            e.wait_ge(SA.sem, SA.at("sg", T))
            n(); SD.took("rg", e.reciprocal(sd[:, :], sd[:, :]))
            for i in range(2):
                gg = par[:, bass.ds(dtile + (PC["gate_g"][0] + i), 1)]
                n(); SD.took(f"yg{i}", stt(uu[:, i], uu[:, i], gg, sd[:, :], ALU.mult, ALU.mult))
                e.wait_ge(SA.sem, SA.at(f"hi{i}", T))
                SD.took(f"lo{i}", tt(tile(x0l, o_tile + i), uu[:, i:i + 1], tile(x0h, o_tile + i).bitcast(F32), ALU.subtract))

        def ssd_scalar(e, t, gl, o_tile):
            T = t[:2]
            e.wait_ge(SE.sem, SE.at("tb", T))
            SA.took("bt", e.activation(btok[:, :, :], bk[7].rearrange("p (c n) -> p c n", c=NC_), ACT.Copy))
            for c in range(NC_):
                z = c % 2
                e.wait_ge(SD.sem, SD.at(f"g{c}", T))
                SA.took(f"e{c}", e.activation(dec[:, z], dec[:, z], ACT.Exp))
                if c >= 2:
                    e.wait_ge(SP.sem, SP.at(f"c{c - 2}", T) if c > 2 else SP.at("xw", T))
                    if c == 3:
                        e.wait_ge(SD.sem, SD.at("S1", T))
                else:
                    e.wait_ge(SP.sem, SP.before(f"c{c + 2}" if c == 0 else "c3", T))
                SA.took(f"x{c}", e.activation(ecs[:, z], bk[z].rearrange("p (r l) -> p r l", r=HG), ACT.Exp))
            for i in range(2):
                e.wait_ge(SD.sem, SD.at(f"uz{i}", T))
                SA.took(f"q{i}", e.activation(usq[:, i], uu[:, i], ACT.Square))
            e.wait_ge(SE.sem, SE.at("sum", T))
            SA.took("sg", e.activation(sd[:, :], bk[6], ACT.Sqrt, bias=eps5[:, :], scale=1.0 / 256))
            for i in range(2):
                e.wait_ge(SD.sem, SD.at(f"yg{i}", T))
                SA.took(f"hi{i}", e.activation(tile(x0h, o_tile + i), uu[:, i:i + 1], ACT.Copy))

        def ssd_pool(e, t, gl, g):
            T = t[:2]
            e.wait_ge(SE.sem, SE.before("a3", T))
            e.wait_ge(SD.sem, SD.before("g3", T))
            SP.next(e, T).took("G", e.tensor_copy(G4[:, :, :, :], T4[:, :, :, bass.ds(g * 4, 4)]))
            e.wait_ge(SE.sem, SE.before("n2", T))
            e.wait_ge(SD.sem, SD.at("xd1", T))
            SP.next(e, T).took("xw", e.tensor_tensor(xw[:, :, :, :], xdt[:, :, :, :], G4[:, 3].unsqueeze(3).to_broadcast([LANES, NC_, HG, HP]), ALU.mult))
            for c in (1, 2, 3):
                e.wait_ge(SA.sem, SA.at(f"x{c}", T))
                e.wait_ge(SE.sem, SE.at(f"y{c - 2}", T) if c == 3 else SE.before("y3", T))
                ccol = bct[:, 2 + gl, c * LANES:(c + 1) * LANES].unsqueeze(1).to_broadcast([LANES, HG, LANES])
                SP.next(e, T).took(f"c{c}", e.tensor_tensor(cs[:, c % 2], ccol, ecs[:, c % 2], ALU.mult))

        def mamba(e, units, ssd, out):
            with e.Fori(0, 2) as hf:
                with e.Fori(0, 2) as pr:
                    if units:
                        units(e, hf, pr)
                    for gl in range(2):
                        ssd(e, (hf * 4 + pr * 2, gl, hf * 24 + pr * 12 + 12), gl, hf, pr)
                if out:
                    out(e, hf)

        def mamba_tensor(e):
            SE.open(e)

            def out(e, hf):
                def there(k):
                    return SD.sem, SD.at(f"lo{k % 2}", (hf * 4, k // 2))
                turns(e, 8, lambda t, j: pe_unit(e, U_MAMBA + 24, j, hf * 8 + t, x0h, x0l, there if j == 0 else None))
            mamba(e, in_tensor, lambda e, t, gl, hf, pr: ssd_tensor(e, t, gl), out)

        def mamba_vector(e):
            SD.open(e)

            def out(e, hf):
                def body(t, j):
                    dve_split(e, U_MAMBA + 24 + j + 2, hf * 8 + t)
                    b = evac_start(e, U_MAMBA + 24, j, hf * 8 + t)
                    m = t * 4 + j
                    e.tensor_tensor(tile(h, m), tile(h, m), one(b), ALU.add).then_inc(bank_free, 1)
                turns(e, 8, body)
            mamba(e, in_vector, lambda e, t, gl, hf, pr: ssd_vector(e, t, gl, pr * 4 + 2 * gl, hf * 8 + pr * 4 + 2 * gl), out)
            e.wait_ge(bank_free, U_KV2 + 4)
            e.sem_inc(h_ready, 8)
            more_x_vector(e, 8, "kv2", x1h, x1l)
            more_x_vector(e, 9, "b_norm", x0h, x0l)

        def mamba_scalar(e):
            SA.open(e)
            mamba(e, in_scalar, lambda e, t, gl, hf, pr: ssd_scalar(e, t, gl, pr * 4 + 2 * gl),
                  lambda e, hf: turns(e, 8, lambda t, j: act_split(e, U_MAMBA + 24 + j + 2, hf * 8 + t)))
            more_x_scalar(e, 8, 8, "kv2", x1h)
            more_x_scalar(e, 8, 9, "b_norm", x0h)

        def mamba_pool(e):
            SP.open(e)
            e.wait_ge(dta, 1)
            e.wait_ge(DM1.sem, DM1.at("dif"))
            mamba(e, None, lambda e, t, gl, hf, pr: ssd_pool(e, t, gl, hf * 4 + pr * 2 + gl), None)

        DH_, LAMBDA_INIT = 8, 0.8 - 0.6 * math.exp(-0.3)
        at = [own]
        K2 = own_buf("K2", [DH_, TOK])
        V2tok = own_buf("V2tok", [4, DM])
        q2 = own_buf("q2", [DH_, TOK])
        gate = own_buf("gate", [DH_, TOK])
        v32 = own_buf("v32", [2, TOK])
        lprod, lsum, lexp = own_buf("lprod", [2, 64]), own_buf("lsum", [2]), own_buf("lexp", [2])
        nlam, sub_gl = own_buf("nlam", [1]), own_buf("sub_gl", [1])
        s2t = {n: own_buf("s2t_" + n, [4, 2]) for n in "mx nm sm rc".split()}
        at = [x0_at]
        Q2s = own_buf("Q2s", [2, TOK])
        K2s = own_buf("K2s", [2, TOK])
        V2s = own_buf("V2s", [2, 4, LANES])
        S2 = own_buf("S2", [4, 2, TOK])
        W2T = own_buf("W2T", [2, TOK])
        O32 = put("O32", [LANES, 2, TOK], at=acc_at)
        assert at[0] <= x0_at + 32768
        VT2 = Steps(sem("v2_turned"), "t", ahead=2)
        VK2 = Steps(sem("v2_kept"), "k", ahead=2)
        GS2 = Steps(sem("gate_silu"), "g", ahead=2)
        LM = Steps(sem("lambda_steps"), "pr sum nlam0 nlam sub")
        lam_exp = sem("lambda_exp")

        def kv2_scalar(e):
            act_norm(e, 8, eps5)
            e.wait_ge(LM.sem, LM.at("sum"))
            e.activation(lexp[:, :], lsum[:, :], ACT.Exp).then_inc(lam_exp, 1)
            VK2.open(e)
            turns(e, 8, lambda t, j: act_split(e, U_KV2 + j + 2, t))

            def keep(t, j):
                T = (t * 4, j)
                e.wait_ge(VT2.sem, VT2.at("t", T))
                VK2.took("k", e.activation(V2tok[:, :, bass.ds(t * LANES * 4 + j * LANES, LANES)], bk[5 + j % 2].rearrange("p (c n) -> p c n", c=4), ACT.Copy))

            def body(t, j):
                act_split(e, U_KV2 + 8 + j + 2, t)
                if j:
                    keep(t, j - 1)
                if j == 3:
                    keep(t, 3)
            turns(e, 8, body)

        def kv2_vector(e):
            dve_norm(e, 8)
            LM.open(e)
            l4 = V("lam_qk").rearrange("p (a b d) -> p a b d", a=2, b=2)
            LM.took("pr", e.tensor_tensor(lprod[:, :, :], l4[:, :, 0], l4[:, :, 1], ALU.mult))
            LM.next(e).took("sum", e.reduce_sum(lsum[:, :].unsqueeze(2), lprod[:, :, :], axis=AX.X))
            e.wait_ge(lam_exp, 1)
            LM.next(e).took("nlam0", e.tensor_tensor(nlam[:, :], lexp[:, 1:2], lexp[:, 0:1], ALU.subtract))
            LM.next(e).took("nlam", e.tensor_scalar(nlam[:, :], nlam[:, :], -LAMBDA_INIT, None, ALU.add))
            LM.next(e).took("sub", e.tensor_scalar(sub_gl[:, :], V("sub_g"), 1.0 - LAMBDA_INIT, None, ALU.mult))

            def k_body(t, j):
                dve_split(e, U_KV2 + j + 2, t)
                b = evac_start(e, U_KV2, j, t)
                e.tensor_tensor(tile(K2, t * 4 + j), one(b), one(R[:, :]), ALU.mult).then_inc(bank_free, 1)
            turns(e, 8, k_body)

            def v_body(t, j):
                dve_split(e, U_KV2 + 8 + j + 2, t)
                b = evac_start(e, U_KV2 + 8, j, t)
                e.wait_ge(VT2.sem, VT2.at("t", (t * 4, j - 2)))
                e.tensor_tensor(v32[:, j % 2], b, R[:, :], ALU.mult).then_inc(bank_free, 1)
            turns(e, 8, v_body)

        def kv2_tensor(e):
            VT2.open(e)
            pe_norm(e, 8)
            turns(e, 8, lambda t, j: pe_unit(e, U_KV2, j, t, x1h, x1l, ready(x_ready, 64) if j == 0 else None))

            def turn(t, j):
                e.wait_ge(bank_free, after(U_KV2 + 8, j, t, 5))
                e.wait_ge(VK2.sem, VK2.at("k", (t * 4, j - 2)))
                for c in range(4):
                    last = e.transpose(bank[5 + j % 2][:, c * LANES:(c + 1) * LANES], v32[:, j % 2, c * LANES:(c + 1) * LANES], C("ident"))
                VT2.took("t", last)

            def body(t, j):
                pe_unit(e, U_KV2 + 8, j, t, x1h, x1l)
                if j:
                    turn(t, j - 1)
                if j == 3:
                    turn(t, 3)
            turns(e, 8, body)

        def qg2_scalar(e):
            GS2.open(e)
            turns(e, 8, lambda t, j: act_split(e, U_QG2 + j + 2, t))

            def body(t, j):
                act_split(e, U_QG2 + 8 + j + 2, t)
                e.wait_ge(bank_free, after(U_QG2 + 8, j, t, 5))
                GS2.took("g", e.activation(tile(gate, t * 4 + j), one((a32 if j % 2 else t32)[:, :]), ACT.Silu))
            turns(e, 8, body)

        def qg2_vector(e):
            def q_body(t, j):
                dve_split(e, U_QG2 + j + 2, t)
                b = evac_start(e, U_QG2, j, t)
                e.scalar_tensor_tensor(tile(q2, t * 4 + j), one(b), 0.125, one(R[:, :]), ALU.mult, ALU.mult).then_inc(bank_free, 1)
            turns(e, 8, q_body)

            def g_body(t, j):
                dve_split(e, U_QG2 + 8 + j + 2, t)
                b = evac_start(e, U_QG2 + 8, j, t)
                e.wait_ge(GS2.sem, GS2.at("g", (t * 4, j - 2)))
                e.tensor_tensor((a32 if j % 2 else t32)[:, :], b, R[:, :], ALU.mult).then_inc(bank_free, 1)
            turns(e, 8, g_body)

        def qg2_tensor(e):
            turns(e, 16, lambda t, j: pe_unit(e, U_QG2, j, t, x0h, x0l, ready(x_ready, 72) if j == 0 else None))

        DT = 4 * DH_
        FP = Steps(sem("diff_copies"), "K Q V")
        FM = Steps(sem("diff_max"), "m0 m1 max neg", ahead=8)
        FE = Steps(sem("diff_exp"), "e0 e1", ahead=8)
        FW = Steps(sem("diff_weights"), "rec lrec w0 w1", ahead=8)
        FS = Steps(sem("diff_scores"), "s", ahead=8)
        FT = Steps(sem("diff_turned"), "t", ahead=8)
        FC = Steps(sem("diff_kept"), "w", ahead=8)
        FO = Steps(sem("diff_out"), "o", ahead=8)
        FK = Steps(sem("diff_out_kept"), "k", ahead=8)
        HA = Steps(sem("head_scalar"), "sq sd hi", ahead=4)
        HD = Steps(sem("head_vector"), "rc y yg lo", ahead=4)
        HE = Steps(sem("head_sum"), "sum", ahead=4)

        def diff_pool(e):
            FP.open(e)
            e.wait_ge(unit_done, U_O2)
            e.wait_ge(bank_free, U_O2 + 4)
            e.wait_ge(VK2.sem, VK2.at("k", 7))
            with e.Fori(0, DH_ // 2) as i:
                for x in range(2):
                    e.wait_ge(FS.sem, FS.at("s", (i * 8, 4 * x - 5)))
                    FP.next(e, (i * 2, x)).took("K", e.tensor_copy(K2s[:, x:x + 1], tile(K2, i * 2 + x)))
                    FP.next(e, (i * 2, x)).took("Q", e.tensor_copy(Q2s[:, x:x + 1], tile(q2, i * 2 + x)))
                    e.wait_ge(FO.sem, FO.at("o", (i * 8, 4 * x - 5)))
                    FP.next(e, (i * 2, x)).took("V", e.tensor_copy(V2s[:, x], V2tok[:, :, bass.ds(i * (2 * LANES) + x * LANES, LANES)]))

        def ended(i, T, lag):
            q = T - lag
            return (i * 2, q // 4) if q % 4 == 3 and runs(i, q, DT) else None

        def diff_tensor(e):
            for s in (FS, FT, FO, HE):
                s.open(e)

            def step(i, T):
                if runs(i, T, DT):
                    x, n, b = T // 4, T % 4, 2 * (T % 2)
                    if n == 0:
                        e.wait_ge(FP.sem, FP.at("Q", (i * 2, x)))
                    e.wait_ge(FM.sem, FM.at("m1", (i * 8, T - 2)))
                    for s in range(2):
                        last = e.matmul(bank[b + s][:, 0:LANES * (n + 1)], Q2s[64 * s:64 * s + 64, x, n * LANES:(n + 1) * LANES],
                                        K2s[64 * s:64 * s + 64, x, 0:LANES * (n + 1)], start=True, stop=True)
                    FS.took("s", last)
                q = T - 3
                if runs(i, q, DT):
                    n = q % 4
                    e.wait_ge(FW.sem, FW.at("w1", (i * 8, q)))
                    e.wait_ge(FC.sem, FC.at("w", (i * 8, q - 2)))
                    for c in range(n + 1):
                        last = e.transpose(bank[5 + q % 2][:, c * LANES:(c + 1) * LANES], S2[:, q % 4, 0, c * LANES:(c + 1) * LANES], C("ident"))
                    FT.took("t", last)
                q = T - 4
                if runs(i, q, DT):
                    x, n = q % 8 // 4, q % 4
                    if n == 0:
                        e.wait_ge(FP.sem, FP.at("V", (i * 2, q // 4)))
                    e.wait_ge(FC.sem, FC.at("w", (i * 8, q)))
                    e.wait_ge(FK.sem, FK.at("k", (i * 8, q - 1)))
                    for c in range(n + 1):
                        last = e.matmul(bank[7][:, n * LANES:(n + 1) * LANES], V2s[:, x, c], W2T[:, q % 2, c * LANES:(c + 1) * LANES], start=(c == 0), stop=(c == n))
                    FO.took("o", last)
                H = ended(i, T, 5)
                if H:
                    e.wait_ge(HA.sem, HA.at("sq", H))
                    HE.took("sum", e.matmul(bk[4], C("ones"), t32[:, :], start=True, stop=True))
            piped(e, step, DT, 8)

        def diff_vector(e):
            for s in (FM, FW, HD):
                s.open(e)

            def step(i, T):
                if runs(i, T, DT):
                    x, n, b, z = T // 4, T % 4, 2 * (T % 2), T % 4
                    t, N = (i * 8, T), LANES * (T % 4 + 1)
                    e.wait_ge(FS.sem, FS.at("s", t))
                    e.wait_ge(FT.sem, FT.at("t", (i * 8, T - 4)))
                    s0 = CC["slope"][0] + x
                    slope = const[:, s0:s0 + 1] if isinstance(i, int) and i == 0 else const[:, bass.ds(i * 2 + s0, 1)]
                    for s in range(2):
                        FM.took(f"m{s}", e.scalar_tensor_tensor(S2[:, z, s, 0:N], C("dist", lo=TOK - N), slope, bank[b + s][:, 0:N], ALU.mult, ALU.add))
                    FM.next(e, t).took("max", e.reduce_max(s2t["mx"][:, z].unsqueeze(2), S2[:, z, :, 0:N], axis=AX.X))
                    FM.next(e, t).took("neg", e.tensor_scalar(s2t["nm"][:, z], s2t["mx"][:, z], -1.0, None, ALU.mult))
                q = T - 2
                if runs(i, q, DT):
                    t, z, N = (i * 8, q), q % 4, LANES * (q % 4 + 1)
                    e.wait_ge(FE.sem, FE.at("e1", t))
                    FW.next(e, t).took("rec", e.reciprocal(s2t["rc"][:, z], s2t["sm"][:, z]))
                    FW.next(e, t).took("lrec", e.tensor_tensor(s2t["rc"][:, z, 1:2], s2t["rc"][:, z, 1:2], nlam[:, :], ALU.mult))
                    FW.next(e, t).took("w0", e.tensor_scalar(S2[:, z, 0, 0:N], S2[:, z, 0, 0:N], s2t["rc"][:, z, 0:1], None, ALU.mult))
                    FW.next(e, t).took("w1", e.scalar_tensor_tensor(S2[:, z, 0, 0:N], S2[:, z, 1, 0:N], s2t["rc"][:, z, 1:2], S2[:, z, 0, 0:N], ALU.mult, ALU.add))
                H = ended(i, T, 7)
                if H:
                    y = H[1] % 2
                    e.wait_ge(HA.sem, HA.at("sd", H))
                    HD.next(e, H).took("rc", e.reciprocal(R[:, :], sd[:, :]))
                    e.wait_ge(FK.sem, FK.at("k", (i * 8, T - 7)))
                    HD.next(e, H).took("y", e.scalar_tensor_tensor(O32[:, y], O32[:, y], sub_gl[:, :], R[:, :], ALU.mult, ALU.mult))
                    HD.next(e, H).took("yg", e.tensor_tensor(O32[:, y:y + 1], O32[:, y:y + 1], tile(gate, i * 2 + H[1]), ALU.mult))
                H = ended(i, T, 8)
                if H:
                    y = H[1] % 2
                    e.wait_ge(HA.sem, HA.at("hi", H))
                    HD.took("lo", e.tensor_tensor(tile(x1l, i * 2 + H[1]), O32[:, y:y + 1], tile(x1h, i * 2 + H[1]).bitcast(F32), ALU.subtract))
            piped(e, step, DT, 8)

        def diff_scalar(e):
            for s in (FE, FC, FK, HA):
                s.open(e)

            def step(i, T):
                q = T - 1
                if runs(i, q, DT):
                    t, z, N = (i * 8, q), q % 4, LANES * (q % 4 + 1)
                    e.wait_ge(FM.sem, FM.at("neg", t))
                    e.wait_ge(FW.sem, FW.at("w1", (i * 8, q - 4)))
                    for s in range(2):
                        FE.took(f"e{s}", e.activation(S2[:, z, s, 0:N], S2[:, z, s, 0:N], ACT.Exp, bias=s2t["nm"][:, z, s:s + 1], accum_out=s2t["sm"][:, z, s:s + 1]))
                q = T - 3
                if runs(i, q, DT):
                    N = LANES * (q % 4 + 1)
                    e.wait_ge(FT.sem, FT.at("t", (i * 8, q)))
                    e.wait_ge(FO.sem, FO.at("o", (i * 8, q - 2)))
                    FC.took("w", e.activation(W2T[:, q % 2, 0:N], bank[5 + q % 2][:, 0:N], ACT.Copy))
                q = T - 4
                if runs(i, q, DT):
                    n = q % 4
                    e.wait_ge(FO.sem, FO.at("o", (i * 8, q)))
                    if n == 0:
                        e.wait_ge(HD.sem, HD.at("lo", (i * 2, q // 4 - 2)))
                    FK.took("k", e.activation(O32[:, q % 8 // 4, n * LANES:(n + 1) * LANES], bank[7][:, n * LANES:(n + 1) * LANES], ACT.Copy))
                H = ended(i, T, 8)
                if H:
                    e.wait_ge(HD.sem, HD.at("yg", H))
                    HA.took("hi", e.activation(tile(x1h, i * 2 + H[1]), O32[:, H[1] % 2:H[1] % 2 + 1], ACT.Copy))
                H = ended(i, T, 4)
                if H:
                    e.wait_ge(FK.sem, FK.at("k", (i * 8, T - 4)))
                    e.wait_ge(HE.sem, HE.at("sum", (H[0], H[1] - 1)))
                    HA.took("sq", e.activation(t32[:, :], O32[:, H[1] % 2], ACT.Square))
                H = ended(i, T, 6)
                if H:
                    e.wait_ge(HE.sem, HE.at("sum", H))
                    e.wait_ge(HD.sem, HD.at("rc", (H[0], H[1] - 1)))
                    HA.took("sd", e.activation(sd[:, :], bk[4], ACT.Sqrt, bias=eps5[:, :], scale=1.0 / LANES))
            piped(e, step, DT, 8)

        def wo2_scalar(e):
            for m in range(8):
                act_split(e, U_O2 + m + 2, 0)
            act_norm(e, 9, eps5)

        def wo2_vector(e):
            for m in range(8):
                dve_split(e, U_O2 + m + 2, 0)
                b = evac_start(e, U_O2, m, 0)
                e.tensor_tensor(h[:, m], h[:, m], b, ALU.add).then_inc(bank_free, 1)
                e.wait_ge(bank_free, U_O2 + m + 5)
                e.sem_inc(h_ready, 1)
            dve_norm(e, 9)
            with e.Fori(0, KT) as m:
                e.scalar_tensor_tensor(tile(h, m), tile(h, m), Vd("final2", m), one(R[:, :]), ALU.mult, ALU.mult).then_inc(h_ready, 1)

        def wo2_tensor(e):
            for m in range(8):
                pe_unit(e, U_O2, m, 0, x1h, x1l, (lambda k: (HD.sem, HD.at("lo", k))) if m == 0 else None)
            pe_norm(e, 9)

        def store(e):
            for m in range(KT):
                e.wait_ge(h_ready, 8 * 10 + m + 1)
                e.dma_start(a["out"][m * LANES:(m + 1) * LANES, :], h[:, m]).then_inc(stored, 16)
            e.wait_ge(stored, 16 * KT)

        mlp0, mlp1 = mlp_parts(0, 2, 1, 2, "ple0"), mlp_parts(1, 5, 5, 6, "ple1")
        ple0, ple1 = ple_parts(0, 3, 3, "kv"), ple_parts(1, 6, 7, None)
        block = ctx.enter_context(nc.Block())

        @block.sync
        def _(e):
            s5_loads(e)
            for i in range(2):
                e.dma_start(raw[:, i], a["w"][i]).then_inc(raw_loaded[i], 16)
            s5_sync(e)
            e.wait_ge(h_ready, 9)
            e.dma_start(p_in[:, :, :, :], a["pT"]).then_inc(p_loaded, 16)
            with e.Fori(1, PAIRS // 2) as i:
                for s in range(2):
                    e.wait_ge(w_split, i * 4 + (2 * s - 2))
                    e.dma_start(raw[:, s], a["w"][bass.ds(i * 2 + s, 1)].rearrange("o p a k m -> p (o a) k m")).then_inc(raw_loaded[s], 16)
            if PAIRS % 2:
              e.wait_ge(w_split, 2 * PAIRS - 4)
              e.dma_start(raw[:, 0], a["w"][PAIRS - 1]).then_inc(raw_loaded[0], 16)
            store(e)

        @block.gpsimd
        def _(e):
            s5_pool(e)
            for n in (1, 2, 3):
                pool_h(e, n)
            att_pool(e)
            e.wait_ge(h_ready, 33)
            for n in (4, 5, 6, 7):
                pool_h(e, n)
            mamba_pool(e)
            e.wait_ge(h_ready, 65)
            pool_h(e, 8)
            diff_pool(e)
            e.wait_ge(h_ready, 73)
            pool_h(e, 9)

        @block.scalar
        def _(e):
            act_split(e, 0, 0, True)
            act_split(e, 1, 0, True)
            s5_scalar(e)
            glu_scalar(e)
            mlp0[0](e)
            ple0[0](e)
            more_x_scalar(e, 3, 4, "mix1", x0h)
            kv_scalar(e)
            q_scalar(e)
            att_scalar(e)
            wo_scalar(e)
            mlp1[0](e)
            ple1[0](e)
            final1_scalar(e)
            dt_scalar(e)
            mamba_scalar(e)
            kv2_scalar(e)
            qg2_scalar(e)
            diff_scalar(e)
            wo2_scalar(e)

        @block.vector
        def _(e):
            e.sem_inc(bank_free, 4)
            dve_split(e, 0, 0)
            dve_split(e, 1, 0)
            s5_vector(e)
            glu_vector(e)
            mlp0[1](e)
            ple0[1](e)
            more_x_vector(e, 4, "mix1", x0h, x0l)
            kv_vector(e)
            q_vector(e)
            att_vector(e)
            wo_vector(e)
            mlp1[1](e)
            ple1[1](e)
            final1_vector(e)
            dt_vector(e)
            mamba_vector(e)
            kv2_vector(e)
            qg2_vector(e)
            diff_vector(e)
            wo2_vector(e)

        @block.tensor
        def _(e):
            s5_tensor(e)
            glu_tensor(e)
            mlp0[2](e)
            ple0[2](e)
            kv_tensor(e)
            q_tensor(e)
            att_tensor(e)
            wo_tensor(e)
            mlp1[2](e)
            ple1[2](e)
            final1_tensor(e)
            dt_tensor(e)
            mamba_tensor(e)
            kv2_tensor(e)
            qg2_tensor(e)
            diff_tensor(e)
            wo2_tensor(e)


def constants():
    f = np.float32
    c = {}
    eye = np.eye(128, dtype=f)
    c["ident"] = eye
    turn = np.zeros((128, 128), f)
    turn[64:, :64], turn[:64, 64:] = -np.eye(64), np.eye(64)
    c["turn"] = turn
    swap = np.zeros((128, 128), f)
    for base in (0, 64):
        for d in range(8):
            swap[base + d + 8, base + d] = -1
            swap[base + d, base + d + 8] = 1
    c["ropeswap"] = swap
    c["ones"] = np.ones((128, 128), f)
    k, q = np.arange(128)[:, None], np.arange(128)[None, :]
    c["tri"] = (k <= q).astype(f)
    sgn = np.where(np.arange(128) < 64, -1, 1).astype(f)[:, None]
    c["sgn"], c["nsgn"] = sgn, -sgn
    c["sel"] = (np.arange(128)[:, None] // 16 == np.arange(8)[None]).astype(f)
    c["cidx"] = np.tile(np.arange(64, dtype=f), (128, 1))
    c["cnz"] = np.tile((np.arange(64) > 0).astype(f), (128, 1))
    c["id16"] = np.pad(np.eye(16, dtype=f), ((0, 112), (0, 0)))
    inv = f(500000.0) ** (-np.arange(0, 16, 2, dtype=f) / f(16))
    ang = np.arange(512, dtype=f)[None] * inv[:, None]
    rc, rs = np.ones((64, 512), f), np.zeros((64, 512), f)
    rc[0:8] = rc[8:16] = np.cos(ang)
    rs[0:8] = rs[8:16] = np.sin(ang)
    c["rcos"], c["rsin"] = np.tile(rc, (2, 1)), np.tile(rs, (2, 1))
    qi, kj = np.arange(128)[:, None] + 128, np.arange(256)[None]
    c["band"] = np.where((kj <= qi) & (qi - kj < 128), 0, -1e30).astype(f)
    c["band0"] = np.where(kj < 128, f(-1e30), c["band"])
    qi, kj = np.arange(128)[:, None], np.arange(512)[None] - 384
    c["dist"] = np.where(kj // 64 <= qi // 64, np.abs(qi - kj), 1e30).astype(f)
    c["slope"] = np.tile(-f(2.0) ** (-f(8.0) * np.arange(1, 9, dtype=f) / f(8.0)), (128, 1))
    return np.ascontiguousarray(np.concatenate([c[n] for n, _ in CONSTS], axis=1).astype(f))


def lay_out(x, p, norm_mix, ssm_lambda_re, ssm_lambda_im, ssm_log_dt, ssm_b_re, ssm_b_im, ssm_c_re,
            ssm_c_im, ssm_d, ssm_w_glu, kv_norm, w_k, w_v, w_q, attn_sinks, w_o, norm_mlp, w_up, w_down,
            norm_ple, w_ple_gate, w_ple_proj, norm_final, a_norm_g_2, a_w_in_2, a_conv_w_2, a_conv_b_2,
            a_dt_bias_2, a_a_log_2, a_d_skip_2, a_gate_norm_g_2, a_w_out_2, kv_norm_g_2, w_kv_2,
            b_norm_g_2, b_w_in_2, b_lambda_2, b_sub_g_2, b_w_out_2, final_norm_g_2):
    f = np.float32
    units = []

    def unit(w, r0, c0):
        units.append(w[r0:r0 + DM, c0:c0 + 128].reshape(KT, 128, 128).transpose(1, 0, 2))

    def cols(w, n, c0=0, r0=0):
        for m in range(n):
            unit(w, r0, c0 + 128 * m)

    def ple(w):
        w = w.reshape(2, 128, 2, 4, 128)
        for j in range(2):
            units.append(w[:, :, j].transpose(1, 2, 0, 3).reshape(128, KT, 128))

    def mlp(i):
        for q in range(4):
            cols(w_up[i], 8, q * DM)
            cols(w_down[i], 8, 0, q * DM)

    for m in range(8):
        unit(ssm_w_glu[0], 0, DM + 128 * m)
        unit(ssm_w_glu[0], 0, 128 * m)
    mlp(0)
    ple(w_ple_proj[0])
    cols(w_ple_gate[0], 8)
    cols(w_k, 2)
    cols(w_v, 2)
    cols(w_q[0], 8)
    cols(w_o[0], 8)
    mlp(1)
    ple(w_ple_proj[1])
    cols(w_ple_gate[1], 8)
    win = a_w_in_2[0]
    units.append(np.pad(win[:, 6144:6176].reshape(KT, 128, 32).transpose(1, 0, 2), ((0, 0), (0, 0), (0, 96))))
    for half in range(2):
        for pair in range(2):
            g = 4 * half + 2 * pair
            cols(win, 4, 2048 + 256 * g)
            cols(win, 2, 4096 + 128 * g)
            cols(win, 2, 5120 + 128 * g)
            cols(win, 4, 256 * g)
        cols(a_w_out_2[0], 8, 0, half * DM)
    cols(w_kv_2, 16)
    cols(b_w_in_2[0], 16)
    cols(b_w_out_2[0], 8)
    assert len(units) == UNITS
    units.append(np.zeros((128, KT, 128), f))
    w = np.ascontiguousarray(np.stack(units).reshape(PAIRS, 2, 128, KT, 128).transpose(0, 2, 1, 3, 4))

    v = {}
    vec = lambda t: t.reshape(-1, 128).T
    gains = [norm_mix[0], norm_mix[1], norm_mlp[0], norm_mlp[1], norm_ple[0], norm_ple[1], kv_norm, norm_final,
             a_norm_g_2[0], kv_norm_g_2, b_norm_g_2[0], final_norm_g_2]
    for n, g in zip(GAINS, gains):
        v[n] = vec(g)
    over = lambda t: np.tile(t.reshape(1, -1), (128, 1))
    v["lam_re"] = np.tile(ssm_lambda_re[0].T, (2, 1))
    v["lam_im"] = np.tile(ssm_lambda_im[0].T, (2, 1))
    v["log_dt"] = over(ssm_log_dt[0])
    v["gain_u"] = np.tile(norm_mix[0].reshape(64, 16).T, (8, 1))
    v["d_h"] = np.pad(ssm_d[0].reshape(64, 16).T, ((0, 112), (0, 0)))
    v["conv_w"] = a_conv_w_2[0].reshape(4, 32, 128).transpose(2, 0, 1).reshape(128, 128)
    v["conv_b"] = vec(a_conv_b_2[0])
    v["d_skip"] = vec(np.repeat(a_d_skip_2[0], 64))
    v["gate_g"] = vec(a_gate_norm_g_2[0])
    v["sub_g"] = vec(b_sub_g_2[0])
    v["sinks"] = over(attn_sinks[0])
    v["dt_bias"] = over(a_dt_bias_2[0])
    v["a_log"] = over(a_a_log_2[0])
    v["lam_qk"] = over(b_lambda_2[0])
    par = np.concatenate([v[n] for n, _ in PARAMS], axis=1)

    B = np.stack([np.concatenate([ssm_b_re[0], ssm_b_im[0]], 1), np.concatenate([ssm_b_im[0], ssm_b_re[0]], 1)])
    Cc = np.stack([np.concatenate([ssm_c_re[0], ssm_c_im[0]], 2), np.concatenate([ssm_c_im[0], ssm_c_re[0]], 2)])
    out = {
        "w": w, "const": constants(), "par": par,
        "xT": x[0].T,
        "xu": x[0].reshape(64, 8, 64, 16).transpose(1, 3, 2, 0).reshape(128, 64, 64),
        "B": B.transpose(2, 0, 1, 3),
        "C": Cc.transpose(3, 0, 1, 2),
        "pT": p[:, 0].reshape(2, 512, 2, 128).transpose(3, 0, 2, 1),
    }
    return {k: np.ascontiguousarray(t) for k, t in out.items()}


def kernel(**inputs):
    import concourse.bacc as bacc
    from concourse.bass_utils import run_bass_kernel_spmd

    nc = bacc.Bacc("TRN2", target_bir_lowering=False, num_devices=1)
    arrays = {f"in_{n}_dram": t for n, t in lay_out(**inputs).items()}
    a = {n: nc.dram_tensor(f"in_{n}_dram", arrays[f"in_{n}_dram"].shape, F32, kind="ExternalInput").ap()
         for n in ("w", "const", "par", "xT", "xu", "B", "C", "pT")}
    a["out"] = nc.dram_tensor("out_dram", (DM, TOK), F32, kind="ExternalOutput").ap()
    program(nc, a)
    result = run_bass_kernel_spmd(nc, [arrays], core_ids=[0])
    return np.ascontiguousarray(result.results[0]["out_dram"].T).reshape(1, TOK, DM)
```

```python
import math
from contextlib import ExitStack
import numpy as np
import concourse.bass as bass
from concourse import mybir

F32 = mybir.dt.float32
F32R = mybir.dt.float32r
ACT = mybir.ActivationFunctionType
ALU = mybir.AluOpType
AX = mybir.AxisListType

LANES, TOK, DM = 128, 512, 1024
KT = DM // LANES
SG, SH, SN = 64, 16, 64
STEP = 8
NSTEP = TOK // STEP
GB = LANES // SH
NBLK = SG // GB
SIN_SCALE = 6.283185
PI_SAFE = 3.1415925
ROUND = 12582912.0
TWO_PI_HI, TWO_PI_LO = 6.28125, 2.0 * math.pi - 6.28125

CONSTS = [("ident", 128), ("turn", 128), ("ropeswap", 128), ("ones", 128), ("tri", 128), ("sgn", 1), ("nsgn", 1),
          ("sel", 8), ("cidx", 64), ("cnz", 64), ("id16", 16), ("rcos", 512), ("rsin", 512), ("band", 256), ("band0", 256), ("dist", 512), ("slope", 8)]
GAINS = ["mix0", "mix1", "mlp0", "mlp1", "ple0", "ple1", "kv", "final", "a_norm", "kv2", "b_norm", "final2"]
PARAMS = [(g, 8) for g in GAINS] + [("lam_re", 64), ("lam_im", 64), ("log_dt", 64), ("gain_u", 64), ("d_h", 64),
          ("conv_w", 128), ("conv_b", 32), ("d_skip", 16), ("gate_g", 16), ("sub_g", 1), ("sinks", 16),
          ("dt_bias", 32), ("a_log", 32), ("lam_qk", 256)]


def columns(table):
    at, n = {}, 0
    for name, w in table:
        at[name] = (n, n + w)
        n += w
    return at, n


CC, NCONST = columns(CONSTS)
PC, NPARAM = columns(PARAMS)

U_GLU, U_MLP0, U_P0, U_GATE0 = 0, 16, 80, 82
U_KV, U_Q, U_O, U_MLP1, U_P1, U_GATE1 = 90, 94, 102, 110, 174, 176
U_DT, U_MAMBA, U_KV2, U_QG2, U_O2 = 184, 185, 249, 265, 281
UNITS = 289
PAIRS = (UNITS + 1) // 2


class Steps:

    def __init__(self, sem, names, ahead=1):
        self.sem, self.names, self.ahead, self.here = sem, names.split(), ahead, 0

    def open(self, e):
        e.sem_inc(self.sem, self.ahead * len(self.names))

    def count(self, turn, more):
        n = len(self.names)
        loop, t = turn if isinstance(turn, tuple) else (0, turn) if isinstance(turn, int) else (turn, 0)
        more += (t + self.ahead) * n
        assert more >= 0
        return more if isinstance(loop, int) and loop == 0 else loop * n + more

    def at(self, name, turn=0):
        return self.count(turn, self.names.index(name) + 1)

    def before(self, name, turn):
        return self.at(name, turn) - len(self.names) if isinstance(turn, int) else self.count(turn, self.names.index(name) + 1 - len(self.names))

    def next(self, e, turn=0):
        e.wait_ge(self.sem, self.count(turn, self.here % len(self.names)))
        return self

    def took(self, name, ins):
        want = self.names[self.here % len(self.names)]
        assert want == name, (name, want)
        self.here += 1
        ins.then_inc(self.sem, 1)


def program(nc, a):
    ctx = ExitStack()
    with ctx:
        base = [(nc.sbuf_base + 255) // 256 * 256]

        def put(name, shape, dt=F32, at=None):
            size = int(np.prod(shape[1:])) * 4
            if at is None:
                at = base[0]
                base[0] += (size + 31) // 32 * 32
                assert base[0] <= nc.sbuf_usable_end, (name, base[0], nc.sbuf_usable_end)
            return nc.alloc_sbuf_tensor_at(name, shape, dt, offset=at)

        def sem(name):
            return ctx.enter_context(nc.semaphore(name))

        const = put("const", [LANES, NCONST])
        par = put("par", [LANES, NPARAM])
        h = put("h", [LANES, KT, TOK])
        raw = put("raw", [LANES, 2, 2, KT, LANES])
        w_hi = put("w_hi", [LANES, 2, KT, LANES], F32R)
        w_lo = put("w_lo", [LANES, 2, KT, LANES], F32R)
        x0_at = base[0]
        x0h = put("x0h", [LANES, KT, TOK], F32R)
        x0l = put("x0l", [LANES, KT, TOK], F32R)
        x1h = put("x1h", [LANES, KT, TOK], F32R)
        x1l = put("x1l", [LANES, KT, TOK], F32R)
        acc_at = base[0]
        acc = put("acc", [LANES, TOK])
        sq = put("sq", [LANES, TOK])
        sd = put("sd", [LANES, TOK])
        R = put("R", [LANES, TOK])
        t32_at = base[0]
        t32 = put("t32", [LANES, TOK])
        a32 = put("a32", [LANES, TOK])
        half_pi, eps6, eps5 = put("half_pi", [LANES, 1]), put("eps6", [LANES, 1]), put("eps5", [LANES, 1])
        between = put("between", [LANES, 2, 8])
        own = base[0]
        room = nc.sbuf_usable_end - own

        def C(name, lo=0, hi=None, rows=LANES):
            a0, a1 = CC[name]
            return const[0:rows, a0 + lo:(a1 if hi is None else a0 + hi)]

        def V(name, lo=0, hi=None, rows=LANES):
            a0, a1 = PC[name]
            return par[0:rows, a0 + lo:(a1 if hi is None else a0 + hi)]

        def Vd(name, i):
            if name == "final_a":
                return between[:, 0, i:i + 1] if isinstance(i, int) else between[:, 0, bass.ds(i, 1)]
            a0, a1 = PC[name]
            return par[:, a0 + i:a0 + i + 1] if isinstance(i, int) else par[:, bass.ds(i + a0, 1)]

        def tile(t, i):
            return t[:, i:i + 1] if isinstance(i, int) else t[:, bass.ds(i, 1)]

        def one(ap):
            return ap.rearrange("p (o n) -> p o n", o=1)

        bank = [ctx.enter_context(nc.psum_tensor(f"bank{i}", [LANES, TOK], F32)) for i in range(8)]
        bk = [b[:, :] for b in bank]

        par_loaded, h_loaded, const_loaded, bc_loaded = (sem(n) for n in ("par_loaded", "h_loaded", "const_loaded", "bc_loaded"))
        raw_loaded = [sem("raw_loaded_0"), sem("raw_loaded_1")]
        hi_split, w_split = sem("hi_split"), sem("w_split")
        unit_done, bank_free = sem("unit_done"), sem("bank_free")
        h_ready, x_hi, x_ready = sem("h_ready"), sem("x_hi"), sem("x_ready")
        squared, acc_ready, norm_mm, sd_ready, r_ready = (sem(n) for n in ("squared", "acc_ready", "norm_mm", "sd_ready", "r_ready"))
        stored = sem("stored")

        def after(u0, j, n4, more):
            return u0 + j + more + (n4 * 4)

        def pe_unit(e, u0, j, n4, xh, xl, first=None):
            b = bk[(u0 + j) % 4]
            w = (u0 + j) % 2
            e.wait_ge(w_split, after(u0, j, n4, 1))
            e.wait_ge(bank_free, after(u0, j, n4, 1))
            for k in range(KT):
                if first is not None:
                    e.wait_ge(*first(k))
                e.matmul(b, w_hi[:, w, k], xh[:, k], start=(k == 0), stop=False)
                e.matmul(b, w_hi[:, w, k], xl[:, k], start=False, stop=False)
                last = e.matmul(b, w_lo[:, w, k], xh[:, k], start=False, stop=(k == KT - 1))
            last.then_inc(unit_done, 1)

        def act_split(e, v0, n4, lead=False):
            if isinstance(n4, int) and v0 + 4 * n4 >= UNITS:
                return
            e.wait_ge(raw_loaded[(v0 // 2) % 2], n4 * 16 + (v0 // 4 + 1) * 16)
            if not lead:
                e.wait_ge(unit_done, n4 * 4 + (v0 - 1))
            e.activation(w_hi[:, v0 % 2], raw[:, (v0 // 2) % 2, v0 % 2], ACT.Copy).then_inc(hi_split, 1)

        def dve_split(e, v0, n4):
            if isinstance(n4, int) and v0 + 4 * n4 >= UNITS:
                return
            e.wait_ge(hi_split, n4 * 4 + (v0 + 1))
            e.tensor_tensor(w_lo[:, v0 % 2], raw[:, (v0 // 2) % 2, v0 % 2], w_hi[:, v0 % 2].bitcast(F32),
                            ALU.subtract).then_inc(w_split, 1)

        def evac_start(e, u0, j, n4):
            e.wait_ge(unit_done, after(u0, j, n4, 1))
            return bk[(u0 + j) % 4]

        def act_x(e, n, p, m, gain, xh):
            e.wait_ge(h_ready, m + (8 * n + 1))
            e.activation(tile(xh, m), tile(h, m), ACT.Copy, scale=Vd(gain, m)).then_inc(x_hi, 1)

        def dve_x(e, p, m, gain, xh, xl):
            e.wait_ge(x_hi, m + (8 * p + 1))
            e.scalar_tensor_tensor(tile(xl, m), tile(h, m), Vd(gain, m), tile(xh, m).bitcast(F32),
                                   ALU.mult, ALU.subtract).then_inc(x_ready, 1)

        def pool_start(e, n):
            if n:
                e.wait_ge(norm_mm, n)
                e.wait_ge(acc_ready, 8 * n)
            e.memset(acc[:, :], 0.0).then_inc(squared, 1)
            e.wait_ge(squared, 9 * n + 1)

        def pool_square(e, n, m):
            e.wait_ge(h_ready, m + (8 * n + 1))
            e.wait_ge(acc_ready, m + 8 * n)
            e.tensor_tensor(one(sq[:, :]), tile(h, m), tile(h, m), ALU.mult).then_inc(squared, 1)
            e.wait_ge(squared, m + (9 * n + 2))
            e.tensor_tensor(acc[:, :], acc[:, :], sq[:, :], ALU.add).then_inc(acc_ready, 1)

        def pe_norm(e, n):
            e.wait_ge(acc_ready, 8 * n + 8)
            e.matmul(bk[4], C("ones"), acc[:, :], start=True, stop=True).then_inc(norm_mm, 1)

        def act_norm(e, n, eps):
            e.wait_ge(norm_mm, n + 1)
            if n:
                e.wait_ge(r_ready, n)
            e.activation(sd[:, :], bk[4], ACT.Sqrt, bias=eps[:, :], scale=1.0 / DM).then_inc(sd_ready, 1)

        def dve_norm(e, n):
            e.wait_ge(sd_ready, n + 1)
            e.reciprocal(R[:, :], sd[:, :]).then_inc(r_ready, 1)
            e.wait_ge(r_ready, n + 1)

        def turns(e, n, body):
            if n == 4:
                for j in range(4):
                    body(0, j)
                return
            with e.Fori(0, n // 4) as i:
                for j in range(4):
                    body(i, j)

        at = [own]

        def own_buf(name, shape, dt=F32, lanes=LANES):
            at[0] = (at[0] + 31) // 32 * 32
            t = put(name, [lanes] + list(shape), dt, at=at[0])
            at[0] += int(np.prod(shape)) * 4
            assert at[0] <= nc.sbuf_usable_end, name
            return t

        B_st = own_buf("B_st", [2, SG, SH])
        C_st = own_buf("C_st", [2, SG, SH])
        psi = own_buf("psi", [SG])
        mag8 = own_buf("mag8", [SG])
        ru = own_buf("ru", [NSTEP])
        TA = own_buf("TA", [2, SG, STEP + 1])
        PB = own_buf("PB", [2, SG, STEP])
        sinb = own_buf("sinb", [2, GB, NSTEP])
        cosb = own_buf("cosb", [2, GB, NSTEP])
        Sx = own_buf("Sx", [2, GB, NSTEP])
        Zb = own_buf("Zb", [GB, NSTEP])
        D0 = own_buf("D0", [2, GB, NSTEP])
        Wb = own_buf("Wb", [GB, NSTEP])
        tA = own_buf("tA", [GB, NSTEP])
        Ksb = own_buf("Ksb", [2, GB, STEP, SH], lanes=SH)
        Ysb = own_buf("Ysb", [STEP, GB, SH], lanes=NSTEP)
        Tm = own_buf("Tm", [2, GB, STEP, SH])
        at = [x0_at + 32768]
        small = {n: own_buf("s5_" + n, [SG]) for n in
                 "dt lrdt th k phi aphi k8 phi8 mag sn cs den rden nr c1 c2 t3 cr ci s2r s2i s4r s4i".split()}
        AR = own_buf("AR", [2, SG, STEP])
        cmA = own_buf("cmA", [SG, STEP])
        cmB = own_buf("cmB", [SG, STEP])
        ru3 = own_buf("ru3", [NSTEP, STEP])
        at = [x0_at + 32768 + 16384 + 12288]
        DI = own_buf("DI", [SG, SH], lanes=SH)
        at = [x0_at]
        TB = own_buf("TB", [GB, STEP, SH])
        TBt = own_buf("TBt", [GB, STEP, SH])
        TC = own_buf("TC", [2, GB, STEP + 1, SH])
        TCt = own_buf("TCt", [GB, STEP + 1, SH])
        ST = own_buf("ST", [GB, LANES])
        Ub = own_buf("Ub", [2, GB, NSTEP])
        Ur = own_buf("Ur", [GB, NSTEP])
        assert at[0] <= x0_at + 32768
        grid = lambda t: t[:, :].rearrange("p (g c) -> p g c", g=GB)
        ang, kk, ff, absf, tB, g32 = grid(acc), grid(sq), grid(sd), grid(t32), grid(R), a32

        zeroed, dt_ready, phase_ready, trig_ready, tables_ready, ru_ready = (
            sem(n) for n in ("zeroed", "dt_ready", "phase_ready", "trig_ready", "tables_ready", "ru_ready"))
        vec_chain, u_loaded = sem("vec_chain"), sem("u_loaded")
        t_loaded = [sem("t_loaded_even"), sem("t_loaded_odd")]
        DB = Steps(sem("s5_in_tables"), "TB1 TB2 TB", ahead=4)
        DV = Steps(sem("s5_states"), "pr1 pr2 V Z po1 po2 W", ahead=4)
        DK = Steps(sem("s5_direct"), "Kd", ahead=4)
        AS = Steps(sem("s5_kept"), "ST1 ST2 K1 K2 Sx", ahead=4)
        AN = Steps(sem("s5_angles"), "absf sin cos", ahead=4)
        AY = Steps(sem("s5_y_kept"), "Y1 Y2", ahead=4)
        AX5 = Steps(sem("s5_gelu"), "g hi", ahead=4)
        EA = Steps(sem("s5_step_sums"), "ST1 ST2 K1 K2 S", ahead=4)
        EB = Steps(sem("s5_outputs"), "JS JZ Y1 Y2", ahead=4)
        DL = Steps(sem("s5_y_low"), "lo", ahead=4)
        ET = Steps(sem("s5_y_turned"), "YT", ahead=4)
        P5 = Steps(sem("s5_pool"), "ang D0 k f TC1 TC2 TC U1 U", ahead=4)
        chain = [0]

        def link(e, ins):
            chain[0] += 1
            ins.then_inc(vec_chain, 1)
            e.wait_ge(vec_chain, chain[0])

        def piped(e, step, total, drain, per=8):
            for T in range(per):
                step(0, T)
            with e.Fori(1, total // per) as i:
                for T in range(per):
                    step(i, T)
            for T in range(drain):
                step(total // per, T)

        def runs(i, q, total, per=8):
            return not isinstance(i, int) or 0 <= per * i + q < total

        def cut(t, i, q, width=GB, axis=1):
            d = slice((i * 2 + q) * width, (i * 2 + q + 1) * width) if isinstance(i, int) else bass.ds(i * (2 * width) + q * width, width)
            return t[:, d] if axis == 1 else t[:, :, d]

        def s5_loads(e):
            e.dma_start(par[:, :], a["par"]).then_inc(par_loaded, 16)
            e.dma_start(h[:, :, :], a["xT"].rearrange("(k p) n -> p k n", p=LANES)).then_inc(h_loaded, 16)
            e.dma_start(const[:, :], a["const"]).then_inc(const_loaded, 16)
            e.dma_start(B_st[:, :, :, :], a["B"]).then_inc(bc_loaded, 16)
            e.dma_start(C_st[:, :, :, :], a["C"]).then_inc(bc_loaded, 16)
            e.dma_start(Ur[:, :, :], a["xu"][:, 0:GB]).then_inc(u_loaded, 16)

        def s5_sync(e):
            for z in range(2):
                e.sem_inc(t_loaded[z], 16 * STEP)

            def block(i, q):
                if runs(i, q + 1, NBLK, 2):
                    e.wait_ge(P5.sem, P5.at("U1", (i * 2, q)))
                    e.dma_start(Ur[:, :, :], cut(a["xu"], i, q + 1)).then_inc(u_loaded, 16)
                e.wait_ge(DK.sem, DK.at("Kd", (i * 2, q)))
                for s in range(STEP):
                    e.dma_start(Tm[s * SH:(s + 1) * SH, q, :, s:STEP, :],
                                Ksb[:, q, :, 0:STEP - s, :]).then_inc(t_loaded[q], 16)
            with e.Fori(0, NBLK // 2 - 1) as i:
                for q in range(2):
                    block(i, q)
            for q in range(2):
                block(NBLK // 2 - 1, q)

        def s5_pool(e):
            e.memset(Tm[:, :, :, :, :], 0.0).then_inc(zeroed, 1)
            P5.open(e)
            e.wait_ge(h_loaded, 16)
            e.sem_inc(h_ready, 8)
            pool_start(e, 0)
            for m in range(KT):
                pool_square(e, 0, m)
            e.wait_ge(const_loaded, 16)
            e.wait_ge(bc_loaded, 32)
            e.wait_ge(tables_ready, 1)
            e.wait_ge(ru_ready, 1)
            full = [LANES, GB, NSTEP]
            f4 = [LANES, GB, STEP + 1, SH]
            tt = e.tensor_tensor
            with e.Fori(0, NBLK // 2) as i:
                for q in range(2):
                    t = (i * 2, q)
                    P5.next(e, t).took("ang", tt(ang, cut(psi, i, q).unsqueeze(2).to_broadcast(full), C("cidx").unsqueeze(1).to_broadcast(full), ALU.mult))
                    e.wait_ge(DV.sem, DV.at("Z", (i * 2, q - 2)))
                    e.wait_ge(P5.sem, P5.at("ang", t))
                    P5.took("D0", tt(D0[:, q], cut(mag8, i, q).unsqueeze(2).to_broadcast(full), C("cnz").unsqueeze(1).to_broadcast(full), ALU.mult))
                    P5.took("k", e.tensor_scalar(kk, ang, ROUND, ROUND, ALU.add, ALU.subtract))
                    e.wait_ge(P5.sem, P5.at("k", t))
                    e.wait_ge(AN.sem, AN.at("sin", (i * 2, q - 1)))
                    P5.took("f", tt(ff, ang, kk, ALU.subtract))
                    e.wait_ge(EB.sem, EB.at("Y2", (i * 2, q - 2)))
                    P5.took("TC1", tt(TC[:, q], cut(C_st[:, 0], i, q).unsqueeze(2).to_broadcast(f4), cut(TA[:, 0], i, q).unsqueeze(3).to_broadcast(f4), ALU.mult))
                    P5.next(e, t).took("TC2", tt(TCt[:, :, :, :], cut(C_st[:, 1], i, q).unsqueeze(2).to_broadcast(f4), cut(TA[:, 1], i, q).unsqueeze(3).to_broadcast(f4), ALU.mult))
                    P5.next(e, t).took("TC", tt(TC[:, q], TC[:, q], TCt[:, :, :, :], ALU.add))
                    e.wait_ge(u_loaded, i * 32 + (16 * q + 16))
                    P5.took("U1", tt(Ub[:, q], Ur[:, :, :], cut(V("gain_u"), i, q).unsqueeze(2).to_broadcast(full), ALU.mult))
                    P5.next(e, t).took("U", tt(Ub[:, q], Ub[:, q], ru[:, :].unsqueeze(1).to_broadcast(full), ALU.mult))

        def s5_scalar(e):
            s = small
            e.wait_ge(par_loaded, 16)
            e.activation(s["dt"][:, :], V("log_dt"), ACT.Exp).then_inc(dt_ready, 1)
            e.wait_ge(phase_ready, 1)
            e.activation(s["mag"][:, :], s["lrdt"][:, :], ACT.Exp)
            e.activation(mag8[:, :], s["lrdt"][:, :], ACT.Exp, scale=8.0)
            e.activation(s["sn"][:, :], s["phi"][:, :], ACT.Sin)
            e.activation(s["cs"][:, :], s["aphi"][:, :], ACT.Sin, bias=half_pi[:, :], scale=-1.0).then_inc(trig_ready, 1)
            act_split(e, 0, 0, True)
            act_split(e, 1, 0, True)
            act_norm(e, 0, eps6)

            def step(i, T):
                if runs(i, T, NBLK, 2):
                    q, t = T, (i * 2, T)
                    e.wait_ge(P5.sem, P5.at("f", t))
                    e.wait_ge(AN.sem, AN.at("cos", (i * 2, q - 1)))
                    AN.took("absf", e.activation(absf, ff, ACT.Abs))
                    e.wait_ge(DV.sem, DV.at("po2", (i * 2, q - 2)))
                    AN.took("sin", e.activation(sinb[:, q], ff, ACT.Sin, scale=SIN_SCALE))
                    e.wait_ge(AN.sem, AN.at("absf", t))
                    AN.took("cos", e.activation(cosb[:, q], absf, ACT.Sin, bias=half_pi[:, :], scale=-SIN_SCALE))
                    e.wait_ge(EA.sem, EA.at("S", (i * 2, q - 1)))
                    for k in (1, 2):
                        e.wait_ge(EA.sem, EA.at(f"ST{k}", t))
                        AS.took(f"ST{k}", e.activation(ST[:, 4 * k - 4:4 * k, :], bk[k - 1].rearrange("p (g n) -> p g n", g=4), ACT.Copy))
                    e.wait_ge(t_loaded[q], i * (16 * STEP) + 16 * STEP)
                    for k in (1, 2):
                        e.wait_ge(EA.sem, EA.at(f"K{k}", t))
                        AS.took(f"K{k}", e.activation(Ksb[:, q, 4 * k - 4:4 * k, :, :], bank[4 + k][0:SH, :].rearrange("p (g s h) -> p g s h", g=4, s=STEP), ACT.Copy))
                    e.wait_ge(EA.sem, EA.at("S", t))
                    e.wait_ge(EB.sem, EB.at("JS", (i * 2, q - 2)))
                    AS.took("Sx", e.activation(Sx[:, q], grid(bank[2]), ACT.Copy))
                q = T - 2
                if runs(i, q, NBLK, 2):
                    t = (i * 2, q)
                    e.wait_ge(ET.sem, ET.at("YT", t))
                    e.wait_ge(DL.sem, DL.at("lo", (i * 2, q - 1)))
                    tok = bk[7].rearrange("p (s c) -> p s c", s=STEP)
                    AX5.took("g", e.activation(g32[:, :].rearrange("p (c s) -> p s c", s=STEP), tok, ACT.Gelu_apprx_tanh))
                    AX5.took("hi", e.activation(cut(x1h, i, q, 1).rearrange("p o (c s) -> p (o s) c", s=STEP), tok, ACT.Gelu_apprx_tanh))
                q = T - 1
                if runs(i, q, NBLK, 2):
                    e.wait_ge(ET.sem, ET.at("YT", (i * 2, q - 1)))
                    for k in (1, 2):
                        e.wait_ge(EB.sem, EB.at(f"Y{k}", (i * 2, q)))
                        AY.took(f"Y{k}", e.activation(Ysb[:, :, 4 * k - 4:4 * k, :].rearrange("p s g h -> p g s h"), ybank(k)[0:NSTEP, :].rearrange("p (g s h) -> p g s h", g=4, s=STEP), ACT.Copy))
            for s_ in (AS, AN, AY, AX5):
                s_.open(e)
            piped(e, step, NBLK, 2, 2)
            e.sem_inc(x_hi, 8)

        def ybank(k):
            return bank[4 if k == 1 else 2]

        def s5_vector(e):
            s = small
            v = lambda n: s[n][:, :]
            e.memset(half_pi[:, :], math.pi / 2)
            e.memset(eps6[:, :], 1e-6)
            e.memset(eps5[:, :], 1e-5)
            e.memset(Wb[:, :, 0:1], 0.0).then_inc(zeroed, 1)
            for s_ in (DB, DV, DK, DL):
                s_.open(e)
            e.wait_ge(par_loaded, 16)
            e.wait_ge(dt_ready, 1)
            tt, ts = e.tensor_tensor, e.tensor_scalar
            link(e, tt(between[:, 0], V("final"), V("a_norm"), ALU.mult))
            link(e, tt(between[:, 1], V("final"), V("final"), ALU.mult))
            link(e, tt(v("lrdt"), V("lam_re"), v("dt"), ALU.mult))
            link(e, tt(v("th"), V("lam_im"), v("dt"), ALU.mult))

            def reduced(out, x, k):
                link(e, ts(v(k), v(x), 1.0 / (2 * math.pi), ROUND, ALU.mult, ALU.add))
                link(e, ts(v(k), v(k), ROUND, None, ALU.subtract))
                link(e, e.scalar_tensor_tensor(v(out), v(k), -TWO_PI_HI, v(x), ALU.mult, ALU.add))
                link(e, e.scalar_tensor_tensor(v(out), v(k), -TWO_PI_LO, v(out), ALU.mult, ALU.add))

            reduced("phi", "th", "k")
            link(e, ts(v("th"), v("phi"), 8.0, None, ALU.mult))
            link(e, ts(v("phi"), v("phi"), PI_SAFE, -PI_SAFE, ALU.min, ALU.max))
            link(e, e.scalar_tensor_tensor(v("aphi"), v("phi"), -1.0, v("phi"), ALU.mult, ALU.max))
            e.sem_inc(phase_ready, 1)
            reduced("phi8", "th", "k8")
            link(e, ts(psi[:, :], v("phi8"), 1.0 / (2 * math.pi), None, ALU.mult))
            e.wait_ge(trig_ready, 1)
            ar, ai = TA[:, 0, :, 1], TA[:, 1, :, 1]
            e.memset(TA[:, 0, :, 0:1], 1.0)
            e.memset(TA[:, 1, :, 0:1], 0.0)
            e.memset(AR[:, 0, :, 7:8], 1.0)
            e.memset(AR[:, 1, :, 7:8], 0.0)
            link(e, tt(ar, v("mag"), v("cs"), ALU.mult))
            link(e, tt(ai, v("mag"), v("sn"), ALU.mult))
            link(e, tt(v("den"), V("lam_re"), V("lam_re"), ALU.mult))
            link(e, tt(v("t3"), V("lam_im"), V("lam_im"), ALU.mult))
            link(e, tt(v("den"), v("den"), v("t3"), ALU.add))
            link(e, e.reciprocal(v("rden"), v("den")))
            link(e, ts(v("nr"), ar, -1.0, None, ALU.add))
            link(e, tt(v("c1"), v("nr"), V("lam_re"), ALU.mult))
            link(e, tt(v("c2"), ai, V("lam_im"), ALU.mult))
            link(e, tt(v("c1"), v("c1"), v("c2"), ALU.add))
            link(e, tt(v("cr"), v("c1"), v("rden"), ALU.mult))
            link(e, tt(v("c1"), ai, V("lam_re"), ALU.mult))
            link(e, tt(v("c2"), v("nr"), V("lam_im"), ALU.mult))
            link(e, tt(v("c1"), v("c1"), v("c2"), ALU.subtract))
            link(e, tt(v("ci"), v("c1"), v("rden"), ALU.mult))

            def cmul(o, x, y, n):
                A, B = cmA[:, :, 0:n], cmB[:, :, 0:n]
                yr, yi = (q.unsqueeze(2).to_broadcast([LANES, SG, n]) for q in y)
                link(e, tt(A, x[0], yr, ALU.mult))
                link(e, tt(B, x[1], yi, ALU.mult))
                link(e, tt(o[0], A, B, ALU.subtract))
                link(e, tt(A, x[0], yi, ALU.mult))
                link(e, tt(B, x[1], yr, ALU.mult))
                link(e, tt(o[1], A, B, ALU.add))

            def cols(t, lo, hi):
                return t[:, 0, :, lo:hi], t[:, 1, :, lo:hi]

            a1 = (ar, ai)
            a2 = (v("s2r"), v("s2i"))
            a4 = (v("s4r"), v("s4i"))
            u2 = lambda q: tuple(x.unsqueeze(2) for x in q)
            cmul(u2(a2), u2(a1), a1, 1)
            cmul(u2(a4), u2(a2), a2, 1)
            cmul(cols(TA, 8, 9), u2(a4), a4, 1)
            cmul(cols(TA, 2, 4), cols(TA, 0, 2), a2, 2)
            cmul(cols(TA, 4, 8), cols(TA, 0, 4), a4, 4)
            link(e, e.tensor_copy(AR[:, :, :, 6:7], TA[:, :, :, 1:2]))
            cmul(cols(AR, 4, 6), cols(AR, 6, 8), a2, 2)
            cmul(cols(AR, 0, 4), cols(AR, 4, 8), a4, 4)
            cmul(cols(PB, 0, 8), cols(AR, 0, 8), (v("cr"), v("ci")), 8)
            f4 = [LANES, GB, STEP, SH]

            def tables(i, q):
                t = (i * 2, q)
                e.wait_ge(EA.sem, EA.at("K2", (i * 2, q - 1)))
                DB.took("TB1", tt(TB[:, :, :, :], cut(B_st[:, 0], i, q).unsqueeze(2).to_broadcast(f4), cut(PB[:, 0], i, q).unsqueeze(3).to_broadcast(f4), ALU.mult))
                DB.took("TB2", tt(TBt[:, :, :, :], cut(B_st[:, 1], i, q).unsqueeze(2).to_broadcast(f4), cut(PB[:, 1], i, q).unsqueeze(3).to_broadcast(f4), ALU.mult))
                DB.next(e, t).took("TB", tt(TB[:, :, :, :], TB[:, :, :, :], TBt[:, :, :, :], ALU.add))

            e.wait_ge(const_loaded, 16)
            link(e, ts(PB[:, 1], PB[:, 1], C("sgn"), None, ALU.mult))
            link(e, ts(TA[:, 0], TA[:, 0], C("nsgn"), None, ALU.mult))
            link(e, ts(TA[:, 1], TA[:, 1], -1.0, None, ALU.mult))
            dfull = [SH, SG, SH]
            link(e, tt(DI[:, :, :], V("d_h", rows=SH).unsqueeze(2).to_broadcast(dfull), C("id16", rows=SH).unsqueeze(1).to_broadcast(dfull), ALU.mult))
            e.sem_inc(tables_ready, 1)
            e.wait_ge(bc_loaded, 32)
            tables(0, 0)
            dve_norm(e, 0)
            rf = [LANES, NSTEP, STEP]
            link(e, tt(ru3[:, :, :], R[:, :].rearrange("p (c s) -> p c s", s=STEP), C("sel").unsqueeze(1).to_broadcast(rf), ALU.mult))
            e.reduce_sum(ru[:, :].unsqueeze(2), ru3[:, :, :], axis=AX.X).then_inc(ru_ready, 1)

            flat = lambda t: t.rearrange("p g c -> p (g c)")

            def step(i, T):
                q = T - 1
                if runs(i, q, NBLK, 2):
                    t, z = (i * 2, q), q % 2
                    n = lambda: DV.next(e, t)
                    e.wait_ge(AS.sem, AS.at("Sx", t))
                    DV.took("pr1", tt(tA[:, :, :], Sx[:, z], cosb[:, z], ALU.mult))
                    e.wait_ge(EB.sem, EB.at("JS", t))
                    DV.took("pr2", tt(tB, grid(bank[3]), sinb[:, z], ALU.mult))
                    n().took("V", tt(tA[:, :, :], tA[:, :, :], tB, ALU.subtract))
                    e.wait_ge(P5.sem, P5.at("D0", t))
                    n().took("Z", e.tensor_tensor_scan(flat(Zb[:, :, :]), flat(D0[:, z]), flat(tA[:, :, :]), 0.0, ALU.mult, ALU.add))
                    n().took("po1", tt(tA[:, :, :], Zb[:, :, :], cosb[:, z], ALU.mult))
                    e.wait_ge(EB.sem, EB.at("JZ", t))
                    DV.took("po2", tt(tB, grid(bank[3]), sinb[:, z], ALU.mult))
                    e.wait_ge(EB.sem, EB.at("Y2", (i * 2, q - 1)))
                    n().took("W", tt(Wb[:, :, 1:], tA[:, :, :NSTEP - 1], tB[:, :, :NSTEP - 1], ALU.add))
                if runs(i, T, NBLK, 2):
                    e.wait_ge(AS.sem, AS.at("K2", (i * 2, T)))
                    DK.took("Kd", tt(Ksb[:, T % 2, :, 0, :], Ksb[:, T % 2, :, 0, :], cut(DI, i, T), ALU.add))
                if runs(i, T + 1, NBLK, 2):
                    tables(i, T + 1)
                q = T - 2
                if runs(i, q, NBLK, 2):
                    e.wait_ge(AX5.sem, AX5.at("hi", (i * 2, q)))
                    DL.took("lo", e.tensor_tensor(cut(x1l, i, q, 1), one(g32[:, :]), cut(x1h, i, q, 1).bitcast(F32), ALU.subtract))
                    e.wait_ge(DL.sem, DL.at("lo", (i * 2, q)))
                    e.sem_inc(x_ready, 1)

            dve_split(e, 0, 0)
            dve_split(e, 1, 0)
            for q in range(2):
                step(0, q)
            with e.Fori(1, NBLK // 2 - 1) as i:
                for q in range(2):
                    step(i, q)
            for q in range(4):
                step(NBLK // 2 - 1, q)

        def s5_tensor(e):
            for s_ in (EA, EB, ET):
                s_.open(e)
            e.wait_ge(const_loaded, 16)
            pe_norm(e, 0)
            e.wait_ge(zeroed, 2)

            def step(i, T):
                q = T - 1
                if runs(i, q, NBLK, 2):
                    e.wait_ge(AS.sem, AS.at("Sx", (i * 2, q)))
                    e.wait_ge(DV.sem, DV.at("po2", (i * 2, q - 1)))
                    EB.took("JS", e.matmul(bk[3], C("turn"), Sx[:, q % 2].rearrange("p g c -> p (g c)"), start=True, stop=True))
                q = T - 2
                if runs(i, q, NBLK, 2):
                    e.wait_ge(AY.sem, AY.at("Y2", (i * 2, q)))
                    e.wait_ge(AX5.sem, AX5.at("hi", (i * 2, q - 1)))
                    for t in range(STEP):
                        turned = e.transpose if t else e.matmul
                        last = turned(bank[7][:, t * NSTEP:(t + 1) * NSTEP], Ysb[:, t].rearrange("p g h -> p (g h)"), C("ident", hi=NSTEP, rows=NSTEP))
                    ET.took("YT", last)
                if runs(i, T, NBLK, 2):
                    q, t = T, (i * 2, T)
                    z = q % 2
                    e.wait_ge(DB.sem, DB.at("TB", t))
                    for k in (1, 2):
                        e.wait_ge(AS.sem, AS.at(f"ST{k}", (i * 2, q - 1)))
                        for g in range(4):
                            last = e.transpose(bank[k - 1][:, g * LANES:(g + 1) * LANES], TB[:, 4 * k - 4 + g].rearrange("p s h -> p (s h)"), C("ident"))
                        EA.took(f"ST{k}", last)
                    e.wait_ge(P5.sem, P5.at("TC", t))
                    for k in (1, 2):
                        e.wait_ge(AS.sem, AS.at(f"K{k}", (i * 2, q - 1)))
                        for g in range(4):
                            gg = 4 * k - 4 + g
                            last = e.matmul(bank[4 + k][0:SH, g * LANES:(g + 1) * LANES], TB[:, gg, STEP - 1], TC[:, z, gg, 0:STEP].rearrange("p s h -> p (s h)"), start=True, stop=True)
                        EA.took(f"K{k}", last)
                    e.wait_ge(P5.sem, P5.at("U", t))
                    e.wait_ge(AS.sem, AS.at("ST2", t))
                    e.wait_ge(AY.sem, AY.at("Y2", (i * 2, q - 2)))
                    for g in range(GB):
                        last = e.matmul(bank[2][:, g * NSTEP:(g + 1) * NSTEP], ST[:, g], Ub[:, z, g], start=True, stop=True)
                    EA.took("S", last)
                q = T - 1
                if runs(i, q, NBLK, 2):
                    t, z = (i * 2, q), q % 2
                    e.wait_ge(DV.sem, DV.at("Z", t))
                    EB.took("JZ", e.matmul(bk[3], C("turn"), Zb[:, :, :].rearrange("p g c -> p (g c)"), start=True, stop=True))
                    e.wait_ge(DV.sem, DV.at("W", t))
                    e.wait_ge(t_loaded[z], i * (16 * STEP) + 16 * STEP * (2 + q // 2))
                    for k in (1, 2):
                        if k == 1:
                            e.wait_ge(AY.sem, AY.at("Y1", (i * 2, q - 1)))
                        elif runs(i, T, NBLK, 2):
                            e.wait_ge(AS.sem, AS.at("Sx", (i * 2, q + 1)))
                        for g in range(4):
                            gg = 4 * k - 4 + g
                            o = ybank(k)[0:NSTEP, g * LANES:(g + 1) * LANES]
                            e.matmul(o, Ub[:, z, gg], Tm[:, z, gg].rearrange("p s h -> p (s h)"), start=True, stop=False)
                            last = e.matmul(o, Wb[:, gg], TC[:, z, gg, 1:].rearrange("p s h -> p (s h)"), start=False, stop=True)
                        EB.took(f"Y{k}", last)
            piped(e, step, NBLK, 2, 2)

        sg = Zb[:, :, :].rearrange("p g c -> p (g c)")
        sg_ready = sem("sg_ready")

        def glu_scalar(e):
            def body(i, j):
                act_split(e, U_GLU + j + 2, i)
                if j % 2 == 0:
                    e.wait_ge(unit_done, after(U_GLU, j, i, 1))
                    e.wait_ge(bank_free, after(U_GLU, j, i, 4))
                    e.activation(sg, bk[(U_GLU + j) % 4], ACT.Sigmoid).then_inc(sg_ready, 1)
                else:
                    act_x(e, 1, 1, i * 2 + j // 2, "mlp0", x0h)
            turns(e, 16, body)

        def glu_vector(e):
            def body(i, j):
                dve_split(e, U_GLU + j + 2, i)
                m = i * 2 + j // 2
                if j % 2 == 0:
                    e.wait_ge(sg_ready, m + 1)
                    e.sem_inc(bank_free, 1)
                else:
                    b = evac_start(e, U_GLU, j, i)
                    e.tensor_tensor(t32[:, :], b, sg, ALU.mult).then_inc(bank_free, 1)
                    e.wait_ge(bank_free, after(U_GLU, j, i, 5))
                    e.tensor_tensor(tile(h, m), tile(h, m), one(t32[:, :]), ALU.add).then_inc(h_ready, 1)
                    e.wait_ge(h_ready, m + 9)
                    dve_x(e, 1, m, "mlp0", x0h, x0l)
            turns(e, 16, body)

        def ready(s, n):
            return lambda k: (s, n + (k + 1))

        def glu_tensor(e):
            turns(e, 16, lambda i, j: pe_unit(e, U_GLU, j, i, x1h, x1l, ready(x_ready, 0) if j == 0 else None))

        def pool_h(e, n, steps=KT):
            pool_start(e, n)
            with e.Fori(0, steps) as m:
                pool_square(e, n, m)

        a_hi, a_ready = sem("a_hi"), sem("a_ready")

        def mlp_parts(i, n, p_in, p_out, gain):
            u0 = (U_MLP0, U_MLP1)[i]
            a0 = 32 * i

            def up_scalar(e, q):
                def body(t, j):
                    act_split(e, u0 + j + 2, q * 4 + t)
                    m = t * 4 + j
                    e.wait_ge(bank_free, after(u0, j, q * 4 + t, 5))
                    e.activation(tile(x1h, m), one(t32[:, :]), ACT.Square).then_inc(a_hi, 1)
                    e.wait_ge(a_ready, q * 8 + m + (a0 + 1))
                    e.activation(a32[:, :], t32[:, :], ACT.Square).then_inc(a_hi, 1)
                turns(e, 8, body)

            def up_vector(e, q):
                def body(t, j):
                    dve_split(e, u0 + j + 2, q * 4 + t)
                    m = t * 4 + j
                    b = evac_start(e, u0, j, q * 4 + t)
                    e.scalar_tensor_tensor(t32[:, :], b, 0.0, R[:, :], ALU.max, ALU.mult).then_inc(bank_free, 1)
                    e.wait_ge(a_hi, (q * 8 + m) * 2 + (2 * a0 + 2))
                    e.tensor_tensor(tile(x1l, m), one(a32[:, :]), tile(x1h, m).bitcast(F32), ALU.subtract).then_inc(a_ready, 1)
                turns(e, 8, body)

            def up_tensor(e, q):
                turns(e, 8, lambda t, j: pe_unit(e, u0, j, q * 4 + t, x0h, x0l, ready(x_ready, 8 * p_in) if j == 0 else None))

            def down_scalar(e, q, final):
                def body(t, j):
                    act_split(e, u0 + 8 + j + 2, q * 4 + t)
                    if final:
                        act_x(e, n, p_out, t * 4 + j, gain, x0h)
                turns(e, 8, body)

            def down_vector(e, q, final):
                def body(t, j):
                    dve_split(e, u0 + 8 + j + 2, q * 4 + t)
                    m = t * 4 + j
                    b = evac_start(e, u0 + 8, j, q * 4 + t)
                    e.tensor_tensor(tile(h, m), tile(h, m), one(b), ALU.add).then_inc(bank_free, 1)
                    if final:
                        e.wait_ge(bank_free, after(u0 + 8, j, q * 4 + t, 5))
                        e.sem_inc(h_ready, 1)
                        dve_x(e, p_out, m, gain, x0h, x0l)
                turns(e, 8, body)

            def down_tensor(e, q):
                turns(e, 8, lambda t, j: pe_unit(e, u0 + 8, j, q * 4 + t, x1h, x1l, (lambda k: (a_ready, q * 8 + (a0 + k + 2))) if j == 0 else None))

            def vector(e):
                if i == 0:
                    e.sem_inc(a_ready, 1)
                dve_norm(e, n - 1)
                with e.Fori(0, 3) as q:
                    up_vector(e, q)
                    down_vector(e, q, False)
                up_vector(e, 3)
                down_vector(e, 3, True)

            def scalar(e):
                act_norm(e, n - 1, eps6)
                with e.Fori(0, 3) as q:
                    up_scalar(e, q)
                    down_scalar(e, q, False)
                up_scalar(e, 3)
                down_scalar(e, 3, True)

            def tensor(e):
                pe_norm(e, n - 1)
                with e.Fori(0, 3) as q:
                    up_tensor(e, q)
                    down_tensor(e, q)
                up_tensor(e, 3)
                down_tensor(e, 3)

            return scalar, vector, tensor

        at = [own]
        p_in = own_buf("p_in", [2, 2, TOK])
        p_h, p_l = own_buf("p_h", [2, TOK], F32R), own_buf("p_l", [2, TOK], F32R)
        pp_at = at[0]
        Pp = own_buf("Pp", [KT, TOK])
        gs = own_buf("gs", [TOK])
        kept = at[0]
        p_loaded, p_hi, p_ready, p_mm, p_out = (sem(s) for s in ("p_loaded", "p_hi", "p_ready", "p_mm", "p_out"))

        def ple_parts(i, n, p_out_set, gain):
            up, u0 = (U_P0, U_P1)[i], (U_GATE0, U_GATE1)[i]

            def scalar(e):
                if i == 0:
                    e.wait_ge(p_loaded, 16)
                else:
                    e.wait_ge(unit_done, U_P1)
                e.activation(p_h[:, :, :], p_in[:, i], ACT.Copy).then_inc(p_hi, 1)
                for j in range(2):
                    act_split(e, up + j + 2, 0)
                    for mm in range(4):
                        t = 8 * i + 4 * j + mm
                        e.wait_ge(p_mm, t + 1)
                        e.activation(Pp[:, 4 * j + mm], bk[4 + mm], ACT.Copy).then_inc(p_out, 1)
                act_norm(e, n - 1, eps6)

                for m in range(8):
                    act_split(e, u0 + m + 2, 0)
                    e.wait_ge(bank_free, u0 + m + 5)
                    e.activation(gs[:, :], t32[:, :], ACT.Sigmoid).then_inc(sg_ready, 1)
                    if gain and m:
                        act_x(e, n, p_out_set, m - 1, gain, x1h)
                if gain:
                    act_x(e, n, p_out_set, 7, gain, x1h)

            def vector(e):
                e.wait_ge(p_hi, i + 1)
                e.tensor_tensor(p_l[:, :, :], p_in[:, i], p_h[:, :, :].bitcast(F32), ALU.subtract).then_inc(p_ready, 1)
                for j in range(2):
                    dve_split(e, up + j + 2, 0)
                    e.wait_ge(unit_done, up + j + 1)
                    e.sem_inc(bank_free, 1)
                dve_norm(e, n - 1)
                e.wait_ge(p_out, 8 * i + 8)

                for m in range(8):
                    dve_split(e, u0 + m + 2, 0)
                    b = evac_start(e, u0, m, 0)
                    e.tensor_tensor(t32[:, :], b, R[:, :], ALU.mult).then_inc(bank_free, 1)
                    if gain and m:
                        dve_x(e, p_out_set, m - 1, gain, x1h, x1l)
                    e.wait_ge(sg_ready, m + (8 + 8 * i + 1))
                    e.tensor_tensor(one(a32[:, :]), one(gs[:, :]), tile(Pp, m), ALU.mult).then_inc(gated, 1)
                    e.wait_ge(gated, m + (8 * i + 1))
                    e.tensor_tensor(tile(h, m), tile(h, m), one(a32[:, :]), ALU.add).then_inc(h_ready, 1)
                if gain:
                    dve_x(e, p_out_set, 7, gain, x1h, x1l)

            def tensor(e):
                e.wait_ge(p_ready, i + 1)
                for j in range(2):
                    e.wait_ge(w_split, up + j + 1)
                    e.wait_ge(bank_free, up + j + 1)
                    for mm in range(4):
                        t = 8 * i + 4 * j + mm
                        if j:
                            e.wait_ge(p_out, t - 3)
                        w = (up + j) % 2
                        for k in range(2):
                            kk = 2 * mm + k
                            e.matmul(bk[4 + mm], w_hi[:, w, kk], p_h[:, k], start=(k == 0), stop=False)
                            e.matmul(bk[4 + mm], w_hi[:, w, kk], p_l[:, k], start=False, stop=False)
                            last = e.matmul(bk[4 + mm], w_lo[:, w, kk], p_h[:, k], start=False, stop=(k == 1))
                        last.then_inc(p_mm, 1)
                    e.wait_ge(p_mm, 8 * i + 4 * j + 4)
                    e.sem_inc(unit_done, 1)
                e.wait_ge(p_out, 8 * i + 8)
                pe_norm(e, n - 1)
                turns(e, 8, lambda t, j: pe_unit(e, u0, j, t, x0h, x0l, ready(x_ready, 8 * (p_out_set - 1)) if j == 0 else None))

            return scalar, vector, tensor

        gated = sem("gated")

        def more_x_scalar(e, n, p, gain, xh):
            with e.Fori(0, KT) as m:
                act_x(e, n, p, m, gain, xh)

        def more_x_vector(e, p, gain, xh, xl):
            with e.Fori(0, KT) as m:
                dve_x(e, p, m, gain, xh, xl)

        at = [kept]
        kdup = own_buf("kdup", [4, TOK])
        kv32 = own_buf("kv32", [4, TOK])
        v_tok = own_buf("v_tok", [4, 256])
        q32 = put("q32", [LANES, KT, TOK], at=pp_at)
        at = [x0_at]
        Ks = own_buf("Ks", [2, LANES + TOK])
        Qs = own_buf("Qs", [2, 2, TOK])
        Vs = own_buf("Vs", [2, 5, 64])
        Sm = own_buf("Sm", [4, 2, 2, 256])
        PT = put("PT", [LANES, 2, 512], at=acc_at)
        st = {n: own_buf("st_" + n, [4, 4]) for n in "mx nm df sm es rc".split()}
        assert at[0] <= x0_at + 32768
        rope_mm, kv_t, kv_tok, k_dup = sem("rope_mm"), sem("kv_t"), sem("kv_tok"), sem("k_dup")
        RO = Steps(sem("rope_steps"), "cos sin sum")

        def rope_tensor(e, u0, j, n4, src, turn):
            e.wait_ge(bank_free, after(u0, j, n4, 5))
            e.wait_ge(RO.sem, RO.at("sin", (turn[0], turn[1] - 2)))
            e.matmul(bk[5 + j % 2], C("ropeswap"), src, start=True, stop=True).then_inc(rope_mm, 1)

        def rope_vector(e, src, j, turn):
            RO.next(e, turn).took("cos", e.tensor_tensor(one(t32[:, :]), src, one(C("rcos")), ALU.mult))
            e.wait_ge(rope_mm, turn + 1 if isinstance(turn, int) else turn[0] + (turn[1] + 1))
            RO.next(e, turn).took("sin", e.tensor_tensor(a32[:, :], bk[5 + j % 2], C("rsin"), ALU.mult))
            RO.next(e, turn).took("sum", e.tensor_tensor(src, one(t32[:, :]), one(a32[:, :]), ALU.add))

        def kv_scalar(e):
            act_norm(e, 3, eps6)
            for j in range(4):
                act_split(e, U_KV + j + 2, 0)
                if j in (2, 3):
                    t = j - 2
                    e.wait_ge(RO.sem, RO.at("sum", t))
                    for half in range(2):
                        for to in range(2):
                            last = e.activation(kdup[64 * to:64 * to + 64, 2 * t + half], kv32[64 * half:64 * half + 64, t], ACT.Copy)
                            last.then_inc(k_dup, 1)
            for t in range(2):
                e.wait_ge(kv_t, t + 1)
                e.activation(v_tok[:, :, LANES * t:LANES * (t + 1)], bk[7 - 2 * t].rearrange("p (c n) -> p c n", c=4), ACT.Copy).then_inc(kv_tok, 1)

        def kv_vector(e):
            dve_norm(e, 3)
            RO.open(e)
            for j in range(4):
                dve_split(e, U_KV + j + 2, 0)
                b = evac_start(e, U_KV, j, 0)
                e.tensor_tensor(kv32[:, j], b, R[:, :], ALU.mult).then_inc(bank_free, 1)
                if j in (1, 2):
                    e.wait_ge(bank_free, U_KV + j + 4)
                    rope_vector(e, kv32[:, j - 1:j], j - 1, j - 1)

        def kv_tensor(e):
            pe_norm(e, 3)
            for j in range(4):
                pe_unit(e, U_KV, j, 0, x1h, x1l, ready(x_ready, 24) if j == 0 else None)
                if j in (1, 2):
                    e.wait_ge(bank_free, U_KV + j + 4)
                    e.matmul(bk[4 + j], C("ropeswap"), kv32[:, j - 1], start=True, stop=True).then_inc(rope_mm, 1)
            for t in range(2):
                e.wait_ge(bank_free, U_KV + 7 + t)
                if t:
                    e.wait_ge(RO.sem, RO.at("sin", 0))
                for c in range(4):
                    last = e.transpose(bank[7 - 2 * t][:, c * LANES:(c + 1) * LANES], kv32[:, 2 + t, c * LANES:(c + 1) * LANES], C("ident"))
                last.then_inc(kv_t, 1)

        def q_scalar(e):
            turns(e, 8, lambda t, j: act_split(e, U_Q + j + 2, t))

        def q_vector(e):
            def body(t, j):
                dve_split(e, U_Q + j + 2, t)
                m = t * 4 + j
                b = evac_start(e, U_Q, j, t)
                e.tensor_tensor(tile(q32, m), one(b), one(R[:, :]), ALU.mult).then_inc(bank_free, 1)
                if j:
                    e.wait_ge(bank_free, after(U_Q, j - 1, t, 5))
                    rope_vector(e, tile(q32, t * 4 + (j - 1)), j - 1, (t * 4, j + 1))
                if j == 3:
                    e.wait_ge(bank_free, after(U_Q, j, t, 5))
                    rope_vector(e, tile(q32, m), j, (t * 4, j + 2))
            turns(e, 8, body)

        def q_tensor(e):
            e.wait_ge(kv_tok, 2)

            def body(t, j):
                pe_unit(e, U_Q, j, t, x0h, x0l, ready(x_ready, 32) if j == 0 else None)
                m = t * 4 + j
                if j:
                    rope_tensor(e, U_Q, j - 1, t, tile(q32, t * 4 + (j - 1)), (t * 4, j + 1))
                if j == 3:
                    rope_tensor(e, U_Q, 3, t, tile(q32, m), (t * 4, j + 2))
            turns(e, 8, body)

        PKQ = Steps(sem("att_copies"), "K Q V")
        DA = Steps(sem("att_max"), "m0 m1 max sink neg dif", ahead=8)
        AB = Steps(sem("att_exp"), "e0 e1 e2 e3 es", ahead=8)
        DC = Steps(sem("att_scale"), "den rec scale", ahead=8)
        ES = Steps(sem("att_scores"), "s", ahead=8)
        ED = Steps(sem("att_turned"), "t0 t1", ahead=8)
        AE = Steps(sem("att_weights"), "w0 w1", ahead=8)
        EF = Steps(sem("att_out"), "o", ahead=8)
        AG = Steps(sem("att_out_hi"), "hi", ahead=8)
        DH = Steps(sem("att_out_lo"), "lo", ahead=8)
        pads = sem("pads")
        NT = 16

        def att_pool(e):
            PKQ.open(e)
            e.wait_ge(unit_done, U_O)
            for t, cut in ((Ks, Ks[:, :, 0:LANES]), (Vs, Vs[:, :, 0])):
                e.memset(cut, 0.0).then_inc(pads, 1)
            e.wait_ge(RO.sem, RO.at("sum", 9))
            e.wait_ge(k_dup, 8)
            e.wait_ge(kv_tok, 2)
            with e.Fori(0, 2) as i:
                for x in range(2):
                    kh = (i * 2, x)
                    e.wait_ge(ES.sem, ES.at("s", (i * 8, 4 * x - 5)))
                    PKQ.next(e, kh).took("K", e.tensor_copy(Ks[:, x:x + 1, LANES:], tile(kdup, i * 2 + x)))
                    PKQ.next(e, kh).took("Q", e.tensor_copy(Qs[:, x], q32[:, bass.ds(i * 4 + 2 * x, 2)]))
                    e.wait_ge(EF.sem, EF.at("o", (i * 8, 4 * x - 5)))
                    PKQ.next(e, kh).took("V", e.tensor_copy(Vs[:, x, 1:5], v_tok[:, :, bass.ds(i * 128 + 64 * x, 64)]))

        def att_tensor(e):
            for s in (ES, ED, EF):
                s.open(e)
            e.wait_ge(pads, 2)

            def step(i, T):
                if runs(i, T, NT):
                    x, n, b = T // 4, T % 4, 2 * (T % 2)
                    if n == 0:
                        e.wait_ge(PKQ.sem, PKQ.at("Q", (i * 2, x)))
                    e.wait_ge(DA.sem, DA.at("m1", (i * 8, T - 2)))
                    for g in range(4):
                        hf, gg = g % 2, g // 2
                        last = e.matmul(bank[b + hf][:, gg * 256:gg * 256 + 256], Qs[64 * hf:64 * hf + 64, x, gg, n * LANES:(n + 1) * LANES],
                                        Ks[64 * hf:64 * hf + 64, x, n * LANES:(n + 2) * LANES], start=True, stop=True)
                    ES.took("s", last)
                q = T - 3
                if runs(i, q, NT):
                    e.wait_ge(DC.sem, DC.at("scale", (i * 8, q)))
                    for kt in range(2):
                        e.wait_ge(AE.sem, AE.at(f"w{kt}", (i * 8, q - 1)))
                        for g in range(4):
                            last = e.transpose(bank[5 + kt][:, g * LANES:(g + 1) * LANES], Sm[:, q % 4, g // 2, g % 2, kt * LANES:(kt + 1) * LANES], C("ident"))
                        ED.took(f"t{kt}", last)
                q = T - 4
                if runs(i, q, NT):
                    x, n = q % 8 // 4, q % 4
                    if n == 0:
                        e.wait_ge(PKQ.sem, PKQ.at("V", (i * 2, q // 4)))
                    e.wait_ge(AE.sem, AE.at("w1", (i * 8, q)))
                    e.wait_ge(DH.sem, DH.at("lo", (i * 8, q - 2)))
                    for hf in range(2):
                        for kt in range(2):
                            last = e.matmul(bank[7 - 3 * (q % 2)][64 * hf:64 * hf + 64, 0:256], Vs[:, x, n + kt], PT[:, kt, hf * 256:hf * 256 + 256], start=(kt == 0), stop=(kt == 1))
                    EF.took("o", last)
            piped(e, step, NT, 6)

        def att_vector(e):
            for s in (DA, DC, DH):
                s.open(e)

            def step(i, T):
                if runs(i, T, NT):
                    b, z, t = 2 * (T % 2), T % 4, (i * 8, T)
                    e.wait_ge(ES.sem, ES.at("s", t))
                    e.wait_ge(ED.sem, ED.at("t1", (i * 8, T - 4)))
                    mask = C("band0" if T % 4 == 0 else "band").unsqueeze(1).to_broadcast([LANES, 2, 256])
                    for hf in range(2):
                        DA.took(f"m{hf}", e.scalar_tensor_tensor(Sm[:, z, hf], bank[b + hf][:, :].rearrange("p (g k) -> p g k", g=2), 0.125, mask, ALU.mult, ALU.add))
                    flat = Sm[:, z].rearrange("p a b k -> p (a b) k")
                    DA.next(e, t).took("max", e.reduce_max(st["mx"][:, z].unsqueeze(2), flat, axis=AX.X))
                    s0 = PC["sinks"][0]
                    sk = par[:, bass.ds(i * 8 + (s0 + 4 * (T // 4)), 4)].rearrange("p (g f) -> p f g", f=2)
                    v = lambda nm: st[nm][:, z].rearrange("p (f g) -> p f g", f=2)
                    DA.next(e, t).took("sink", e.tensor_tensor(v("mx"), v("mx"), sk, ALU.max))
                    DA.next(e, t).took("neg", e.tensor_scalar(st["nm"][:, z], st["mx"][:, z], -1.0, None, ALU.mult))
                    DA.next(e, t).took("dif", e.tensor_tensor(v("df"), sk, v("mx"), ALU.subtract))
                q = T - 2
                if runs(i, q, NT):
                    t, z = (i * 8, q), q % 4
                    e.wait_ge(AB.sem, AB.at("es", t))
                    DC.next(e, t).took("den", e.tensor_tensor(st["rc"][:, z], st["sm"][:, z], st["es"][:, z], ALU.add))
                    DC.next(e, t).took("rec", e.reciprocal(st["rc"][:, z], st["rc"][:, z]))
                    flat = Sm[:, z].rearrange("p a b k -> p (a b) k")
                    DC.next(e, t).took("scale", e.tensor_tensor(flat, flat, st["rc"][:, z].unsqueeze(2).to_broadcast([LANES, 4, 256]), ALU.mult))
                q = T - 5
                if runs(i, q, NT):
                    e.wait_ge(AG.sem, AG.at("hi", (i * 8, q)))
                    DH.took("lo", e.tensor_tensor(o_tiles(x1l, i, q), o_bank(q), o_tiles(x1h, i, q).bitcast(F32), ALU.subtract))
            piped(e, step, NT, 6)

        def o_tiles(x1, i, q):
            n, k = q % 4, 2 * (q // 4)
            return x1[:, i * 4 + k:i * 4 + k + 2, n * LANES:(n + 1) * LANES] if isinstance(i, int) else x1[:, bass.ds(i * 4 + k, 2), n * LANES:(n + 1) * LANES]

        def o_bank(q):
            return bank[7 - 3 * (q % 2)][:, 0:256].rearrange("p (g q) -> p g q", g=2)

        def att_scalar(e):
            for s in (AB, AE, AG):
                s.open(e)

            def step(i, T):
                q = T - 1
                if runs(i, q, NT):
                    z = q % 4
                    e.wait_ge(DA.sem, DA.at("dif", (i * 8, q)))
                    for g in range(4):
                        s = Sm[:, z, g // 2, g % 2]
                        AB.took(f"e{g}", e.activation(s, s, ACT.Exp, bias=st["nm"][:, z, g:g + 1], accum_out=st["sm"][:, z, g:g + 1]))
                    AB.took("es", e.activation(st["es"][:, z], st["df"][:, z], ACT.Exp))
                q = T - 3
                if runs(i, q, NT):
                    e.wait_ge(EF.sem, EF.at("o", (i * 8, q - 1)))
                    for kt in range(2):
                        e.wait_ge(ED.sem, ED.at(f"t{kt}", (i * 8, q)))
                        AE.took(f"w{kt}", e.activation(PT[:, kt], bk[5 + kt], ACT.Copy))
                q = T - 4
                if runs(i, q, NT):
                    e.wait_ge(EF.sem, EF.at("o", (i * 8, q)))
                    AG.took("hi", e.activation(o_tiles(x1h, i, q), o_bank(q), ACT.Copy))
            piped(e, step, NT, 6)

        def wo_scalar(e):
            def body(t, j):
                act_split(e, U_O + j + 2, t)
                act_x(e, 4, 5, t * 4 + j, "mlp1", x0h)
            turns(e, 8, body)

        def wo_vector(e):
            def body(t, j):
                dve_split(e, U_O + j + 2, t)
                m = t * 4 + j
                b = evac_start(e, U_O, j, t)
                e.tensor_tensor(tile(h, m), tile(h, m), one(b), ALU.add).then_inc(bank_free, 1)
                e.wait_ge(bank_free, after(U_O, j, t, 5))
                e.sem_inc(h_ready, 1)
                dve_x(e, 5, m, "mlp1", x0h, x0l)
            turns(e, 8, body)

        def wo_tensor(e):
            def there(k):
                return DH.sem, DH.at("lo", 4 * (k // 2) + 3)
            turns(e, 8, lambda t, j: pe_unit(e, U_O, j, t, x1h, x1l, there if j == 0 else None))

        at = [kept]
        acc7, sq7 = own_buf("acc7", [TOK]), own_buf("sq7", [TOK])
        squared7, acc7_ready = sem("squared7"), sem("acc7_ready")
        N7 = Steps(sem("norm7_steps"), "first once twice root both")

        def pool_h67(e):
            pool_start(e, 6)
            e.memset(acc7[:, :], 0.0).then_inc(acc7_ready, 1)
            with e.Fori(0, KT) as m:
                pool_square(e, 6, m)
                e.wait_ge(acc7_ready, m + 1)
                e.tensor_tensor(sq7[:, :], sq[:, :], between[:, 1, bass.ds(m, 1)].to_broadcast([LANES, TOK]), ALU.mult).then_inc(squared7, 1)
                e.wait_ge(squared7, m + 1)
                e.tensor_tensor(acc7[:, :], acc7[:, :], sq7[:, :], ALU.add).then_inc(acc7_ready, 1)
            e.wait_ge(acc7_ready, 9)
            e.sem_inc(squared, 9)
            e.sem_inc(acc_ready, 8)

        def pool_scaled(e):
            e.wait_ge(x_ready, 64)
            e.wait_ge(N7.sem, N7.at("first"))
            for m in range(KT):
                e.tensor_tensor(tile(h, m), tile(h, m), one(V("final", m, m + 1).to_broadcast([LANES, TOK])), ALU.mult).then_inc(h_gained, 1)
                e.wait_ge(h_gained, m + 1)
                e.tensor_tensor(tile(h, m), tile(h, m), one(acc[:, :]), ALU.mult).then_inc(h_ready, 1)
        h_gained = sem("h_gained")

        NC_, HEADS, HG, HP = 4, 32, 4, 64
        at = [kept]
        at = [own]
        T4 = own_buf("T4", [5, NC_, HEADS])
        G4 = own_buf("G4", [5, NC_, HG])
        zd = own_buf("zd", [NC_, HEADS]); az = own_buf("az", [NC_, HEADS]); s1 = own_buf("s1", [NC_, HEADS])
        s2_ = own_buf("s2_", [NC_, HEADS]); pq = own_buf("pq", [NC_, HEADS]); ea = own_buf("ea", [HEADS])
        dtr = own_buf("dtr", [TOK], lanes=HEADS)
        pre = own_buf("pre", [2, TOK + 3])
        cv = own_buf("cv", [2, TOK])
        dec_late = put("dec_late", [LANES, 2, 4, LANES], at=at[0] - 2 * TOK * 4)
        at[0] = (at[0] + 31) // 32 * 32
        xt = own_buf("xt", [4, TOK])
        bct = own_buf("bct", [4, TOK])
        zs = own_buf("zs", [4, TOK])
        xdt = own_buf("xdt", [NC_, HG, HP]); xw = own_buf("xw", [NC_, HG, HP])
        btok = own_buf("btok", [NC_, LANES]); cbm = own_buf("cbm", [NC_, LANES])
        dec = own_buf("dec", [2, HG, LANES]); ecs = own_buf("ecs", [2, HG, LANES]); cs = own_buf("cs", [2, HG, LANES])
        state = own_buf("state", [3, HG, HP])
        uu = put("uu", [LANES, 2, TOK], at=t32_at)
        usq = put("usq", [LANES, 2, TOK], at=acc_at)
        dts, dtx, dtt, dta = (sem(n) for n in ("dt_turned", "dt_exp", "dt_cumulated", "dt_act"))
        DM1 = Steps(sem("dt_steps"), "raw z az den r s s2 p17 p15 p13 p11 p9 p7 p5 p3 l mz dt adt nacs dif")

        def dt_scalar(e):
            act_split(e, U_DT + 2, 0)
            act_norm(e, 6, eps6)
            e.wait_ge(N7.sem, N7.at("twice"))
            e.activation(sd[:, :], sq[:, :], ACT.Sqrt, bias=eps5[:, :], scale=1.0 / DM).then_inc(sd_ready, 1)
            e.activation(ea[:, :], V("a_log"), ACT.Exp)
            e.wait_ge(DM1.sem, DM1.at("az"))
            e.activation(s1[:, :, :], az[:, :, :], ACT.Exp, scale=-1.0).then_inc(dtx, 1)
            e.wait_ge(DM1.sem, DM1.at("dif"))
            e.activation(T4[:, 3], zd[:, :, :], ACT.Exp).then_inc(dta, 1)
            e.activation(T4[:, 4], bank[6][:, 128:256].rearrange("p (c h) -> p c h", c=NC_), ACT.Exp).then_inc(dta, 1)

        def dt_vector(e):
            tt, ts, stt = e.tensor_tensor, e.tensor_scalar, e.scalar_tensor_tensor
            d = lambda name, ins: DM1.took(name, ins)
            n = lambda: DM1.next(e)
            DM1.open(e)
            dve_split(e, U_DT + 2, 0)
            N7.open(e)
            e.wait_ge(sd_ready, 7)
            N7.took("first", e.reciprocal(acc[:, :], sd[:, :]))
            e.wait_ge(norm_mm, 8)
            N7.next(e).took("once", e.tensor_tensor(sq[:, :], bk[5], acc[:, :], ALU.mult))
            N7.next(e).took("twice", e.tensor_tensor(sq[:, :], sq[:, :], acc[:, :], ALU.mult))
            e.sem_inc(r_ready, 1)
            e.wait_ge(sd_ready, 8)
            N7.took("root", e.reciprocal(R[:, :], sd[:, :]))
            N7.next(e).took("both", e.tensor_tensor(R[:, :], R[:, :], acc[:, :], ALU.mult))
            e.wait_ge(N7.sem, N7.at("both"))
            e.sem_inc(r_ready, 1)
            b = evac_start(e, U_DT, 0, 0)
            d("raw", tt(dtr[:, :], bank[U_DT % 4][0:HEADS, :], R[0:HEADS, :], ALU.mult))
            n()
            e.sem_inc(bank_free, 1)
            for t in (pre,):
                e.memset(t[:, :, 0:3], 0.0)
            e.wait_ge(dts, 1)
            full = [LANES, NC_, HEADS]
            n(); d("z", tt(zd[:, :, :], bank[5][:, 0:128].rearrange("p (c h) -> p c h", c=NC_), V("dt_bias").unsqueeze(1).to_broadcast(full), ALU.add))
            n(); d("az", stt(az[:, :, :], zd[:, :, :], -1.0, zd[:, :, :], ALU.mult, ALU.max))
            e.wait_ge(dtx, 1)
            n(); d("den", ts(pq[:, :, :], s1[:, :, :], 2.0, None, ALU.add))
            n(); d("r", e.reciprocal(pq[:, :, :], pq[:, :, :]))
            n(); d("s", tt(s1[:, :, :], s1[:, :, :], pq[:, :, :], ALU.mult))
            n(); d("s2", tt(s2_[:, :, :], s1[:, :, :], s1[:, :, :], ALU.mult))
            n(); d("p17", ts(pq[:, :, :], s2_[:, :, :], 1 / 17, None, ALU.mult))
            for k in (15, 13, 11, 9, 7, 5, 3):
                n(); d(f"p{k}", stt(pq[:, :, :], pq[:, :, :], 1 / k, s2_[:, :, :], ALU.add, ALU.mult))
            n(); d("l", stt(pq[:, :, :], pq[:, :, :], 1.0, s1[:, :, :], ALU.add, ALU.mult))
            n(); d("mz", ts(zd[:, :, :], zd[:, :, :], 0.0, None, ALU.max))
            n(); d("dt", stt(T4[:, 0], pq[:, :, :], 2.0, zd[:, :, :], ALU.mult, ALU.add))
            n(); d("adt", stt(T4[:, 1], T4[:, 0], -1.0, ea[:, :].unsqueeze(1).to_broadcast(full), ALU.mult, ALU.mult))
            e.wait_ge(dtt, 1)
            cum = bank[6][:, 0:128].rearrange("p (c h) -> p c h", c=NC_)
            end = bank[6][:, 128:256].rearrange("p (c h) -> p c h", c=NC_)
            n(); d("nacs", ts(T4[:, 2], cum, -1.0, None, ALU.mult))
            n(); d("dif", tt(zd[:, :, :], end, T4[:, 2], ALU.add))

        def dt_tensor(e):
            pe_unit(e, U_DT, 0, 0, x1h, x1l, ready(x_ready, 56))
            pe_norm(e, 6)
            e.wait_ge(acc_ready, 64)
            e.matmul(bk[5], C("ones"), acc7[:, :], start=True, stop=True).then_inc(norm_mm, 1)
            e.wait_ge(DM1.sem, DM1.at("raw"))
            for c in range(NC_):
                last = e.transpose(bank[5][:, c * HEADS:(c + 1) * HEADS], dtr[:, c * LANES:(c + 1) * LANES], C("ident", hi=HEADS, rows=HEADS))
            last.then_inc(dts, 1)
            e.wait_ge(DM1.sem, DM1.at("adt"))
            adt = T4[:, 1].rearrange("p c h -> p (c h)")
            e.matmul(bank[6][:, 0:128], C("tri"), adt, start=True, stop=True)
            e.matmul(bank[6][:, 128:256], C("ones"), adt, start=True, stop=True).then_inc(dtt, 1)

        conv, silued = sem("conv"), sem("silued")
        EA2 = Steps(sem("ssd_turned"), "tx0 tx1 tb cb a0 a1")
        EB2 = Steps(sem("ssd_products"), "n0 n1 n2 a2 y0 a3 y1 y2 y3")
        ED2 = Steps(sem("ssd_sum"), "sum", ahead=2)
        DA2 = Steps(sem("ssd_inputs"), "xd0 xd1 cbm g0 g1")
        DB2 = Steps(sem("ssd_masked"), "S1 Sm2 S2 Sm3 S3 g2 M0 g3 M1 M2 M3")
        DC2 = Steps(sem("ssd_gated"), "ud0 uz0 ud1 uz1")
        DD2 = Steps(sem("ssd_normed"), "rg yg0 yg1 lo0 lo1")
        AA2 = Steps(sem("ssd_exp_early"), "bt e0 e1 x1")
        AB2 = Steps(sem("ssd_exp_late"), "e2 x2 e3 x3")
        AC2 = Steps(sem("ssd_squares"), "q0 q1")
        AD2 = Steps(sem("ssd_root"), "sg hi0 hi1", ahead=2)
        PA2 = Steps(sem("ssd_weighted"), "G xw")
        PB2 = Steps(sem("ssd_c_decayed"), "c1 c2 c3")

        def mamba_units(j):
            return ("x", j) if j < 4 else ("bc", j - 4) if j < 8 else ("z", j - 8)

        def in_scalar(e, hf, pr):
            n4 = hf * 8 + pr * 3
            turn = hf * 2 + pr

            def silu(j):
                kind, i = mamba_units(j)
                if kind == "z":
                    e.wait_ge(bank_free, after(U_MAMBA, j, n4, 5))
                    e.activation(zs[:, i], t32[:, :] if i % 2 == 0 else a32[:, :], ACT.Silu).then_inc(silued, 1)
                else:
                    e.wait_ge(conv, turn * 32 + 4 * j + 4)
                    dst = xt[:, i] if kind == "x" else bct[:, i]
                    e.activation(dst, cv[:, j % 2], ACT.Silu).then_inc(silued, 1)

            for j in range(12):
                act_split(e, U_MAMBA + j + 2, n4)
                if j:
                    silu(j - 1)
            silu(11)

        def in_vector(e, hf, pr):
            n4 = hf * 8 + pr * 3
            turn = hf * 2 + pr
            for j in range(12):
                dve_split(e, U_MAMBA + j + 2, n4)
                kind, i = mamba_units(j)
                b = evac_start(e, U_MAMBA, j, n4)
                if kind == "z":
                    e.tensor_tensor(t32[:, :] if i % 2 == 0 else a32[:, :], b, R[:, :], ALU.mult).then_inc(bank_free, 1)
                    if i >= 1:
                        e.wait_ge(silued, turn * 12 + j)
                    continue
                z = j % 2
                e.tensor_tensor(pre[:, z, 3:], b, R[:, :], ALU.mult).then_inc(bank_free, 1)
                if kind == "x":
                    ct = hf * 8 + pr * 4 + i
                else:
                    ct = hf * 4 + pr * 2 + (16 + 8 * (i // 2) + i % 2)
                w = lambda k: par[:, bass.ds(ct + (PC["conv_w"][0] + 32 * k), 1)]
                e.wait_ge(bank_free, after(U_MAMBA, j, n4, 5))
                if j >= 2:
                    e.wait_ge(silued, turn * 12 + (j - 1))
                e.tensor_scalar(cv[:, z], pre[:, z, 3:], w(3), par[:, bass.ds(ct + PC["conv_b"][0], 1)], ALU.mult, ALU.add).then_inc(conv, 1)
                for k in range(3):
                    e.wait_ge(conv, turn * 32 + (4 * j + 1 + k))
                    e.scalar_tensor_tensor(cv[:, z], pre[:, z, k:k + TOK], w(k), cv[:, z], ALU.mult, ALU.add).then_inc(conv, 1)

        def in_tensor(e, hf, pr):
            n4 = hf * 8 + pr * 3
            for j in range(12):
                pe_unit(e, U_MAMBA, j, n4, x1h, x1l)

        decays = [dec[:, 0], dec[:, 1], dec_late[:, 0], dec_late[:, 1]]

        def tensor_A(e, T, gl, units):
            e.wait_ge(silued, units)
            for c2 in range(2):
                e.wait_ge(DB2.sem, DB2.before("S3" if c2 else "S2", T))
                for c in (2 * c2, 2 * c2 + 1):
                    for i in range(2):
                        last = e.transpose(bank[5 + c2][:, (c % 2) * 256 + i * 128:(c % 2) * 256 + (i + 1) * 128], xt[:, 2 * gl + i, c * LANES:(c + 1) * LANES], C("ident"))
                EA2.took(f"tx{c2}", last)
            e.wait_ge(AD2.sem, AD2.at("sg", (T[0], -1)))
            for c in range(NC_):
                last = e.transpose(bank[7][:, c * LANES:(c + 1) * LANES], bct[:, gl, c * LANES:(c + 1) * LANES], C("ident"))
            EA2.took("tb", last)
            e.wait_ge(DA2.sem, DA2.before("cbm", T))
            for c in range(NC_):
                cc = slice(c * LANES, (c + 1) * LANES)
                last = e.matmul(bank[4][:, cc], bct[:, gl, cc], bct[:, 2 + gl, cc], start=True, stop=True)
            EA2.took("cb", last)
            e.wait_ge(PA2.sem, PA2.at("G", T))
            for c in range(2):
                e.wait_ge(DB2.sem, DB2.before(f"g{c + 2}", T))
                e.wait_ge(AB2.sem, AB2.before(f"x{c + 2}", T))
                EA2.took(f"a{c}", cumulated(e, c))

        def cumulated(e, c):
            for r in range(HG):
                last = e.matmul(bank[c % 2][:, r * LANES:(r + 1) * LANES], G4[:, 1, c, r:r + 1].to_broadcast([LANES, LANES]), C("tri"), start=True, stop=True)
            return last

        def tensor_B(e, T, gl):
            e.wait_ge(PA2.sem, PA2.at("xw", T))
            e.wait_ge(AA2.sem, AA2.at("bt", T))
            e.wait_ge(DA2.sem, DA2.at("xd1", T))
            for c in range(3):
                o = bank[5 + c // 2][:, (c % 2) * 256:(c % 2) * 256 + 256]
                EB2.took(f"n{c}", e.matmul(o, btok[:, c], xw[:, c].rearrange("p r w -> p (r w)"), start=True, stop=True))

            def outs(c):
                e.wait_ge(DB2.sem, DB2.at(f"M{c}", T))
                if c == 0:
                    e.wait_ge(DC2.sem, DC2.before("ud1", T))
                else:
                    e.wait_ge(PB2.sem, PB2.at(f"c{c}", T))
                for r in range(HG):
                    o = bank[2 + r // 2][(r % 2) * HP:(r % 2 + 1) * HP, c * LANES:(c + 1) * LANES]
                    last = e.matmul(o, xdt[:, c, r], decays[c][:, r], start=True, stop=(c == 0))
                    if c:
                        last = e.matmul(o, state[:, c - 1, r], cs[:, c % 2, r], start=False, stop=True)
                EB2.took(f"y{c}", last)

            e.wait_ge(DA2.sem, DA2.at("g0", T))
            EB2.took("a2", cumulated(e, 2))
            outs(0)
            e.wait_ge(DA2.sem, DA2.at("g1", T))
            e.wait_ge(AA2.sem, AA2.at("x1", T))
            EB2.took("a3", cumulated(e, 3))
            outs(1)
            outs(2)
            outs(3)

        def tensor_D(e, T, gl):
            e.wait_ge(AC2.sem, AC2.at("q1", T))
            if gl == 0:
                e.wait_ge(AA2.sem, AA2.at("bt", (T[0], 1)))
            else:
                e.wait_ge(AD2.sem, AD2.at("sg", (T[0], 0)))
            e.matmul(bk[7], C("ones"), usq[:, 0], start=True, stop=False)
            ED2.took("sum", e.matmul(bk[7], C("ones"), usq[:, 1], start=False, stop=True))

        def vector_A(e, T, gl):
            tt = e.tensor_tensor
            e.wait_ge(PA2.sem, PA2.at("G", T))
            e.wait_ge(EB2.sem, EB2.before("y3", T))
            for c2 in range(2):
                e.wait_ge(EA2.sem, EA2.at(f"tx{c2}", T))
                if c2 == 0:
                    e.wait_ge(PA2.sem, PA2.before("xw", T))
                DA2.took(f"xd{c2}", tt(xdt[:, 2 * c2:2 * c2 + 2], bank[5 + c2][:, :].rearrange("p (c r w) -> p c r w", c=2, r=HG),
                                       G4[:, 0, 2 * c2:2 * c2 + 2].unsqueeze(3).to_broadcast([LANES, 2, HG, HP]), ALU.mult))
            e.wait_ge(EA2.sem, EA2.at("cb", T))
            e.wait_ge(DB2.sem, DB2.before("M3", T))
            DA2.took("cbm", tt(cbm[:, :, :], bk[4].rearrange("p (c l) -> p c l", c=NC_), C("tri").unsqueeze(1).to_broadcast([LANES, NC_, LANES]), ALU.mult))
            for c in range(2):
                e.wait_ge(EA2.sem, EA2.at(f"a{c}", T))
                DA2.took(f"g{c}", gaps(e, c))

        def gaps(e, c):
            for r in range(HG):
                last = e.tensor_scalar(decays[c][:, r], bank[c % 2][:, r * LANES:(r + 1) * LANES], G4[:, 2, c, r:r + 1], 0.0, ALU.add, ALU.min)
            return last

        def vector_B(e, T, gl):
            tt = e.tensor_tensor
            n = lambda: DB2.next(e, T)
            new = lambda c: bank[5 + c // 2][:, (c % 2) * 256:(c % 2) * 256 + 256].rearrange("p (r w) -> p r w", r=HG)
            e.wait_ge(EB2.sem, EB2.at("n1", T))
            DB2.took("S1", e.tensor_copy(state[:, 0], new(0)))
            for c in (1, 2):
                n().took(f"Sm{c + 1}", tt(state[:, c], state[:, c - 1], G4[:, 4, c].unsqueeze(2).to_broadcast([LANES, HG, HP]), ALU.mult))
                if c == 2:
                    e.wait_ge(EB2.sem, EB2.at("n2", T))
                n().took(f"S{c + 1}", tt(state[:, c], state[:, c], new(c), ALU.add))

            def masked(c):
                A = AA2 if c < 2 else AB2
                e.wait_ge(A.sem, A.at(f"e{c}", T))
                DB2.took(f"M{c}", tt(decays[c], decays[c], cbm[:, c].unsqueeze(1).to_broadcast([LANES, HG, LANES]), ALU.mult))

            e.wait_ge(EB2.sem, EB2.at("a2", T))
            DB2.took("g2", gaps(e, 2))
            masked(0)
            e.wait_ge(EB2.sem, EB2.at("a3", T))
            DB2.took("g3", gaps(e, 3))
            for c in (1, 2, 3):
                masked(c)

        def vector_C(e, T, gl, dtile):
            e.wait_ge(EB2.sem, EB2.at("y3", T))
            e.wait_ge(DD2.sem, DD2.before("lo1", T))
            for i in range(2):
                dsk = par[:, bass.ds(dtile + (PC["d_skip"][0] + i), 1)]
                DC2.took(f"ud{i}", e.scalar_tensor_tensor(uu[:, i], xt[:, 2 * gl + i], dsk, bk[2 + i], ALU.mult, ALU.add))
                DC2.next(e, T).took(f"uz{i}", e.tensor_tensor(uu[:, i], uu[:, i], zs[:, 2 * gl + i], ALU.mult))

        def vector_D(e, T, gl, o_tile, dtile):
            e.wait_ge(AD2.sem, AD2.at("sg", T))
            DD2.took("rg", e.reciprocal(sd[:, :], sd[:, :]))
            for i in range(2):
                gg = par[:, bass.ds(dtile + (PC["gate_g"][0] + i), 1)]
                DD2.next(e, T).took(f"yg{i}", e.scalar_tensor_tensor(uu[:, i], uu[:, i], gg, sd[:, :], ALU.mult, ALU.mult))
            for i in range(2):
                e.wait_ge(AD2.sem, AD2.at(f"hi{i}", T))
                DD2.took(f"lo{i}", e.tensor_tensor(tile(x0l, o_tile + i), uu[:, i:i + 1], tile(x0h, o_tile + i).bitcast(F32), ALU.subtract))

        def scalar_A(e, T, gl):
            e.wait_ge(EA2.sem, EA2.at("tb", T))
            e.wait_ge(EB2.sem, EB2.before("n2", T))
            AA2.took("bt", e.activation(btok[:, :, :], bk[7].rearrange("p (c n) -> p c n", c=NC_), ACT.Copy))
            for c in range(2):
                e.wait_ge(DA2.sem, DA2.at(f"g{c}", T))
                AA2.took(f"e{c}", e.activation(decays[c], decays[c], ACT.Exp))
            e.wait_ge(PB2.sem, PB2.before("c3", T))
            AA2.took("x1", e.activation(ecs[:, 1], bk[1].rearrange("p (r l) -> p r l", r=HG), ACT.Exp))

        def scalar_B(e, T, gl):
            for c in (2, 3):
                e.wait_ge(DB2.sem, DB2.at(f"g{c}", T))
                AB2.took(f"e{c}", e.activation(decays[c], decays[c], ACT.Exp))
                e.wait_ge(PB2.sem, PB2.before("c2", T) if c == 2 else PB2.at("c1", T))
                AB2.took(f"x{c}", e.activation(ecs[:, c % 2], bk[c % 2].rearrange("p (r l) -> p r l", r=HG), ACT.Exp))

        def scalar_C(e, T, gl):
            e.wait_ge(ED2.sem, ED2.before("sum", T))
            for i in range(2):
                e.wait_ge(DC2.sem, DC2.at(f"uz{i}", T))
                AC2.took(f"q{i}", e.activation(usq[:, i], uu[:, i], ACT.Square))

        def scalar_D(e, T, gl, o_tile):
            e.wait_ge(ED2.sem, ED2.at("sum", T))
            e.wait_ge(DD2.sem, DD2.before("yg1", T))
            AD2.took("sg", e.activation(sd[:, :], bk[7], ACT.Sqrt, bias=eps5[:, :], scale=1.0 / 256))
            for i in range(2):
                e.wait_ge(DD2.sem, DD2.at(f"yg{i}", T))
                AD2.took(f"hi{i}", e.activation(tile(x0h, o_tile + i), uu[:, i:i + 1], ACT.Copy))

        def pool_A(e, T, gl, g):
            e.wait_ge(EB2.sem, EB2.before("a3", T))
            e.wait_ge(DB2.sem, DB2.before("g3", T))
            PA2.next(e, T).took("G", e.tensor_copy(G4[:, :, :, :], T4[:, :, :, bass.ds(g * 4, 4)]))
            e.wait_ge(EB2.sem, EB2.before("n2", T))
            e.wait_ge(DA2.sem, DA2.at("xd1", T))
            PA2.next(e, T).took("xw", e.tensor_tensor(xw[:, :, :, :], xdt[:, :, :, :], G4[:, 3].unsqueeze(3).to_broadcast([LANES, NC_, HG, HP]), ALU.mult))

        def pool_B(e, T, gl):
            for c in (1, 2, 3):
                A = AA2 if c < 2 else AB2
                e.wait_ge(A.sem, A.at(f"x{c}", T))
                e.wait_ge(EB2.sem, EB2.at("y1", T) if c == 3 else EB2.before("y2" if c == 2 else "y3", T))
                ccol = bct[:, 2 + gl, c * LANES:(c + 1) * LANES].unsqueeze(1).to_broadcast([LANES, HG, LANES])
                PB2.took(f"c{c}", e.tensor_tensor(cs[:, c % 2], ccol, ecs[:, c % 2], ALU.mult))

        def mamba(e, units, parts, out):
            for hf in range(2):
                with e.Fori(0, 2) as pr:
                    if units:
                        units(e, hf, pr)
                    for part, gl in ("A", 0), ("B", 0), ("C", 0), ("A", 1), ("D", 0), ("B", 1), ("C", 1), ("D", 1):
                        if part in parts:
                            parts[part](e, (hf * 4 + pr * 2, gl), gl, hf, pr)
                if out:
                    out(e, hf)

        def mamba_tensor(e):
            for s_ in (EA2, EB2, ED2):
                s_.open(e)

            def out(e, hf):
                def there(k):
                    return DD2.sem, DD2.at(f"lo{k % 2}", (hf * 4, k // 2))
                turns(e, 8, lambda t, j: pe_unit(e, U_MAMBA + 24, j, hf * 8 + t, x0h, x0l, there if j == 0 else None))
            mamba(e, in_tensor, {
                "A": lambda e, T, gl, hf, pr: tensor_A(e, T, gl, hf * 24 + pr * 12 + 12),
                "B": lambda e, T, gl, hf, pr: tensor_B(e, T, gl),
                "D": lambda e, T, gl, hf, pr: tensor_D(e, T, gl)}, out)

        def mamba_vector(e):
            for s_ in (DA2, DB2, DC2, DD2):
                s_.open(e)

            def out(e, hf):
                def body(t, j):
                    dve_split(e, U_MAMBA + 24 + j + 2, hf * 8 + t)
                    b = evac_start(e, U_MAMBA + 24, j, hf * 8 + t)
                    m = t * 4 + j
                    e.tensor_tensor(tile(h, m), tile(h, m), one(b), ALU.add).then_inc(bank_free, 1)
                    if hf:
                        e.wait_ge(bank_free, after(U_MAMBA + 24, j, hf * 8 + t, 5))
                        e.sem_inc(h_ready, 1)
                        dve_x(e, 8, m, "kv2", x1h, x1l)
                turns(e, 8, body)
            mamba(e, in_vector, {
                "A": lambda e, T, gl, hf, pr: vector_A(e, T, gl),
                "B": lambda e, T, gl, hf, pr: vector_B(e, T, gl),
                "C": lambda e, T, gl, hf, pr: vector_C(e, T, gl, hf * 8 + pr * 4 + 2 * gl),
                "D": lambda e, T, gl, hf, pr: vector_D(e, T, gl, pr * 4 + 2 * gl, hf * 8 + pr * 4 + 2 * gl)}, out)
            more_x_vector(e, 9, "b_norm", x0h, x0l)

        def mamba_scalar(e):
            def out(e, hf):
                def body(t, j):
                    act_split(e, U_MAMBA + 24 + j + 2, hf * 8 + t)
                    if hf:
                        act_x(e, 8, 8, t * 4 + j, "kv2", x1h)
                turns(e, 8, body)
            for s_ in (AA2, AB2, AC2, AD2):
                s_.open(e)
            mamba(e, in_scalar, {
                "A": lambda e, T, gl, hf, pr: scalar_A(e, T, gl),
                "B": lambda e, T, gl, hf, pr: scalar_B(e, T, gl),
                "C": lambda e, T, gl, hf, pr: scalar_C(e, T, gl),
                "D": lambda e, T, gl, hf, pr: scalar_D(e, T, gl, pr * 4 + 2 * gl)},
                  out)
            more_x_scalar(e, 8, 9, "b_norm", x0h)

        def mamba_pool(e):
            for s_ in (PA2, PB2):
                s_.open(e)
            e.wait_ge(dta, 2)
            e.wait_ge(DM1.sem, DM1.at("dif"))
            pool_scaled(e)
            mamba(e, None, {
                "A": lambda e, T, gl, hf, pr: pool_A(e, T, gl, hf * 4 + pr * 2 + gl),
                "B": lambda e, T, gl, hf, pr: pool_B(e, T, gl)}, None)

        DH_, LAMBDA_INIT = 8, 0.8 - 0.6 * math.exp(-0.3)
        at = [own]
        K2 = own_buf("K2", [DH_, TOK])
        V2tok = own_buf("V2tok", [4, DM])
        q2 = own_buf("q2", [DH_, TOK])
        gate = own_buf("gate", [DH_, TOK])
        v32_at = (at[0] + 31) // 32 * 32
        v32 = own_buf("v32", [2, TOK])
        lprod, lsum, lexp = own_buf("lprod", [2, 64]), own_buf("lsum", [2]), own_buf("lexp", [2])
        nlam, sub_gl = own_buf("nlam", [1]), own_buf("sub_gl", [1])
        at = [v32_at]
        s2t = {n: own_buf("s2t_" + n, [4, 2]) for n in "mx nm sm rc".split()}
        at = [x0_at]
        Q2s = own_buf("Q2s", [2, TOK])
        K2s = own_buf("K2s", [2, TOK])
        V2s = own_buf("V2s", [2, 4, LANES])
        S2 = own_buf("S2", [4, 2, TOK])
        W2T = own_buf("W2T", [2, TOK])
        O32 = put("O32", [LANES, 2, TOK], at=acc_at)
        assert at[0] <= x0_at + 32768
        VT2 = Steps(sem("v2_turned"), "t", ahead=2)
        VK2 = Steps(sem("v2_kept"), "k", ahead=2)
        GS2 = Steps(sem("gate_silu"), "g", ahead=2)
        LM = Steps(sem("lambda_steps"), "pr sum nlam0 nlam sub")
        lam_exp = sem("lambda_exp")

        def kv2_scalar(e):
            act_norm(e, 8, eps5)
            e.wait_ge(LM.sem, LM.at("sum"))
            e.activation(lexp[:, :], lsum[:, :], ACT.Exp).then_inc(lam_exp, 1)
            VK2.open(e)
            turns(e, 8, lambda t, j: act_split(e, U_KV2 + j + 2, t))

            def keep(t, j):
                T = (t * 4, j)
                e.wait_ge(VT2.sem, VT2.at("t", T))
                VK2.took("k", e.activation(V2tok[:, :, bass.ds(t * LANES * 4 + j * LANES, LANES)], bk[5 + j % 2].rearrange("p (c n) -> p c n", c=4), ACT.Copy))

            def body(t, j):
                act_split(e, U_KV2 + 8 + j + 2, t)
                if j:
                    keep(t, j - 1)
                if j == 3:
                    keep(t, 3)
            turns(e, 8, body)

        def kv2_vector(e):
            dve_norm(e, 8)
            LM.open(e)
            l4 = V("lam_qk").rearrange("p (a b d) -> p a b d", a=2, b=2)
            LM.took("pr", e.tensor_tensor(lprod[:, :, :], l4[:, :, 0], l4[:, :, 1], ALU.mult))
            LM.next(e).took("sum", e.reduce_sum(lsum[:, :].unsqueeze(2), lprod[:, :, :], axis=AX.X))
            e.wait_ge(lam_exp, 1)
            LM.next(e).took("nlam0", e.tensor_tensor(nlam[:, :], lexp[:, 1:2], lexp[:, 0:1], ALU.subtract))
            LM.next(e).took("nlam", e.tensor_scalar(nlam[:, :], nlam[:, :], -LAMBDA_INIT, None, ALU.add))
            LM.next(e).took("sub", e.tensor_scalar(sub_gl[:, :], V("sub_g"), 1.0 - LAMBDA_INIT, None, ALU.mult))

            def k_body(t, j):
                dve_split(e, U_KV2 + j + 2, t)
                b = evac_start(e, U_KV2, j, t)
                e.tensor_tensor(tile(K2, t * 4 + j), one(b), one(R[:, :]), ALU.mult).then_inc(bank_free, 1)
            turns(e, 8, k_body)

            def v_body(t, j):
                dve_split(e, U_KV2 + 8 + j + 2, t)
                b = evac_start(e, U_KV2 + 8, j, t)
                e.wait_ge(VT2.sem, VT2.at("t", (t * 4, j - 2)))
                e.tensor_tensor(v32[:, j % 2], b, R[:, :], ALU.mult).then_inc(bank_free, 1)
            turns(e, 8, v_body)

        def kv2_tensor(e):
            VT2.open(e)
            pe_norm(e, 8)
            turns(e, 8, lambda t, j: pe_unit(e, U_KV2, j, t, x1h, x1l, ready(x_ready, 64) if j == 0 else None))

            def turn(t, j):
                e.wait_ge(bank_free, after(U_KV2 + 8, j, t, 5))
                e.wait_ge(VK2.sem, VK2.at("k", (t * 4, j - 2)))
                for c in range(4):
                    last = e.transpose(bank[5 + j % 2][:, c * LANES:(c + 1) * LANES], v32[:, j % 2, c * LANES:(c + 1) * LANES], C("ident"))
                VT2.took("t", last)

            def body(t, j):
                pe_unit(e, U_KV2 + 8, j, t, x1h, x1l)
                if j:
                    turn(t, j - 1)
                if j == 3:
                    turn(t, 3)
            turns(e, 8, body)

        def qg2_scalar(e):
            GS2.open(e)
            turns(e, 8, lambda t, j: act_split(e, U_QG2 + j + 2, t))

            def body(t, j):
                act_split(e, U_QG2 + 8 + j + 2, t)
                e.wait_ge(bank_free, after(U_QG2 + 8, j, t, 5))
                GS2.took("g", e.activation(tile(gate, t * 4 + j), one((a32 if j % 2 else t32)[:, :]), ACT.Silu))
            turns(e, 8, body)

        def qg2_vector(e):
            def q_body(t, j):
                dve_split(e, U_QG2 + j + 2, t)
                b = evac_start(e, U_QG2, j, t)
                e.scalar_tensor_tensor(tile(q2, t * 4 + j), one(b), 0.125, one(R[:, :]), ALU.mult, ALU.mult).then_inc(bank_free, 1)
            turns(e, 8, q_body)

            def g_body(t, j):
                dve_split(e, U_QG2 + 8 + j + 2, t)
                b = evac_start(e, U_QG2 + 8, j, t)
                e.wait_ge(GS2.sem, GS2.at("g", (t * 4, j - 2)))
                e.tensor_tensor((a32 if j % 2 else t32)[:, :], b, R[:, :], ALU.mult).then_inc(bank_free, 1)
            turns(e, 8, g_body)

        def qg2_tensor(e):
            turns(e, 16, lambda t, j: pe_unit(e, U_QG2, j, t, x0h, x0l, ready(x_ready, 72) if j == 0 else None))

        DT = 4 * DH_
        FP = Steps(sem("diff_copies"), "K Q V")
        FM = Steps(sem("diff_max"), "m0 m1 max neg", ahead=8)
        FE = Steps(sem("diff_exp"), "e0 e1", ahead=8)
        FW = Steps(sem("diff_weights"), "rec lrec w0 w1", ahead=8)
        FS = Steps(sem("diff_scores"), "s", ahead=8)
        FT = Steps(sem("diff_turned"), "t", ahead=8)
        FC = Steps(sem("diff_kept"), "w", ahead=8)
        FO = Steps(sem("diff_out"), "o", ahead=8)
        FK = Steps(sem("diff_out_kept"), "k", ahead=8)
        HA = Steps(sem("head_scalar"), "sq sd hi", ahead=4)
        HD = Steps(sem("head_vector"), "rc y yg lo", ahead=4)
        HE = Steps(sem("head_sum"), "sum", ahead=4)

        def diff_pool(e):
            FP.open(e)
            e.wait_ge(unit_done, U_O2)
            e.wait_ge(bank_free, U_O2 + 4)
            e.wait_ge(VK2.sem, VK2.at("k", 7))
            with e.Fori(0, DH_ // 2) as i:
                for x in range(2):
                    e.wait_ge(FS.sem, FS.at("s", (i * 8, 4 * x - 5)))
                    FP.next(e, (i * 2, x)).took("K", e.tensor_copy(K2s[:, x:x + 1], tile(K2, i * 2 + x)))
                    FP.next(e, (i * 2, x)).took("Q", e.tensor_copy(Q2s[:, x:x + 1], tile(q2, i * 2 + x)))
                    e.wait_ge(FO.sem, FO.at("o", (i * 8, 4 * x - 5)))
                    FP.next(e, (i * 2, x)).took("V", e.tensor_copy(V2s[:, x], V2tok[:, :, bass.ds(i * (2 * LANES) + x * LANES, LANES)]))

        def ended(i, T, lag):
            q = T - lag
            return (i * 2, q // 4) if q % 4 == 3 and runs(i, q, DT) else None

        def diff_tensor(e):
            for s in (FS, FT, FO, HE):
                s.open(e)

            def step(i, T):
                if runs(i, T, DT):
                    x, n, b = T // 4, T % 4, 2 * (T % 2)
                    if n == 0:
                        e.wait_ge(FP.sem, FP.at("Q", (i * 2, x)))
                    e.wait_ge(FM.sem, FM.at("m1", (i * 8, T - 2)))
                    for s in range(2):
                        last = e.matmul(bank[b + s][:, 0:LANES * (n + 1)], Q2s[64 * s:64 * s + 64, x, n * LANES:(n + 1) * LANES],
                                        K2s[64 * s:64 * s + 64, x, 0:LANES * (n + 1)], start=True, stop=True)
                    FS.took("s", last)
                q = T - 3
                if runs(i, q, DT):
                    n = q % 4
                    e.wait_ge(FW.sem, FW.at("w1", (i * 8, q)))
                    e.wait_ge(FC.sem, FC.at("w", (i * 8, q - 2)))
                    for c in range(n + 1):
                        last = e.transpose(bank[5 + q % 2][:, c * LANES:(c + 1) * LANES], S2[:, q % 4, 0, c * LANES:(c + 1) * LANES], C("ident"))
                    FT.took("t", last)
                q = T - 4
                if runs(i, q, DT):
                    x, n = q % 8 // 4, q % 4
                    if n == 0:
                        e.wait_ge(FP.sem, FP.at("V", (i * 2, q // 4)))
                    e.wait_ge(FC.sem, FC.at("w", (i * 8, q)))
                    e.wait_ge(FK.sem, FK.at("k", (i * 8, q - 1)))
                    for c in range(n + 1):
                        last = e.matmul(bank[7][:, n * LANES:(n + 1) * LANES], V2s[:, x, c], W2T[:, q % 2, c * LANES:(c + 1) * LANES], start=(c == 0), stop=(c == n))
                    FO.took("o", last)
                H = ended(i, T, 5)
                if H:
                    e.wait_ge(HA.sem, HA.at("sq", H))
                    HE.took("sum", e.matmul(bk[4], C("ones"), t32[:, :], start=True, stop=True))
            piped(e, step, DT, 8)

        def diff_vector(e):
            for s in (FM, FW, HD):
                s.open(e)

            def step(i, T):
                if runs(i, T, DT):
                    x, n, b, z = T // 4, T % 4, 2 * (T % 2), T % 4
                    t, N = (i * 8, T), LANES * (T % 4 + 1)
                    e.wait_ge(FS.sem, FS.at("s", t))
                    e.wait_ge(FT.sem, FT.at("t", (i * 8, T - 4)))
                    s0 = CC["slope"][0] + x
                    slope = const[:, s0:s0 + 1] if isinstance(i, int) and i == 0 else const[:, bass.ds(i * 2 + s0, 1)]
                    for s in range(2):
                        FM.took(f"m{s}", e.scalar_tensor_tensor(S2[:, z, s, 0:N], C("dist", lo=TOK - N), slope, bank[b + s][:, 0:N], ALU.mult, ALU.add))
                    FM.next(e, t).took("max", e.reduce_max(s2t["mx"][:, z].unsqueeze(2), S2[:, z, :, 0:N], axis=AX.X))
                    FM.next(e, t).took("neg", e.tensor_scalar(s2t["nm"][:, z], s2t["mx"][:, z], -1.0, None, ALU.mult))
                q = T - 2
                if runs(i, q, DT):
                    t, z, N = (i * 8, q), q % 4, LANES * (q % 4 + 1)
                    e.wait_ge(FE.sem, FE.at("e1", t))
                    FW.next(e, t).took("rec", e.reciprocal(s2t["rc"][:, z], s2t["sm"][:, z]))
                    FW.next(e, t).took("lrec", e.tensor_tensor(s2t["rc"][:, z, 1:2], s2t["rc"][:, z, 1:2], nlam[:, :], ALU.mult))
                    FW.next(e, t).took("w0", e.tensor_scalar(S2[:, z, 0, 0:N], S2[:, z, 0, 0:N], s2t["rc"][:, z, 0:1], None, ALU.mult))
                    FW.next(e, t).took("w1", e.scalar_tensor_tensor(S2[:, z, 0, 0:N], S2[:, z, 1, 0:N], s2t["rc"][:, z, 1:2], S2[:, z, 0, 0:N], ALU.mult, ALU.add))
                H = ended(i, T, 7)
                if H:
                    y = H[1] % 2
                    e.wait_ge(HA.sem, HA.at("sd", H))
                    HD.next(e, H).took("rc", e.reciprocal(R[:, :], sd[:, :]))
                    e.wait_ge(FK.sem, FK.at("k", (i * 8, T - 7)))
                    HD.next(e, H).took("y", e.scalar_tensor_tensor(O32[:, y], O32[:, y], sub_gl[:, :], R[:, :], ALU.mult, ALU.mult))
                    HD.next(e, H).took("yg", e.tensor_tensor(O32[:, y:y + 1], O32[:, y:y + 1], tile(gate, i * 2 + H[1]), ALU.mult))
                H = ended(i, T, 8)
                if H:
                    y = H[1] % 2
                    e.wait_ge(HA.sem, HA.at("hi", H))
                    HD.took("lo", e.tensor_tensor(tile(x1l, i * 2 + H[1]), O32[:, y:y + 1], tile(x1h, i * 2 + H[1]).bitcast(F32), ALU.subtract))
            piped(e, step, DT, 8)

        def diff_scalar(e):
            for s in (FE, FC, FK, HA):
                s.open(e)

            def step(i, T):
                q = T - 1
                if runs(i, q, DT):
                    t, z, N = (i * 8, q), q % 4, LANES * (q % 4 + 1)
                    e.wait_ge(FM.sem, FM.at("neg", t))
                    e.wait_ge(FW.sem, FW.at("w1", (i * 8, q - 4)))
                    for s in range(2):
                        FE.took(f"e{s}", e.activation(S2[:, z, s, 0:N], S2[:, z, s, 0:N], ACT.Exp, bias=s2t["nm"][:, z, s:s + 1], accum_out=s2t["sm"][:, z, s:s + 1]))
                q = T - 3
                if runs(i, q, DT):
                    N = LANES * (q % 4 + 1)
                    e.wait_ge(FT.sem, FT.at("t", (i * 8, q)))
                    e.wait_ge(FO.sem, FO.at("o", (i * 8, q - 2)))
                    FC.took("w", e.activation(W2T[:, q % 2, 0:N], bank[5 + q % 2][:, 0:N], ACT.Copy))
                q = T - 4
                if runs(i, q, DT):
                    n = q % 4
                    e.wait_ge(FO.sem, FO.at("o", (i * 8, q)))
                    if n == 0:
                        e.wait_ge(HD.sem, HD.at("lo", (i * 2, q // 4 - 2)))
                    FK.took("k", e.activation(O32[:, q % 8 // 4, n * LANES:(n + 1) * LANES], bank[7][:, n * LANES:(n + 1) * LANES], ACT.Copy))
                H = ended(i, T, 8)
                if H:
                    e.wait_ge(HD.sem, HD.at("yg", H))
                    HA.took("hi", e.activation(tile(x1h, i * 2 + H[1]), O32[:, H[1] % 2:H[1] % 2 + 1], ACT.Copy))
                H = ended(i, T, 4)
                if H:
                    e.wait_ge(FK.sem, FK.at("k", (i * 8, T - 4)))
                    e.wait_ge(HE.sem, HE.at("sum", (H[0], H[1] - 1)))
                    HA.took("sq", e.activation(t32[:, :], O32[:, H[1] % 2], ACT.Square))
                H = ended(i, T, 6)
                if H:
                    e.wait_ge(HE.sem, HE.at("sum", H))
                    e.wait_ge(HD.sem, HD.at("rc", (H[0], H[1] - 1)))
                    HA.took("sd", e.activation(sd[:, :], bk[4], ACT.Sqrt, bias=eps5[:, :], scale=1.0 / LANES))
            piped(e, step, DT, 8)

        def wo2_scalar(e):
            for m in range(8):
                act_split(e, U_O2 + m + 2, 0)
            act_norm(e, 9, eps5)

        def wo2_vector(e):
            for m in range(8):
                dve_split(e, U_O2 + m + 2, 0)
                b = evac_start(e, U_O2, m, 0)
                e.tensor_tensor(h[:, m], h[:, m], b, ALU.add).then_inc(bank_free, 1)
                e.wait_ge(bank_free, U_O2 + m + 5)
                e.sem_inc(h_ready, 1)
            dve_norm(e, 9)
            with e.Fori(0, KT) as m:
                e.scalar_tensor_tensor(tile(h, m), tile(h, m), Vd("final2", m), one(R[:, :]), ALU.mult, ALU.mult).then_inc(h_ready, 1)

        def wo2_tensor(e):
            for m in range(8):
                pe_unit(e, U_O2, m, 0, x1h, x1l, (lambda k: (HD.sem, HD.at("lo", k))) if m == 0 else None)
            pe_norm(e, 9)

        def store(e):
            for m in range(KT):
                e.wait_ge(h_ready, 8 * 10 + m + 1)
                e.dma_start(a["out"][m * LANES:(m + 1) * LANES, :], h[:, m]).then_inc(stored, 16)
            e.wait_ge(stored, 16 * KT)

        mlp0, mlp1 = mlp_parts(0, 2, 1, 2, "ple0"), mlp_parts(1, 5, 5, 6, "ple1")
        ple0, ple1 = ple_parts(0, 3, 3, "kv"), ple_parts(1, 6, 7, "final_a")
        block = ctx.enter_context(nc.Block())

        @block.sync
        def _(e):
            s5_loads(e)
            for i in range(2):
                e.dma_start(raw[:, i], a["w"][i]).then_inc(raw_loaded[i], 16)
            s5_sync(e)
            e.wait_ge(h_ready, 9)
            e.dma_start(p_in[:, :, :, :], a["pT"]).then_inc(p_loaded, 16)
            with e.Fori(1, PAIRS // 2) as i:
                for s in range(2):
                    e.wait_ge(w_split, i * 4 + (2 * s - 2))
                    e.dma_start(raw[:, s], a["w"][bass.ds(i * 2 + s, 1)].rearrange("o p a k m -> p (o a) k m")).then_inc(raw_loaded[s], 16)
            if PAIRS % 2:
              e.wait_ge(w_split, 2 * PAIRS - 4)
              e.dma_start(raw[:, 0], a["w"][PAIRS - 1]).then_inc(raw_loaded[0], 16)
            store(e)

        @block.gpsimd
        def _(e):
            s5_pool(e)
            for n in (1, 2, 3):
                pool_h(e, n)
            att_pool(e)
            e.wait_ge(h_ready, 33)
            for n in (4, 5):
                pool_h(e, n)
            pool_h67(e)
            mamba_pool(e)
            e.wait_ge(h_ready, 65)
            pool_h(e, 8)
            diff_pool(e)
            e.wait_ge(h_ready, 73)
            pool_h(e, 9)

        @block.scalar
        def _(e):
            s5_scalar(e)
            glu_scalar(e)
            mlp0[0](e)
            ple0[0](e)
            more_x_scalar(e, 3, 4, "mix1", x0h)
            kv_scalar(e)
            q_scalar(e)
            att_scalar(e)
            wo_scalar(e)
            mlp1[0](e)
            ple1[0](e)
            dt_scalar(e)
            mamba_scalar(e)
            kv2_scalar(e)
            qg2_scalar(e)
            diff_scalar(e)
            wo2_scalar(e)

        @block.vector
        def _(e):
            e.sem_inc(bank_free, 4)
            s5_vector(e)
            glu_vector(e)
            mlp0[1](e)
            ple0[1](e)
            more_x_vector(e, 4, "mix1", x0h, x0l)
            kv_vector(e)
            q_vector(e)
            att_vector(e)
            wo_vector(e)
            mlp1[1](e)
            ple1[1](e)
            dt_vector(e)
            mamba_vector(e)
            kv2_vector(e)
            qg2_vector(e)
            diff_vector(e)
            wo2_vector(e)

        @block.tensor
        def _(e):
            s5_tensor(e)
            glu_tensor(e)
            mlp0[2](e)
            ple0[2](e)
            kv_tensor(e)
            q_tensor(e)
            att_tensor(e)
            wo_tensor(e)
            mlp1[2](e)
            ple1[2](e)
            dt_tensor(e)
            mamba_tensor(e)
            kv2_tensor(e)
            qg2_tensor(e)
            diff_tensor(e)
            wo2_tensor(e)


def constants():
    f = np.float32
    c = {}
    eye = np.eye(128, dtype=f)
    c["ident"] = eye
    turn = np.zeros((128, 128), f)
    turn[64:, :64], turn[:64, 64:] = -np.eye(64), np.eye(64)
    c["turn"] = turn
    swap = np.zeros((128, 128), f)
    for base in (0, 64):
        for d in range(8):
            swap[base + d + 8, base + d] = -1
            swap[base + d, base + d + 8] = 1
    c["ropeswap"] = swap
    c["ones"] = np.ones((128, 128), f)
    k, q = np.arange(128)[:, None], np.arange(128)[None, :]
    c["tri"] = (k <= q).astype(f)
    sgn = np.where(np.arange(128) < 64, -1, 1).astype(f)[:, None]
    c["sgn"], c["nsgn"] = sgn, -sgn
    c["sel"] = (np.arange(128)[:, None] // 16 == np.arange(8)[None]).astype(f)
    c["cidx"] = np.tile(np.arange(64, dtype=f), (128, 1))
    c["cnz"] = np.tile((np.arange(64) > 0).astype(f), (128, 1))
    c["id16"] = np.pad(np.eye(16, dtype=f), ((0, 112), (0, 0)))
    inv = f(500000.0) ** (-np.arange(0, 16, 2, dtype=f) / f(16))
    ang = np.arange(512, dtype=f)[None] * inv[:, None]
    rc, rs = np.ones((64, 512), f), np.zeros((64, 512), f)
    rc[0:8] = rc[8:16] = np.cos(ang)
    rs[0:8] = rs[8:16] = np.sin(ang)
    c["rcos"], c["rsin"] = np.tile(rc, (2, 1)), np.tile(rs, (2, 1))
    qi, kj = np.arange(128)[:, None] + 128, np.arange(256)[None]
    c["band"] = np.where((kj <= qi) & (qi - kj < 128), 0, -1e30).astype(f)
    c["band0"] = np.where(kj < 128, f(-1e30), c["band"])
    qi, kj = np.arange(128)[:, None], np.arange(512)[None] - 384
    c["dist"] = np.where(kj // 64 <= qi // 64, np.abs(qi - kj), 1e30).astype(f)
    c["slope"] = np.tile(-f(2.0) ** (-f(8.0) * np.arange(1, 9, dtype=f) / f(8.0)), (128, 1))
    return np.ascontiguousarray(np.concatenate([c[n] for n, _ in CONSTS], axis=1).astype(f))


def lay_out(x, p, norm_mix, ssm_lambda_re, ssm_lambda_im, ssm_log_dt, ssm_b_re, ssm_b_im, ssm_c_re,
            ssm_c_im, ssm_d, ssm_w_glu, kv_norm, w_k, w_v, w_q, attn_sinks, w_o, norm_mlp, w_up, w_down,
            norm_ple, w_ple_gate, w_ple_proj, norm_final, a_norm_g_2, a_w_in_2, a_conv_w_2, a_conv_b_2,
            a_dt_bias_2, a_a_log_2, a_d_skip_2, a_gate_norm_g_2, a_w_out_2, kv_norm_g_2, w_kv_2,
            b_norm_g_2, b_w_in_2, b_lambda_2, b_sub_g_2, b_w_out_2, final_norm_g_2):
    f = np.float32
    units = []

    def unit(w, r0, c0):
        units.append(w[r0:r0 + DM, c0:c0 + 128].reshape(KT, 128, 128).transpose(1, 0, 2))

    def cols(w, n, c0=0, r0=0):
        for m in range(n):
            unit(w, r0, c0 + 128 * m)

    def ple(w):
        w = w.reshape(2, 128, 2, 4, 128)
        for j in range(2):
            units.append(w[:, :, j].transpose(1, 2, 0, 3).reshape(128, KT, 128))

    def mlp(i):
        for q in range(4):
            cols(w_up[i], 8, q * DM)
            cols(w_down[i], 8, 0, q * DM)

    for m in range(8):
        unit(ssm_w_glu[0], 0, DM + 128 * m)
        unit(ssm_w_glu[0], 0, 128 * m)
    mlp(0)
    ple(w_ple_proj[0])
    cols(w_ple_gate[0], 8)
    cols(w_k, 2)
    cols(w_v, 2)
    cols(w_q[0], 8)
    cols(w_o[0], 8)
    mlp(1)
    ple(w_ple_proj[1])
    cols(w_ple_gate[1], 8)
    win = a_w_in_2[0]
    units.append(np.pad(win[:, 6144:6176].reshape(KT, 128, 32).transpose(1, 0, 2), ((0, 0), (0, 0), (0, 96))))
    for half in range(2):
        for pair in range(2):
            g = 4 * half + 2 * pair
            cols(win, 4, 2048 + 256 * g)
            cols(win, 2, 4096 + 128 * g)
            cols(win, 2, 5120 + 128 * g)
            cols(win, 4, 256 * g)
        cols(a_w_out_2[0], 8, 0, half * DM)
    cols(w_kv_2, 16)
    cols(b_w_in_2[0], 16)
    cols(b_w_out_2[0], 8)
    assert len(units) == UNITS
    units.append(np.zeros((128, KT, 128), f))
    w = np.ascontiguousarray(np.stack(units).reshape(PAIRS, 2, 128, KT, 128).transpose(0, 2, 1, 3, 4))

    v = {}
    vec = lambda t: t.reshape(-1, 128).T
    gains = [norm_mix[0], norm_mix[1], norm_mlp[0], norm_mlp[1], norm_ple[0], norm_ple[1], kv_norm, norm_final,
             a_norm_g_2[0], kv_norm_g_2, b_norm_g_2[0], final_norm_g_2]
    for n, g in zip(GAINS, gains):
        v[n] = vec(g)
    over = lambda t: np.tile(t.reshape(1, -1), (128, 1))
    v["lam_re"] = np.tile(ssm_lambda_re[0].T, (2, 1))
    v["lam_im"] = np.tile(ssm_lambda_im[0].T, (2, 1))
    v["log_dt"] = over(ssm_log_dt[0])
    v["gain_u"] = np.tile(norm_mix[0].reshape(64, 16).T, (8, 1))
    v["d_h"] = np.pad(ssm_d[0].reshape(64, 16).T, ((0, 112), (0, 0)))
    v["conv_w"] = a_conv_w_2[0].reshape(4, 32, 128).transpose(2, 0, 1).reshape(128, 128)
    v["conv_b"] = vec(a_conv_b_2[0])
    v["d_skip"] = vec(np.repeat(a_d_skip_2[0], 64))
    v["gate_g"] = vec(a_gate_norm_g_2[0])
    v["sub_g"] = vec(b_sub_g_2[0])
    v["sinks"] = over(attn_sinks[0])
    v["dt_bias"] = over(a_dt_bias_2[0])
    v["a_log"] = over(a_a_log_2[0])
    v["lam_qk"] = over(b_lambda_2[0])
    par = np.concatenate([v[n] for n, _ in PARAMS], axis=1)

    B = np.stack([np.concatenate([ssm_b_re[0], ssm_b_im[0]], 1), np.concatenate([ssm_b_im[0], ssm_b_re[0]], 1)])
    Cc = np.stack([np.concatenate([ssm_c_re[0], ssm_c_im[0]], 2), np.concatenate([ssm_c_im[0], ssm_c_re[0]], 2)])
    out = {
        "w": w, "const": constants(), "par": par,
        "xT": x[0].T,
        "xu": x[0].reshape(64, 8, 64, 16).transpose(1, 3, 2, 0).reshape(128, 64, 64),
        "B": B.transpose(2, 0, 1, 3),
        "C": Cc.transpose(3, 0, 1, 2),
        "pT": p[:, 0].reshape(2, 512, 2, 128).transpose(3, 0, 2, 1),
    }
    return {k: np.ascontiguousarray(t) for k, t in out.items()}


def kernel(**inputs):
    import concourse.bacc as bacc
    from concourse.bass_utils import run_bass_kernel_spmd

    nc = bacc.Bacc("TRN2", target_bir_lowering=False, num_devices=1)
    arrays = {f"in_{n}_dram": t for n, t in lay_out(**inputs).items()}
    a = {n: nc.dram_tensor(f"in_{n}_dram", arrays[f"in_{n}_dram"].shape, F32, kind="ExternalInput").ap()
         for n in ("w", "const", "par", "xT", "xu", "B", "C", "pT")}
    a["out"] = nc.dram_tensor("out_dram", (DM, TOK), F32, kind="ExternalOutput").ap()
    program(nc, a)
    result = run_bass_kernel_spmd(nc, [arrays], core_ids=[0])
    return np.ascontiguousarray(result.results[0]["out_dram"].T).reshape(1, TOK, DM)
```
